# Optimizing a Trainium2 kernel written in Bass

```python
import jax, jax.numpy as jnp
from jax import lax
import numpy as np

D_MODEL = 1024
BATCH = 1
SEQ = 1024
DEPTH = 1

GRID_W = 64
CTX_LEN = 256

D_MIX = D_MODEL
M_HEADS = 4
M_DH = 128
M_WIDTH = M_HEADS * M_DH
A_HEADS = 8
A_KV_HEADS = 2
A_DH = 64
A_GROUP = A_HEADS // A_KV_HEADS
A_WIDTH = A_HEADS * A_DH
A_KV_WIDTH = A_KV_HEADS * A_DH
WINDOW = 128
A_BLOCK = 128
CHUNK = 64
CONV_W = 5
D_FF = 2816
ROPE_BASE = 10000.0
N_MOD = 9
LN_EPS = 1e-5
FFN_RES = 0.5
ALPHA = (2.0 * DEPTH) ** 0.25
BETA = (8.0 * DEPTH) ** -0.25

OFF_QM = 0
OFF_KM = OFF_QM + M_WIDTH
OFF_VM = OFF_KM + M_WIDTH
OFF_OM = OFF_VM + M_WIDTH
OFF_G = OFF_OM + M_WIDTH
N_GATES = 4 * M_HEADS
OFF_QA = OFF_G + N_GATES
OFF_KA = OFF_QA + A_WIDTH
OFF_VA = OFF_KA + A_KV_WIDTH
N_IN = OFF_VA + A_KV_WIDTH

kernel_name = 'hybrid_mlstm_swa_macaron_dit_block'

F32 = jnp.float32

def _layer_norm(x, g, b):
    xf = x.astype(F32)
    mu = xf.mean(-1, keepdims=True)
    var = jnp.square(xf - mu).mean(-1, keepdims=True)
    return ((xf - mu) * lax.rsqrt(var + LN_EPS)).astype(x.dtype) * g + b

def _modulate(x, shift, scale):
    return x * (1.0 + scale) + shift

def _swiglu(h, w13, w2):
    a = h @ w13
    return (jax.nn.silu(a[..., :D_FF]) * a[..., D_FF:]) @ w2

def _ffn_sublayer(x, shift, scale, gate, w13, w2, g, b):
    y = _swiglu(_modulate(x, shift, scale), w13, w2)
    return _layer_norm(ALPHA * x + FFN_RES * gate * y, g, b)

def _centred_dwconv(x, w, b):
    T = x.shape[1]
    pad = CONV_W // 2
    xp = jnp.pad(x, ((0, 0), (pad, pad), (0, 0)))
    out = xp[:, 0:T] * w[0]
    for j in range(1, CONV_W):
        out = out + xp[:, j:j + T] * w[j]
    return out + b

def _axial_rope_tables(rows):
    row = jnp.repeat(jnp.arange(rows, dtype=F32), GRID_W)
    col = jnp.tile(jnp.arange(GRID_W, dtype=F32), rows)
    n_freq = A_DH // 4
    inv = ROPE_BASE ** (-jnp.arange(n_freq, dtype=F32) / n_freq)
    ang = jnp.concatenate([row[:, None] * inv, col[:, None] * inv], -1)
    return jnp.cos(ang), jnp.sin(ang)

def _rope(x, cos, sin):
    xf = x.astype(F32)
    half = A_DH // 2
    x1, x2 = xf[..., :half], xf[..., half:]
    cs = cos[None, :, None, :]
    sn = sin[None, :, None, :]
    return jnp.concatenate([x1 * cs - x2 * sn, x2 * cs + x1 * sn], -1).astype(x.dtype)

def _rev(a):
    return jnp.flip(a, axis=1)

def _mlstm_scan(q, k, v, li, lf, state, return_h):
    B, T, H, d = q.shape
    nc = T // CHUNK

    def to_chunks(a):
        a = a.reshape((B, nc, CHUNK) + a.shape[2:])
        return jnp.swapaxes(jnp.moveaxis(a, 1, 0), 2, 3)

    tril = jnp.tril(jnp.ones((CHUNK, CHUNK), dtype=bool))

    def body(carry, inp):
        C, nv, m = carry
        qc, kc, vc, lic, lfc = inp
        b = jnp.cumsum(lfc, axis=-1)
        b_last = b[..., -1]
        log_w = b_last[..., None] - b + lic
        m_new = jnp.maximum(b_last + m, log_w.max(-1))
        decay = jnp.exp(b_last + m - m_new)
        w = jnp.exp(log_w - m_new[..., None])
        C_new = decay[..., None, None] * C + jnp.einsum('bhs,bhsv,bhsk->bhvk', w, vc, kc)
        n_new = decay[..., None] * nv + jnp.einsum('bhs,bhsk->bhk', w, kc)
        if not return_h:
            return (C_new, n_new, m_new), None
        log_d = b[..., :, None] - b[..., None, :] + lic[..., None, :]
        log_d = jnp.where(tril, log_d, -jnp.inf)
        log_inter = b + m[..., None]
        m_t = jnp.maximum(log_inter, log_d.max(-1))
        dmat = jnp.exp(log_d - m_t[..., None])
        inter = jnp.exp(log_inter - m_t)
        s = jnp.einsum('bhtk,bhsk->bhts', qc, kc) * dmat
        num = jnp.einsum('bhts,bhsv->bhtv', s, vc) + inter[..., None] * jnp.einsum('bhtk,bhvk->bhtv', qc, C)
        den = s.sum(-1) + inter * jnp.einsum('bhtk,bhk->bht', qc, nv)
        h = num / jnp.maximum(jnp.abs(den), jnp.exp(-m_t))[..., None]
        return (C_new, n_new, m_new), h

    xs = (to_chunks(q), to_chunks(k), to_chunks(v), to_chunks(li), to_chunks(lf))
    state_out, hs = lax.scan(body, state, xs)
    if not return_h:
        return state_out, None
    h = jnp.moveaxis(jnp.swapaxes(hs, 2, 3), 0, 1).reshape(B, T, H, d)
    return state_out, h

def _bidir_mlstm(q, k, v, fwd, bwd, init_f, init_b, return_h):
    st_f, h_f = _mlstm_scan(q, k, v, fwd[0], fwd[1], init_f, return_h)
    st_b, h_b = _mlstm_scan(_rev(q), _rev(k), _rev(v), _rev(bwd[0]), _rev(bwd[1]), init_b, return_h)
    h = h_f + _rev(h_b) if return_h else None
    return h, st_f, st_b

def _mlstm_inputs(p, conv_w, conv_b, b_gates):
    B, T = p.shape[:2]
    qk = jax.nn.silu(_centred_dwconv(p[..., OFF_QM:OFF_VM], conv_w, conv_b))
    qk = qk.astype(F32).reshape(B, T, 2, M_HEADS, M_DH)
    q = qk[:, :, 0] * (M_DH ** -0.5)
    k = qk[:, :, 1]
    v = p[..., OFF_VM:OFF_OM].astype(F32).reshape(B, T, M_HEADS, M_DH)
    g = (p[..., OFF_G:OFF_QA] + b_gates).astype(F32).reshape(B, T, 4, M_HEADS)
    fwd = (g[:, :, 0], jax.nn.log_sigmoid(g[:, :, 1]))
    bwd = (g[:, :, 2], jax.nn.log_sigmoid(g[:, :, 3]))
    return q, k, v, fwd, bwd

def _mlstm_readout(h, o_pre, g):
    B, T = h.shape[:2]
    mu = h.mean(-1, keepdims=True)
    var = jnp.square(h - mu).mean(-1, keepdims=True)
    hn = ((h - mu) * lax.rsqrt(var + LN_EPS)).reshape(B, T, M_WIDTH)
    return (hn * g * jax.nn.sigmoid(o_pre.astype(F32))).astype(o_pre.dtype)

def _banded_attention(q, k, v, kc, vc, sink):
    B, n = q.shape[:2]
    nb = n // A_BLOCK
    scale = A_DH ** -0.5
    qb = q.reshape(B, nb, A_BLOCK, A_KV_HEADS, A_GROUP, A_DH)

    def band(a):
        ap = jnp.pad(a, ((0, 0), (A_BLOCK, A_BLOCK), (0, 0), (0, 0)))
        ap = ap.reshape(B, nb + 2, A_BLOCK, A_KV_HEADS, A_DH)
        return jnp.concatenate([ap[:, :-2], ap[:, 1:-1], ap[:, 2:]], axis=2)

    kb, vb = band(k), band(v)
    s_loc = jnp.einsum('bjikgd,bjrkd->bjkgir', qb, kb).astype(F32) * scale
    s_ctx = jnp.einsum('bjikgd,bckd->bjkgic', qb, kc).astype(F32) * scale
    i = jnp.arange(A_BLOCK)
    r = jnp.arange(3 * A_BLOCK)
    j = jnp.arange(nb)
    rel = r[None, :] - A_BLOCK - i[:, None]
    key_pos = (j[:, None] - 1) * A_BLOCK + r[None, :]
    valid = (jnp.abs(rel) <= WINDOW)[None] & ((key_pos >= 0) & (key_pos < n))[:, None, :]
    s_loc = jnp.where(valid[None, :, None, None], s_loc, -jnp.inf)
    sink_f = sink.astype(F32).reshape(1, 1, A_KV_HEADS, A_GROUP, 1)
    m = jnp.maximum(jnp.maximum(s_loc.max(-1), s_ctx.max(-1)), sink_f)
    e_loc = jnp.exp(s_loc - m[..., None])
    e_ctx = jnp.exp(s_ctx - m[..., None])
    den = e_loc.sum(-1) + e_ctx.sum(-1) + jnp.exp(sink_f - m)
    out = (jnp.einsum('bjkgir,bjrkd->bjkgid', e_loc, vb.astype(F32))
           + jnp.einsum('bjkgic,bckd->bjkgid', e_ctx, vc.astype(F32))) / den[..., None]
    return out.transpose(0, 1, 4, 2, 3, 5).reshape(B, n, A_WIDTH).astype(q.dtype)

def _context_attention(q, k, v, sink):
    B, Tc = q.shape[:2]
    qg = q.reshape(B, Tc, A_KV_HEADS, A_GROUP, A_DH)
    s = jnp.einsum('bikgd,bckd->bkgic', qg, k).astype(F32) * (A_DH ** -0.5)
    sink_b = jnp.broadcast_to(sink.astype(F32).reshape(1, A_KV_HEADS, A_GROUP, 1, 1), s.shape[:-1] + (1,))
    p = jax.nn.softmax(jnp.concatenate([s, sink_b], -1), axis=-1)[..., :-1]
    out = jnp.einsum('bkgic,bckd->bikgd', p.astype(v.dtype), v)
    return out.reshape(B, Tc, A_WIDTH)

def _token_mixer(h_lat, h_ctx, w_in, b_gates, conv_w, conv_b, mh_g, sink, w_out, cos, sin, need_ctx):
    B, n = h_lat.shape[:2]
    Tc = h_ctx.shape[1]
    p_l = h_lat @ w_in
    p_c = h_ctx @ w_in
    qc, kc, vc, fwd_c, bwd_c = _mlstm_inputs(p_c, conv_w, conv_b, b_gates)
    zero = (jnp.zeros((B, M_HEADS, M_DH, M_DH), F32), jnp.zeros((B, M_HEADS, M_DH), F32),
            jnp.zeros((B, M_HEADS), F32))
    hm_c, st_f, st_b = _bidir_mlstm(qc, kc, vc, fwd_c, bwd_c, zero, zero, need_ctx)
    ql, kl, vl, fwd_l, bwd_l = _mlstm_inputs(p_l, conv_w, conv_b, b_gates)
    hm_l, _, _ = _bidir_mlstm(ql, kl, vl, fwd_l, bwd_l, st_f, st_b, True)
    m_l = _mlstm_readout(hm_l, p_l[..., OFF_OM:OFF_G], mh_g)
    qa_l = _rope(p_l[..., OFF_QA:OFF_KA].reshape(B, n, A_HEADS, A_DH), cos, sin)
    ka_l = _rope(p_l[..., OFF_KA:OFF_VA].reshape(B, n, A_KV_HEADS, A_DH), cos, sin)
    va_l = p_l[..., OFF_VA:N_IN].reshape(B, n, A_KV_HEADS, A_DH)
    ka_c = p_c[..., OFF_KA:OFF_VA].reshape(B, Tc, A_KV_HEADS, A_DH)
    va_c = p_c[..., OFF_VA:N_IN].reshape(B, Tc, A_KV_HEADS, A_DH)
    a_l = _banded_attention(qa_l, ka_l, va_l, ka_c, va_c, sink)
    y_l = jnp.concatenate([m_l, a_l], -1) @ w_out
    if not need_ctx:
        return y_l, None
    m_c = _mlstm_readout(hm_c, p_c[..., OFF_OM:OFF_G], mh_g)
    qa_c = p_c[..., OFF_QA:OFF_KA].reshape(B, Tc, A_HEADS, A_DH)
    a_c = _context_attention(qa_c, ka_c, va_c, sink)
    y_c = jnp.concatenate([m_c, a_c], -1) @ w_out
    return y_l, y_c

def setup_inputs(seed: int = 0) -> dict:
    key = jax.random.key(seed)
    ks = jax.random.split(key, 24)

    def nrm(k, shape, scale):
        return jax.random.normal(k, shape, F32) * scale

    x = nrm(ks[0], (BATCH, SEQ, D_MODEL), 1.0)
    c = nrm(ks[1], (BATCH, D_MODEL), 1.0)
    ctx = nrm(ks[2], (BATCH, CTX_LEN, D_MODEL), 1.0)
    c_ctx = nrm(ks[3], (D_MODEL,), 1.0)
    w_ada = nrm(ks[4], (DEPTH, D_MODEL, N_MOD * D_MODEL), 0.5 * D_MODEL ** -0.5)
    b_ada = nrm(ks[5], (DEPTH, N_MOD * D_MODEL), 0.02)
    ln_g = 1.0 + nrm(ks[6], (DEPTH, 3, D_MODEL), 0.02)
    ln_b = nrm(ks[7], (DEPTH, 3, D_MODEL), 0.02)
    ffn_w13 = nrm(ks[8], (DEPTH, 2, D_MODEL, 2 * D_FF), D_MODEL ** -0.5)
    ffn_w2 = nrm(ks[9], (DEPTH, 2, D_FF, D_MODEL), BETA * D_FF ** -0.5)
    w_in = nrm(ks[10], (DEPTH, D_MODEL, N_IN), D_MODEL ** -0.5)
    f_bias = jnp.linspace(3.0, 6.0, M_HEADS, dtype=F32)[None, :]
    bi_f = nrm(ks[11], (DEPTH, M_HEADS), 0.1)
    bf_f = f_bias + nrm(ks[12], (DEPTH, M_HEADS), 0.1)
    bi_b = nrm(ks[13], (DEPTH, M_HEADS), 0.1)
    bf_b = f_bias + nrm(ks[14], (DEPTH, M_HEADS), 0.1)
    b_gates = jnp.concatenate([bi_f, bf_f, bi_b, bf_b], -1)
    conv_w = nrm(ks[15], (DEPTH, CONV_W, 2 * M_WIDTH), CONV_W ** -0.5)
    conv_b = nrm(ks[16], (DEPTH, 2 * M_WIDTH), 0.02)
    mh_norm_g = 1.0 + nrm(ks[17], (DEPTH, M_WIDTH), 0.02)
    attn_sink = nrm(ks[18], (DEPTH, A_HEADS), 0.5)
    w_out = nrm(ks[19], (DEPTH, D_MIX, D_MODEL), BETA * D_MIX ** -0.5)
    return {'x': x, 'c': c, 'ctx': ctx, 'c_ctx': c_ctx, 'w_ada': w_ada, 'b_ada': b_ada,
            'ln_g': ln_g, 'ln_b': ln_b, 'ffn_w13': ffn_w13, 'ffn_w2': ffn_w2, 'w_in': w_in,
            'b_gates': b_gates, 'conv_w': conv_w, 'conv_b': conv_b, 'mh_norm_g': mh_norm_g,
            'attn_sink': attn_sink, 'w_out': w_out}

def reference(x, c, ctx, c_ctx, w_ada, b_ada, ln_g, ln_b, ffn_w13, ffn_w2, w_in, b_gates,
              conv_w, conv_b, mh_norm_g, attn_sink, w_out):
    B, n, D = x.shape
    rows = n // GRID_W
    cos, sin = _axial_rope_tables(rows)
    x_lat, x_ctx = x, ctx
    for l in range(DEPTH):
        need_ctx = l < DEPTH - 1
        mod_l = (jax.nn.silu(c) @ w_ada[l] + b_ada[l]).reshape(B, N_MOD, 1, D)
        mod_c = (jax.nn.silu(c_ctx) @ w_ada[l] + b_ada[l]).reshape(N_MOD, 1, 1, D)
        ml = [mod_l[:, i] for i in range(N_MOD)]
        mc = [mod_c[i] for i in range(N_MOD)]
        x_lat = _ffn_sublayer(x_lat, ml[0], ml[1], ml[2], ffn_w13[l, 0], ffn_w2[l, 0], ln_g[l, 0], ln_b[l, 0])
        x_ctx = _ffn_sublayer(x_ctx, mc[0], mc[1], mc[2], ffn_w13[l, 0], ffn_w2[l, 0], ln_g[l, 0], ln_b[l, 0])
        y_lat, y_ctx = _token_mixer(_modulate(x_lat, ml[3], ml[4]), _modulate(x_ctx, mc[3], mc[4]),
                                    w_in[l], b_gates[l], conv_w[l], conv_b[l], mh_norm_g[l],
                                    attn_sink[l], w_out[l], cos, sin, need_ctx)
        x_lat = _layer_norm(ALPHA * x_lat + ml[5] * y_lat, ln_g[l, 1], ln_b[l, 1])
        x_lat = _ffn_sublayer(x_lat, ml[6], ml[7], ml[8], ffn_w13[l, 1], ffn_w2[l, 1], ln_g[l, 2], ln_b[l, 2])
        if need_ctx:
            x_ctx = _layer_norm(ALPHA * x_ctx + mc[5] * y_ctx, ln_g[l, 1], ln_b[l, 1])
            x_ctx = _ffn_sublayer(x_ctx, mc[6], mc[7], mc[8], ffn_w13[l, 1], ffn_w2[l, 1], ln_g[l, 2], ln_b[l, 2])
    return x_lat


_drawn_inputs = setup_inputs


def setup_inputs(seed=0):
    import zlib

    import numpy as np

    out = dict(_drawn_inputs(seed))
    spreads = {}
    factors = {'ctx': 6.132,
     'c_ctx': 3.058,
     'b_ada': 6.56,
     'conv_w': 3.349,
     'conv_b': 64.0,
     'mh_norm_g': 48.977,
     'attn_sink': 64.0}
    for name, (base, spread) in spreads.items():
        noise = np.random.default_rng([zlib.crc32(name.encode()), seed]).standard_normal(out[name].shape)
        drawn = base * np.exp(spread * noise) if base else spread * noise
        out[name] = __import__('jax').numpy.asarray(drawn.astype(out[name].dtype))
    for name, factor in factors.items():
        out[name] = (out[name] * factor).astype(out[name].dtype)
    return out
```

```python
from contextlib import ExitStack

import numpy as np

import concourse.bass as bass
from concourse import mybir

P = 128
F32 = mybir.dt.float32
F32R = mybir.dt.float32r
BF16 = mybir.dt.bfloat16
ALU = mybir.AluOpType
ACT = mybir.ActivationFunctionType
AX_X = mybir.AxisListType.X

D = 1024
KD = D // P
N_LAT, N_CTX = 1024, 256
TL, TC = N_LAT // P, N_CTX // P
TA = TL + TC
N_ALL = N_LAT + N_CTX
D_FF = 2816
FB = D_FF // P
PAIRS = FB // 2
N_MOD = 9
LN_EPS = 1e-5
ALPHA = 2.0 ** 0.25
HALF = 0.5
BANK = 512

M_HEADS, M_DH, M_WIDTH = 4, 128, 512
A_HEADS, A_KV, A_DH = 8, 2, 64
OFF_Q, OFF_K, OFF_V, OFF_O, OFF_G = 0, 512, 1024, 1536, 2048
OFF_QA = OFF_G + 16
OFF_KA = OFF_QA + A_HEADS * A_DH
OFF_VA = OFF_KA + A_KV * A_DH
N_IN = OFF_VA + A_KV * A_DH
CONV_W = 5

ADA_EARLY = 2 * KD
ADA_PER_PAIR = 5

CHUNKS_ALL = [(0, 512), (512, 512), (1024, 256)]
CHUNKS_LAT = [(0, 512), (512, 512)]


def hybrid_block(nc, x, c, ctx, c_ctx, w_ada, b_ada, ln_g, ln_b, ffn_w13, ffn_w2, w_in, b_gates,
                 conv_w, conv_b, mh_norm_g, attn_sink, w_out, rope_cs, out):
    with ExitStack() as keep:
        def tensor(stack, name, shape, dt=F32):
            return stack.enter_context(nc.sbuf_tensor(name, shape, dt))

        def sem(name):
            return keep.enter_context(nc.semaphore(name))

        x_rows = x.rearrange("b (t p) d -> (b t) p d", p=P)
        ctx_rows = ctx.rearrange("b (t p) d -> (b t) p d", p=P)
        out_rows = out.rearrange("b (t p) d -> (b t) p d", p=P)
        ada_view = w_ada.rearrange("l (k p) n -> (l p) k n", p=P)
        w13_view = [ffn_w13[0, i].rearrange("(k p) n -> p k n", p=P) for i in range(2)]
        w2_view = [ffn_w2[0, i] for i in range(2)]
        w_in_view = w_in.rearrange("l (k p) n -> (l p) k n", p=P)
        w_out_view = w_out.rearrange("l (k p) n -> (l p) k n", p=P)

        def token_rows(t):
            return x_rows[t] if t < TL else ctx_rows[t - TL]

        psum = keep.enter_context(nc.psum_tensor("psum", [P, 8, BANK], F32))

        ident = tensor(keep, "ident", [P, P])
        params = tensor(keep, "params", [P, 120])
        more = tensor(keep, "more", [P, 64])
        mod = tensor(keep, "mod", [P, N_MOD * KD, 2])
        in_scale = tensor(keep, "in_scale", [P, 2, KD])
        in_shift = tensor(keep, "in_shift", [P, 2, KD])
        ln_stats = tensor(keep, "ln_stats", [P, 2, 24])
        minus_half = tensor(keep, "minus_half", [P, 8])
        tok_gate = tensor(keep, "tok_gate", [P, 4, TA, 2 * M_HEADS])
        decay_all = tensor(keep, "decay_all", [P, 2 * M_HEADS, TA])
        decay = tensor(keep, "decay", [P, 32])

        arena_at = nc.sbuf_base

        def place(name, kib, shape, dt=F32):
            return nc.alloc_sbuf_tensor_at(name, shape, dt, offset=arena_at + int(kib * 1024))

        xh_lat = place("xh_lat", 0, [P, KD, N_LAT], F32R)
        xl_lat = place("xl_lat", 32, [P, KD, N_LAT], F32R)
        xh_ctx = place("xh_ctx", 64, [P, KD, N_CTX], F32R)
        xl_ctx = place("xl_ctx", 72, [P, KD, N_CTX], F32R)
        y = place("y", 80, [P, TA, D])
        raw = place("raw", 120, [P, 2, KD, P])
        ada_raw = place("ada_raw", 128, [P, KD, P])
        w13h = place("w13h", 132, [P, 2, 2, KD, P], F32R)
        w13l = place("w13l", 148, [P, 2, 2, KD, P], F32R)
        w2h = place("w2h", 164, [P, 2, D], F32R)
        w2l = place("w2l", 172, [P, 2, D], F32R)
        gh = place("gh", 180, [P, 2, N_ALL], F32R)
        gl = place("gl", 190, [P, 2, N_ALL], F32R)
        glu_sig = place("glu_sig", 200, [P, BANK])
        glu = place("glu", 202, [P, BANK])
        EARLY = 6
        ada_early = place("ada_early", 164, [P, EARLY, KD, P])
        rows_a = place("rows_a", 188, [P, P])
        rows_b = place("rows_b", 188.5, [P, P])
        turn_buf1 = place("turn_buf1", 190, [P, 2, BANK])
        gate_row = place("gate_row", 120, [P, 2, D])
        res_row = place("res_row", 128, [P, 3, D])
        turn_buf2 = place("turn_buf2", 140, [P, 2, BANK])

        qT = place("qT", 80, [P, M_HEADS, N_LAT])
        kT = place("kT", 96, [P, M_HEADS, N_ALL])
        qaT = place("qaT", 64, [P, A_HEADS // 2, N_LAT])
        kaT = place("kaT", 116, [P, N_ALL])
        va = place("va", 121, [P, TA, P])
        vext = place("vext", 126, [P, TA, M_HEADS, M_DH + 1])
        u_row = place("u_row", 146.25, [P, N_ALL])
        conv_in = place("conv_in", 151.5, [P, 1288])
        conv_sum = place("conv_sum", 156.625, [P, 1284])
        p_raw = place("p_raw", 162, [P, 2, KD, P])
        p_wh = place("p_wh", 170, [P, 2, KD, 256], F32R)
        p_wl = place("p_wl", 186, [P, 2, KD, 256], F32R)
        gate_wh = place("gate_wh", 178, [P, KD, P], F32R)
        gate_wl = place("gate_wl", 194, [P, KD, P], F32R)
        gate_raw = place("gate_raw", 182, [P, KD, 16])
        gate_bias = place("gate_bias", 182.5, [P, 1])
        rope_ab = place("rope_ab", 202, [P, 2, 256])
        rope_tab = place("rope_tab", 152, [P, TL, 2, A_DH // 2])
        rope_out = place("rope_out", 154, [P, 2, 256])
        o_sig = place("o_sig", 156, [P, 2, 256])
        gate_all = place("gate_all", 116, [P, N_ALL])
        gate_abs = place("gate_abs", 121, [P, N_ALL])
        li_row = place("li_row", 126, [P, N_ALL])
        lf_row = place("lf_row", 131, [P, N_ALL])
        b_row = place("b_row", 136, [P, N_ALL])
        m_row = place("m_row", 141, [P, N_ALL])
        a_row = place("a_row", 80, [P, N_ALL])
        e_row = place("e_row", 85, [P, N_ALL])
        a_nat = place("a_nat", 90, [P, N_ALL])
        w_nat = place("w_nat", 116, [P, N_ALL])
        inter_nat = place("inter_nat", 121, [P, N_ALL])
        floor_nat = place("floor_nat", 126, [P, N_ALL])

        k_tok = place("k_tok", 0, [P, TA, M_WIDTH])
        scores = place("scores", 20, [P, TL, M_HEADS, P])
        att_p = place("att_p", 36, [P, 2, 640])
        att_pT = place("att_pT", 41, [P, 2, 640])
        norm_gain = place("norm_gain", 47, [P, M_WIDTH])
        o_in = place("o_in", 49, [P, 2, M_WIDTH])
        d_exp = place("d_exp", 54, [P, 2, M_HEADS, P])
        p_tok = place("p_tok", 58, [P, 2, M_HEADS, P])
        state = place("state", 151.5, [P, 2, M_HEADS, M_DH + 1])
        w_v = place("w_v", 155.75, [P, 2, M_HEADS, M_DH + 1])
        num = place("num", 160, [P, 2, M_HEADS, M_DH + 1])
        h_new = place("h_new", 164.25, [P, M_HEADS, M_DH])
        y_in = place("y_in", 168, [P, TL, D])
        scan_mask = place("scan_mask", 200, [P, 2, M_HEADS, P], BF16)
        band_mask = place("band_mask", 202, [P, 2, P], BF16)
        ident_b = place("ident_b", 202.5, [P, P], BF16)
        sink = place("sink", 202.75, [P, A_HEADS])
        small = place("small", 203, [P, 64])
        att_small = place("att_small", 203.25, [P, 4, 4])
        wo_h = place("wo_h", 126, [P, 2, KD, 256], F32R)
        wo_l = place("wo_l", 142, [P, 2, KD, 256], F32R)
        wo_raw = place("wo_raw", 158, [P, 2, KD, P])
        gate_row2 = place("gate_row2", 112, [P, 1, D])
        res_row2 = place("res_row2", 168, [P, 3, D])
        turn_buf3 = place("turn_buf3", 180, [P, 2, BANK])
        ln_rows2 = place("ln_rows2", 184, [P, 2, D])
        ln_rows3 = place("ln_rows3", 144, [P, 4, D])

        x2_dram = nc.dram_tensor("x2_rows", [TL, P, D], F32, kind="Internal").ap()
        x1_dram = nc.dram_tensor("x1_rows", [TL, P, D], F32, kind="Internal").ap()
        o_dram = nc.dram_tensor("o_rows", [TL, P, M_WIDTH], F32, kind="Internal").ap()

        def xpart(low, k, at, size):
            if at < N_LAT:
                return (xl_lat if low else xh_lat)[:, k, at:at + size]
            return (xl_ctx if low else xh_ctx)[:, k, at - N_LAT:at - N_LAT + size]

        ident_set = sem("ident_set")
        const_set = sem("const_set")
        rows_in = sem("rows_in")
        c_silu = sem("c_silu")
        rows_turned = sem("rows_turned")
        rows_kept = sem("rows_kept")
        early_in = [sem(f"early_in{i}") for i in range(EARLY)]
        early_used = sem("early_used")
        mod_ready = sem("mod_ready")
        dve_step = sem("dve_step")
        x_in = [sem(f"x_in{t}") for t in range(3)]
        ada_in = sem("ada_in")
        ada_used = sem("ada_used")
        out_done = sem("out_done")

        steps = [0]

        def step(dve, instruction):
            steps[0] += 1
            instruction.then_inc(dve_step, 1)
            dve.wait_ge(dve_step, steps[0])

        class Turn:

            def __init__(self, name, chunks):
                self.chunks = chunks
                self.units = [(n, k) for n in range(len(chunks)) for k in range(KD)]
                self.turned = sem(name + "_turned")
                self.scaled = sem(name + "_scaled")
                self.high = sem(name + "_high")
                self.low = sem(name + "_low")

        def turn_pe(pe, T, banks, rows_wait):
            for u, (n, k) in enumerate(T.units):
                at, size = T.chunks[n]
                if k == 0:
                    rows_wait(pe, n)
                if u >= len(banks):
                    pe.wait_ge(T.scaled, u - len(banks) + 1)
                for i in range(size // P):
                    last = nc.tensor.transpose(psum[:, banks[u % len(banks)], i * P:(i + 1) * P],
                                               y[:, at // P + i, k * P:(k + 1) * P], ident[:])
                last.then_inc(T.turned, 1)

        def turn_act(act, T, banks, buf, before, only=None):
            before(act)
            for u, (n, k) in enumerate(T.units):
                if only not in (None, n):
                    continue
                at, size = T.chunks[n]
                v = int(at >= N_LAT)
                act.wait_ge(T.turned, u + 1)
                if u >= 2:
                    act.wait_ge(T.low, u - 1)
                nc.scalar.activation(buf[:, u % 2, 0:size], psum[:, banks[u % len(banks)], 0:size], ACT.Identity,
                                     bias=in_shift[:, v, k:k + 1], scale=in_scale[:, v, k:k + 1]).then_inc(T.scaled, 1)

        def turn_dve(dve, T, buf, only=None):
            for u, (n, k) in enumerate(T.units):
                if only not in (None, n):
                    continue
                at, size = T.chunks[n]
                dve.wait_ge(T.scaled, u + 1)
                high = xpart(0, k, at, size)
                nc.vector.tensor_copy(high, buf[:, u % 2, 0:size]).then_inc(T.high, 1)
                dve.wait_ge(T.high, u + 1)
                nc.vector.tensor_tensor(xpart(1, k, at, size), buf[:, u % 2, 0:size], high.bitcast(F32),
                                        ALU.subtract).then_inc(T.low, 1)

        class Ffn:

            def __init__(self, name, which, chunks, ada):
                self.which, self.chunks, self.ada = which, chunks, ada
                self.tiles = sum(size for _, size in chunks) // P
                self.n = len(chunks)
                self.hi = sem(name + "_hi")
                self.lo = sem(name + "_lo")
                self.ab_ready = sem(name + "_ab_ready")
                self.sig_ready = sem(name + "_sig_ready")
                self.glu_ready = sem(name + "_glu_ready")
                self.gh_ready = sem(name + "_gh_ready")
                self.gl_ready = sem(name + "_gl_ready")
                self.y_ready = sem(name + "_y_ready")
                self.y_summed = sem(name + "_y_summed")
                self.raw_in = [sem(f"{name}_raw_in{i}") for i in range(2)]

        def piece_of(pair, i):
            return 2 + 6 * pair + i

        Y_BANKS = (4, 5, 6)

        def ffn_sp(sp, F):
            w13, w2 = w13_view[F.which], w2_view[F.which]

            def w13_piece(q, slot, block, part):
                sp.dma_start(raw[:, slot], w13[:, :, bass.ds(part * D_FF + block * P, P)]).then_inc(F.raw_in[slot], 16)

            def w2_piece(slot, block):
                sp.dma_start(raw[:, slot].rearrange("p k n -> p (k n)"), w2[bass.ds(block * P, P), :])\
                    .then_inc(F.raw_in[slot], 16)

            def ada_piece(pair, i, first):
                n = pair * ADA_PER_PAIR + i
                if not F.ada:
                    return
                if i or not first:
                    sp.wait_ge(ada_used, n)
                sp.dma_start(ada_raw[:], ada_view[:, :, bass.ds((ADA_EARLY + n) * P, P)]).then_inc(ada_in, 16)

            def pair_pieces(pair, first, last):
                q = piece_of(pair, 0)
                for i in range(2):
                    sp.wait_ge(F.lo, q + i - 1)
                    w13_piece(q + i, i, 2 * pair + 1, i)
                ada_piece(pair, 0, first)
                for i in range(2):
                    sp.wait_ge(F.lo, q + 2 + i - 1)
                    w2_piece(i, 2 * pair + i)
                ada_piece(pair, 1, first)
                if not last:
                    for i in range(2):
                        sp.wait_ge(F.lo, q + 4 + i - 1)
                        w13_piece(q + 4 + i, i, 2 * pair + 2, i)
                for i in range(2, ADA_PER_PAIR):
                    ada_piece(pair, i, first)

            for i in range(2):
                w13_piece(i, i, 0, i)
            pair_pieces(0, True, False)
            with sp.Fori(1, PAIRS - 1) as pair:
                pair_pieces(pair, False, False)
            pair_pieces(PAIRS - 1, False, True)
            if F.ada:
                ada_last = PAIRS * ADA_PER_PAIR
                sp.wait_ge(ada_used, ada_last)
                sp.dma_start(ada_raw[:], ada_view[:, :, (ADA_EARLY + ada_last) * P:(ADA_EARLY + ada_last + 1) * P])\
                    .then_inc(ada_in, 16)

        def split_target(q_in_pair):
            if q_in_pair in (0, 1):
                return w13h[:, 1, q_in_pair], w13l[:, 1, q_in_pair]
            if q_in_pair in (2, 3):
                i = q_in_pair - 2
                return (w2h[:, i].rearrange("p (k n) -> p k n", k=KD), w2l[:, i].rearrange("p (k n) -> p k n", k=KD))
            return w13h[:, 0, q_in_pair - 4], w13l[:, 0, q_in_pair - 4]

        def ffn_act(act, F):
            per = 2 * F.n

            def split_high(q, count, to, slot, free_sem=None, free=None):
                act.wait_ge(F.raw_in[slot], count)
                if free_sem is not None:
                    act.wait_ge(free_sem, free)
                nc.scalar.activation(to[0], raw[:, slot], ACT.Copy).then_inc(F.hi, 1)

            def glu_act(pair, first, b, n):
                g = pair * per + b * F.n + n
                at, size = F.chunks[n]
                k = (b * F.n + n) % 2
                act.wait_ge(F.ab_ready, g + 1)
                if not (first and b == 0 and n == 0):
                    act.wait_ge(F.glu_ready, g)
                nc.scalar.activation(glu_sig[:, 0:size], psum[:, 2 * k, 0:size], ACT.Silu).then_inc(F.sig_ready, 1)
                act.wait_ge(F.glu_ready, g + 1)
                if not first:
                    act.wait_ge(F.y_ready, 2 * F.tiles * pair)
                nc.scalar.activation(gh[:, b, at:at + size], glu[:, 0:size], ACT.Copy).then_inc(F.gh_ready, 1)

            def body(pair, first, last):
                def splits(i0, free_sem, free):
                    for i in (i0, i0 + 1):
                        q = piece_of(pair, i)
                        split_high(q, 16 * (3 * pair + 2 + i // 2), split_target(i), i % 2,
                                   free_sem, free)
                splits(0, None if first else F.ab_ready, per * pair)
                glu_act(pair, first, 0, 0)
                splits(2, None if first else F.y_ready, 2 * F.tiles * pair)
                for n in range(1, F.n):
                    glu_act(pair, first, 0, n)
                glu_act(pair, first, 1, 0)
                if not last:
                    splits(4, F.ab_ready, per * pair + F.n)
                for n in range(1, F.n):
                    glu_act(pair, first, 1, n)

            for i in range(2):
                split_high(i, 16, (w13h[:, 0, i], None), i)
            body(0, True, False)
            with act.Fori(1, PAIRS - 1) as pair:
                body(pair, False, False)
            body(PAIRS - 1, False, True)

        def ffn_dve(dve, F, before_last_y, tile_summed):
            per = 2 * F.n

            def split_low(q, to, slot):
                dve.wait_ge(F.hi, q + 1)
                nc.vector.tensor_tensor(to[1], raw[:, slot], to[0].bitcast(F32), ALU.subtract).then_inc(F.lo, 1)

            def glu_dve(pair, first, b, n):
                g = pair * per + b * F.n + n
                at, size = F.chunks[n]
                k = (b * F.n + n) % 2
                dve.wait_ge(F.sig_ready, g + 1)
                if not (first and b == 0 and n == 0):
                    dve.wait_ge(F.gl_ready, g)
                nc.vector.tensor_tensor(glu[:, 0:size], psum[:, 2 * k + 1, 0:size], glu_sig[:, 0:size],
                                        ALU.mult).then_inc(F.glu_ready, 1)
                dve.wait_ge(F.gh_ready, g + 1)
                nc.vector.tensor_tensor(gl[:, b, at:at + size], glu[:, 0:size],
                                        gh[:, b, at:at + size].bitcast(F32), ALU.subtract).then_inc(F.gl_ready, 1)

            def body(pair, first, last):
                def splits(i0):
                    for i in (i0, i0 + 1):
                        split_low(piece_of(pair, i), split_target(i), i % 2)
                splits(0)
                glu_dve(pair, first, 0, 0)
                splits(2)
                for n in range(1, F.n):
                    glu_dve(pair, first, 0, n)
                glu_dve(pair, first, 1, 0)
                if not last:
                    splits(4)
                for n in range(1, F.n):
                    glu_dve(pair, first, 1, n)
                if F.ada:
                    dve.wait_ge(ada_used, ADA_PER_PAIR * (pair + 1))
                    at = ADA_EARLY + ADA_PER_PAIR * pair
                    nc.vector.tensor_tensor(
                        mod[:, bass.ds(at, ADA_PER_PAIR), :],
                        psum[:, 7, 0:2 * ADA_PER_PAIR].rearrange("p (a b) -> p a b", b=2),
                        params[:, bass.ds(at, ADA_PER_PAIR)].unsqueeze(2).to_broadcast([P, ADA_PER_PAIR, 2]),
                        ALU.add).then_inc(mod_ready, 1)
                if last:
                    before_last_y(dve)
                if not first:
                    dve.wait_ge(F.y_summed, 2 * F.tiles * pair)
                for u in range(2 * F.tiles):
                    dve.wait_ge(F.y_ready, 2 * F.tiles * pair + u + 1)
                    rows = y[:, u // 2, (u % 2) * BANK:(u % 2 + 1) * BANK]
                    bank = psum[:, Y_BANKS[u % 3], :]
                    if first:
                        nc.vector.tensor_copy(rows, bank).then_inc(F.y_summed, 1)
                    else:
                        nc.vector.tensor_tensor(rows, bank, rows, ALU.add).then_inc(F.y_summed, 1)
                    if last and u % 2 == 1:
                        dve.wait_ge(F.y_summed, 2 * F.tiles * pair + u + 1)
                        tile_summed(dve, u // 2)

            for i in range(2):
                split_low(i, (w13h[:, 0, i], w13l[:, 0, i]), i)
            body(0, True, False)
            with dve.Fori(1, PAIRS - 1) as pair:
                body(pair, False, False)
            body(PAIRS - 1, False, True)

        def ffn_pe(pe, F, turn, before_last_y):
            per = 2 * F.n
            units = 2 * F.tiles
            prev_user = {u: (u - 3 if u >= 3 else max(v for v in range(units) if v % 3 == u) - units)
                         for u in range(units)}

            def ada(pair, i):
                if not F.ada:
                    return
                n = pair * ADA_PER_PAIR + i
                if i == 0:
                    pe.wait_ge(mod_ready, pair + 1)
                pe.wait_ge(ada_in, 16 * (n + 1))
                for k in range(KD):
                    last = nc.tensor.matmul(psum[:, 7, 2 * i:2 * i + 2], ada_raw[:, k, :], more_c[:, k, :],
                                            start=k == 0, stop=k == KD - 1)
                last.then_inc(ada_used, 1)

            def body(pair, first, last_pair):
                for b in range(2):
                    pe.wait_ge(F.lo, piece_of(pair, 0) + 2 * b)
                    for n, (at, size) in enumerate(F.chunks):
                        g = pair * per + b * F.n + n
                        k2 = (b * F.n + n) % 2
                        if first and b == 0:
                            pe.wait_ge(turn.low, KD * (n + 1))
                        if not (first and b * F.n + n < 2):
                            pe.wait_ge(F.glu_ready, g - 1)
                        for part in range(2):
                            o = psum[:, 2 * k2 + part, 0:size]
                            for k in range(KD):
                                wh, wl = w13h[:, b, part, k], w13l[:, b, part, k]
                                high, low = xpart(0, k, at, size), xpart(1, k, at, size)
                                nc.tensor.matmul(o, wh, high, start=k == 0, stop=False)
                                nc.tensor.matmul(o, wh, low, start=False, stop=False)
                                last = nc.tensor.matmul(o, wl, high, start=False, stop=k == KD - 1)
                        last.then_inc(F.ab_ready, 1)
                        if b * F.n + n < ADA_PER_PAIR:
                            ada(pair, b * F.n + n)
                if last_pair:
                    before_last_y(pe)
                pe.wait_ge(F.lo, piece_of(pair, 4))
                for u in range(units):
                    t, half = u // 2, u % 2
                    n = next(i for i, (at, size) in enumerate(F.chunks) if at <= t * P < at + size)
                    if half == 0 and (t * P == F.chunks[n][0]):
                        pe.wait_ge(F.gl_ready, pair * per + F.n + n + 1)
                    if not first or u >= 3:
                        pe.wait_ge(F.y_summed, units * pair + prev_user[u] + 1)
                    o = psum[:, Y_BANKS[u % 3], :]
                    cols = slice(half * BANK, (half + 1) * BANK)
                    for b in range(2):
                        lh, ll = gh[:, b, t * P:(t + 1) * P], gl[:, b, t * P:(t + 1) * P]
                        nc.tensor.matmul(o, lh, w2h[:, b, cols], start=b == 0, stop=False)
                        nc.tensor.matmul(o, lh, w2l[:, b, cols], start=False, stop=False)
                        last = nc.tensor.matmul(o, ll, w2h[:, b, cols], start=False, stop=b == 1)
                    last.then_inc(F.y_ready, 1)

            body(0, True, False)
            with pe.Fori(1, PAIRS - 1) as pair:
                body(pair, False, False)
            body(PAIRS - 1, False, True)

        class Norm:

            def __init__(self, name):
                self.gates_summed = sem(name + "_gates_summed")
                self.gates_kept = sem(name + "_gates_kept")
                self.rows_in = [sem(f"{name}_rows_in{i}") for i in range(3)]
                self.added = sem(name + "_added")
                self.measured = sem(name + "_measured")
                self.inverted = sem(name + "_inverted")
                self.done = sem(name + "_done")
                self.affined = sem(name + "_affined")

        def gate_rows_pe(pe, N, which, vectors):
            for v in range(vectors):
                for k in range(KD):
                    column = mod[:, which * KD + k, v:v + 1].to_broadcast([P, P])
                    last = nc.tensor.matmul(psum[:, 2 * v + k // 4, (k % 4) * P:(k % 4 + 1) * P], column, ident[:],
                                            start=True, stop=True)
            last.then_inc(N.gates_summed, 1)

        def gate_rows_act(act, N, vectors, scale):
            act.wait_ge(N.gates_summed, 1)
            for v in range(vectors):
                for half in range(2):
                    nc.scalar.activation(gate_row[:, v, half * BANK:(half + 1) * BANK], psum[:, 2 * v + half, :],
                                         ACT.Copy, scale=scale).then_inc(N.gates_kept, 1)

        def norm_sums_dve(dve, N, t, residual):
            s = ln_stats[:, t % 2]
            if t >= 2:
                dve.wait_ge(N.done, t - 1)
            for half in range(2):
                step(dve, nc.vector.bn_stats(s[:, 6 * half:6 * half + 6], y[:, t, half * BANK:(half + 1) * BANK]))
            step(dve, nc.vector.bn_aggr(s[:, 12:14], s[:, 0:12].rearrange("p (a b) -> p a b", b=6)))
            step(dve, nc.vector.tensor_scalar_add(s[:, 14:15], s[:, 13:14], LN_EPS))
            nc.vector.tensor_scalar_mul(s[:, 15:16], s[:, 12:13], -1.0).then_inc(N.measured, 1)

        def norm_pool(pool, N, t):
            s = ln_stats[:, t % 2]
            pool.wait_ge(N.measured, t + 1)
            nc.gpsimd.tensor_tensor(s[:, 16:17], s[:, 14:15], minus_half[:, 0:1], ALU.pow).then_inc(N.inverted, 1)
            pool.wait_ge(N.inverted, 2 * t + 1)
            nc.gpsimd.tensor_tensor(s[:, 17:18], s[:, 15:16], s[:, 16:17], ALU.mult).then_inc(N.inverted, 1)

        def norm_act(act, N, t):
            s = ln_stats[:, t % 2]
            act.wait_ge(N.inverted, 2 * t + 2)
            nc.scalar.activation(y[:, t, :], y[:, t, :], ACT.Identity, bias=s[:, 17:18], scale=s[:, 16:17])\
                .then_inc(N.done, 1)

        def ffn_residual_dve(dve, F, N, vectors):
            def tile_summed(dve, t):
                if t == 0:
                    dve.wait_ge(N.gates_kept, 2 * vectors)
                step(dve, nc.vector.tensor_tensor(y[:, t, :], y[:, t, :], gate_row[:, int(t >= TL), :], ALU.mult))
                dve.wait_ge(N.rows_in[t % 3], 16 * (t // 3 + 1))
                nc.vector.scalar_tensor_tensor(y[:, t, :], res_row[:, t % 3, :], ALPHA, y[:, t, :],
                                               op0=ALU.mult, op1=ALU.add).then_inc(N.added, 1)
                dve.wait_ge(N.added, t + 1)
                norm_sums_dve(dve, N, t, None)
            return tile_summed

        def affine_of(dve, norm, scale_at, shift_at):
            gain = params[:, 72 + norm * KD:72 + (norm + 1) * KD].unsqueeze(1).to_broadcast([P, 2, KD])
            bias = params[:, 96 + norm * KD:96 + (norm + 1) * KD].unsqueeze(1).to_broadcast([P, 2, KD])
            scale = mod[:, scale_at * KD:(scale_at + 1) * KD, :].rearrange("p k v -> p v k")
            shift = mod[:, shift_at * KD:(shift_at + 1) * KD, :].rearrange("p k v -> p v k")
            step(dve, nc.vector.scalar_tensor_tensor(in_scale[:], scale, 1.0, gain, op0=ALU.add, op1=ALU.mult))
            step(dve, nc.vector.scalar_tensor_tensor(in_shift[:], scale, 1.0, bias, op0=ALU.add, op1=ALU.mult))
            step(dve, nc.vector.tensor_tensor(in_shift[:], in_shift[:], shift, ALU.add))

        UNITS = [("k", OFF_K, OFF_K + P, 0), ("k", OFF_K + 2 * P, OFF_K + 3 * P, 1),
                 ("q", OFF_Q, OFF_Q + P, 0), ("q", OFF_Q + 2 * P, OFF_Q + 3 * P, 1),
                 ("v", OFF_V, OFF_V + P, 0), ("v", OFF_V + 2 * P, OFF_V + 3 * P, 1),
                 ("kv", OFF_KA, OFF_VA, 0),
                 ("qa", OFF_QA, OFF_QA + 2 * P, 0), ("qa", OFF_QA + P, OFF_QA + 3 * P, 1),
                 ("o", OFF_O, OFF_O + P, 0), ("o", OFF_O + 2 * P, OFF_O + 3 * P, 1)]

        def outputs():
            out = [("gates", -1, 0, at, size) for at, size in CHUNKS_ALL]
            for u, (kind, _, _, which) in enumerate(UNITS):
                if kind in "kq":
                    for half in range(2):
                        for at, size in (CHUNKS_ALL if kind == "k" else CHUNKS_LAT):
                            out.append((kind, u, 2 * which + half, at, size))
                else:
                    for t in range(TA if kind in ("v", "kv") else TL):
                        out.append((kind, u, which, t * P, P))
            return out

        OUTPUTS = outputs()
        P_BANKS = 7
        by_vector = [kind in ("kv", "qa") for kind, *_ in OUTPUTS]

        def read_before(j, vector):
            return sum(1 for i in range(j + 1) if by_vector[i] == vector)

        p_in = [sem(f"p_in{i}") for i in range(2)]
        gate_in = sem("gate_in")
        gate_clear = sem("gate_clear")
        gate_w = sem("gate_w")
        gate_low = sem("gate_low")
        p_hi = sem("p_hi")
        p_lo = sem("p_lo")
        p_ready = sem("p_ready")
        p_read_act = sem("p_read_act")
        p_read_dve = sem("p_read_dve")
        conv_done = sem("conv_done")
        conv_kept = sem("conv_kept")
        q_scaled = sem("q_scaled")
        x1_stored = sem("x1_stored")
        rope_in = sem("rope_in")
        roped = sem("roped")
        rope_turned = sem("rope_turned")
        rope_kept = sem("rope_kept")
        o_stored = [sem(f"o_stored{i}") for i in range(2)]
        pads_set = sem("pads_set")
        gate_step_act = sem("gate_step_act")
        gate_step_dve = sem("gate_step_dve")
        gate_args = sem("gate_args")
        gate_exps = sem("gate_exps")
        gate_copies = sem("gate_copies")
        gate_turned = sem("gate_turned")
        gate_kept = sem("gate_kept")
        ROPED = [j for j, (kind, u, which, at, size) in enumerate(OUTPUTS)
                 if kind == "qa" or kind == "kv"]

        def unit_last(u):
            return max(j for j, o in enumerate(OUTPUTS) if o[1] == u)

        def proj_sp(sp):
            sp.wait_ge(F1.y_ready, 2 * TA * PAIRS)
            sp.dma_start(gate_raw[:], w_in_view[:, :, OFF_G:OFF_G + 16]).then_inc(gate_in, 16)
            sp.wait_ge(gate_clear, 1)
            for row, at in ((0, 0), (32, 8), (64, 4), (96, 12)):
                sp.dma_start(gate_bias[row:row + 4, :], b_gates[0, at:at + 4].rearrange("(p a) -> p a", a=1))\
                    .then_inc(gate_in, 16)

            def piece(q):
                if q >= 2:
                    sp.wait_ge(p_lo, q - 1)
                at = UNITS[q // 2][1 + q % 2]
                sp.dma_start(p_raw[:, q % 2], w_in_view[:, :, at:at + P]).then_inc(p_in[q % 2], 16)
            piece(0)
            piece(1)
            for t in range(TL):
                sp.wait_ge(N1.done, t + 1)
                sp.dma_start(x1_dram[t], y[:, t, :]).then_inc(x1_stored, 16)
            for q in range(2, 2 * len(UNITS)):
                piece(q)
                if UNITS[q // 2][0] == "kv" and q % 2 == 0:
                    sp.wait_ge(conv_kept, 8)
                    for t in range(TL):
                        sp.dma_start(rope_tab[:, t], rope_cs[:, t * P:(t + 1) * P, :].rearrange("s p f -> p s f"))\
                            .then_inc(rope_in, 16)
            n = 0
            for j, (kind, u, which, at, size) in enumerate(OUTPUTS):
                if kind == "o":
                    sp.wait_ge(p_read_act, read_before(j, False))
                    sp.dma_start(o_dram[at // P, :, which * 256:(which + 1) * 256], o_sig[:, n % 2]).then_inc(o_stored[n % 2], 16)
                    n += 1

        def spans(row):
            def nat(t, at, size):
                part = t[row:row + 32, at:at + size]
                return part if row == 0 else part[:, ::-1]
            return [(slice(0, N_CTX), lambda t: nat(t, N_LAT, N_CTX)),
                    (slice(N_CTX, N_ALL), lambda t: nat(t, 0, N_LAT))]

        def proj_act(act):
            def high(q):
                u = q // 2
                act.wait_ge(p_in[q % 2], 16 * (q // 2 + 1))
                if u >= 2:
                    act.wait_ge(p_ready, unit_last(u - 2) + 1)
                elif u == 1:
                    act.wait_ge(p_ready, 3)
                nc.scalar.activation(p_wh[:, u % 2, :, (q % 2) * P:(q % 2 + 1) * P], p_raw[:, q % 2], ACT.Copy)\
                    .then_inc(p_hi, 1)
            act.wait_ge(gate_clear, 2)
            act.wait_ge(gate_in, 16 * 5)
            for row, at in ((0, 0), (32, 8), (64, 4), (96, 12)):
                nc.scalar.activation(gate_wh[:, :, row:row + 4], gate_raw[:, :, at:at + 4], ACT.Copy).then_inc(gate_w, 1)
            high(0)
            high(1)
            conv_n = 0
            o_n = 0
            kept = 0
            for j, (kind, u, which, at, size) in enumerate(OUTPUTS):
                first_of_unit = j == 0 or OUTPUTS[j - 1][1] != u
                if first_of_unit and kind != "gates" and u + 1 < len(UNITS):
                    high(2 * u + 2)
                    high(2 * u + 3)
                bank = psum[:, j % P_BANKS, :]
                if kind == "gates":
                    act.wait_ge(p_ready, j + 1)
                    nc.scalar.activation(gate_all[:, at:at + size], bank[:, 0:size], ACT.Identity, bias=gate_bias[:, 0:1])\
                        .then_inc(p_read_act, 1)
                    if at >= N_LAT:
                        gates_act_logs(act)
                elif kind in "kq":
                    act.wait_ge(p_ready, j + 1)
                    if at == 0 and conv_n:
                        act.wait_ge(conv_done, conv_n)
                    if at == 0 and not conv_n:
                        act.wait_ge(pads_set, 1)
                        act.wait_ge(x1_stored, 16 * TL)
                    to = 2 + at if at < N_LAT else 1030 + at - N_LAT
                    nc.scalar.activation(conv_in[:, to:to + size], bank[:, 0:size], ACT.Copy).then_inc(p_read_act, 1)
                    last = at + size == (N_ALL if kind == "k" else N_LAT)
                    if last:
                        conv_n += 1
                        act.wait_ge(conv_done, conv_n)
                        dst = (kT if kind == "k" else qT)[:, which, :]
                        inst = nc.scalar.activation(dst[:, 0:N_LAT], conv_sum[:, 0:N_LAT], ACT.Silu)
                        if kind == "k":
                            inst = nc.scalar.activation(dst[:, N_LAT:N_ALL], conv_sum[:, 1028:1028 + N_CTX], ACT.Silu)
                        inst.then_inc(conv_kept, 1)
                        if conv_n == 1:
                            gates_act_exps(act)
                elif kind == "v":
                    act.wait_ge(p_ready, j + 1)
                    nc.scalar.activation(vext[:, at // P, 2 * which:2 * which + 2, 0:M_DH],
                                         bank[:, 0:256].rearrange("p (h d) -> p h d", h=2), ACT.Copy).then_inc(p_read_act, 1)
                elif kind == "o":
                    act.wait_ge(p_ready, j + 1)
                    if o_n >= 2:
                        act.wait_ge(o_stored[o_n % 2], 16 * (o_n // 2))
                    nc.scalar.activation(o_sig[:, o_n % 2], bank[:, 0:256], ACT.Sigmoid).then_inc(p_read_act, 1)
                    o_n += 1
                else:
                    act.wait_ge(rope_turned, kept + 1)
                    t = at // P
                    if kind == "kv":
                        nc.scalar.activation(kaT[:, at:at + P], psum[:, 7, 0:P], ACT.Copy).then_inc(rope_kept, 1)
                    else:
                        nc.scalar.activation(qaT[:, 2 * which:2 * which + 2, at:at + P],
                                             psum[:, 7, 0:256].rearrange("p (a b) -> p a b", a=2), ACT.Copy,
                                             scale=A_DH ** -0.5).then_inc(rope_kept, 1)
                    kept += 1

        def gates_act_logs(act):
            act.wait_ge(gate_step_dve, 1)
            nc.scalar.activation(gate_abs[64:P, :], gate_abs[64:P, :], ACT.Exp, scale=-1.0).then_inc(gate_step_act, 1)
            act.wait_ge(gate_step_act, 1)
            nc.scalar.activation(gate_abs[64:P, :], gate_abs[64:P, :], ACT.Ln, bias=1.0).then_inc(gate_step_act, 1)

        def gates_act_exps(act):
            act.wait_ge(gate_args, 1)
            nc.scalar.activation(decay[0:64, 20:30], decay[0:64, 20:30], ACT.Exp)
            for row in (0, 32):
                (c_scan, c_nat), (l_scan, l_nat) = spans(row)
                rows = slice(row, row + 32)
                nc.scalar.activation(c_nat(w_nat), e_row[rows, c_scan], ACT.Exp)
                nc.scalar.activation(l_nat(w_nat), e_row[rows, l_scan], ACT.Exp)
                nc.scalar.activation(l_nat(inter_nat), lf_row[rows, l_scan], ACT.Exp)
                last = nc.scalar.activation(l_nat(floor_nat), m_row[rows, l_scan], ACT.Exp, scale=-1.0)
            last.then_inc(gate_exps, 1)

        def gates_dve(dve):
            n = [0]

            def gstep(i):
                n[0] += 1
                i.then_inc(gate_step_dve, 1)
                dve.wait_ge(gate_step_dve, n[0])
            dve.wait_ge(p_read_act, 3)
            f = gate_all[64:P, :]
            gstep(nc.vector.scalar_tensor_tensor(gate_abs[64:P, :], f, -1.0, f, op0=ALU.mult, op1=ALU.max))
            gstep(nc.vector.tensor_scalar_min(f, f, 0.0))
            dve.wait_ge(gate_step_act, 2)
            gstep(nc.vector.tensor_tensor(f, f, gate_abs[64:P, :], ALU.subtract))
            for row in (0, 32):
                rows = slice(row, row + 32)
                for scan, nat in spans(row):
                    nc.vector.tensor_copy(li_row[rows, scan], nat(gate_all))
            for row in (0, 32):
                rows = slice(row, row + 32)
                for scan, nat in spans(row):
                    src = gate_all[64 + row:96 + row, :]
                    cols = src[:, N_LAT:N_ALL] if scan.start == 0 else src[:, 0:N_LAT]
                    last = nc.vector.tensor_copy(lf_row[rows, scan], cols if row == 0 else cols[:, ::-1])
            gstep(last)
            for t in range(TA):
                cols = slice(t * P, (t + 1) * P)
                nc.vector.tensor_tensor_scan(b_row[0:64, cols], lf_row[0:64, cols], lf_row[0:64, cols], 0.0,
                                             ALU.add, ALU.bypass)
            gstep(nc.vector.tensor_tensor_scan(m_row[0:64, :], lf_row[0:64, :], li_row[0:64, :], 0.0, ALU.add, ALU.max))
            gstep(nc.vector.tensor_tensor(a_row[0:64, :], li_row[0:64, :], b_row[0:64, :], ALU.subtract))
            gstep(nc.vector.tensor_tensor(b_row[0:64, :], b_row[0:64, :], m_row[0:64, :], ALU.subtract))
            ends = slice(P - 1, N_ALL, P)
            nc.vector.tensor_copy(decay[0:64, 0:TA], b_row[0:64, ends])
            nc.vector.memset(decay[0:64, TA:TA + 1], 0.0)
            gstep(nc.vector.tensor_copy(decay[0:64, TA + 1:2 * TA], m_row[0:64, P - 1:N_ALL - P:P]))
            by_chunk = lambda t: t[0:64, :].rearrange("p (c t) -> p c t", t=P)
            wide = lambda at: decay[0:64, at:at + TA].unsqueeze(2).to_broadcast([64, TA, P])
            nc.vector.tensor_tensor(decay[0:64, 20:30], decay[0:64, 0:TA], decay[0:64, TA:2 * TA], ALU.add)
            nc.vector.tensor_tensor(by_chunk(e_row), by_chunk(a_row), wide(0), ALU.add)
            nc.vector.tensor_tensor(by_chunk(lf_row), by_chunk(b_row), wide(TA), ALU.add).then_inc(gate_args, 1)
            for row in (0, 32):
                rows = slice(row, row + 32)
                for scan, nat in spans(row):
                    nc.vector.tensor_copy(nat(a_nat), a_row[rows, scan])
                    last = nc.vector.tensor_copy(nat(u_row), b_row[rows, scan])
            last.then_inc(gate_copies, 1)

        GATE_TURNS = [(i, t) for i in range(4) for t in range(TA if i < 2 else TL)]
        GATE_ROUNDS = [GATE_TURNS[i:i + 8] for i in range(0, len(GATE_TURNS), 8)]

        def gates_pe(pe):
            pe.wait_ge(gate_exps, 1)
            pe.wait_ge(gate_copies, 1)
            for r, turns in enumerate(GATE_ROUNDS):
                if r:
                    pe.wait_ge(gate_kept, r)
                for n, (i, t) in enumerate(turns):
                    src = (a_nat, w_nat, inter_nat, floor_nat)[i][0:64, t * P:(t + 1) * P]
                    last = nc.tensor.transpose(psum[:, 7, 64 * n:64 * (n + 1)], src, ident[0:64, 0:64])
                if r == len(GATE_ROUNDS) - 1:
                    for i in range(2 * M_HEADS):
                        row = 32 * (i // M_HEADS) + i % M_HEADS
                        last = nc.tensor.matmul(psum[:, 7, 256 + 10 * i:266 + 10 * i],
                                                ident[0:64, row:row + 1].to_broadcast([64, P]), decay[0:64, 20:30],
                                                start=True, stop=True)
                last.then_inc(gate_turned, 1)

        def gates_keep_dve(dve):
            for r, turns in enumerate(GATE_ROUNDS):
                dve.wait_ge(gate_turned, r + 1)
                for i in range(4):
                    mine = [(n, t) for n, (q, t) in enumerate(turns) if q == i]
                    if mine:
                        n0, n1 = mine[0][0], mine[-1][0] + 1
                        t0, t1 = mine[0][1], mine[-1][1] + 1
                        last = nc.vector.tensor_copy(
                            tok_gate[:, i, t0:t1].rearrange("p t (d h) -> p t d h", d=2),
                            psum[:, 7, 64 * n0:64 * n1].rearrange("p (t d r) -> p t d r", d=2, r=32)[:, :, :, 0:M_HEADS])
                if r == len(GATE_ROUNDS) - 1:
                    last = nc.vector.tensor_copy(decay_all[:], psum[:, 7, 256:336].rearrange("p (r c) -> p r c", c=TA))
                last.then_inc(gate_kept, 1)

        def proj_dve(dve):
            for i in range(4):
                row, at = ((0, 0), (32, 8), (64, 4), (96, 12))[i]
                dve.wait_ge(gate_w, i + 1)
                nc.vector.tensor_tensor(gate_wl[:, :, row:row + 4], gate_raw[:, :, at:at + 4],
                                        gate_wh[:, :, row:row + 4].bitcast(F32), ALU.subtract).then_inc(gate_low, 1)

            def low(q):
                u = q // 2
                dve.wait_ge(p_hi, q + 1)
                cols = slice((q % 2) * P, (q % 2 + 1) * P)
                nc.vector.tensor_tensor(p_wl[:, u % 2, :, cols], p_raw[:, q % 2], p_wh[:, u % 2, :, cols].bitcast(F32),
                                        ALU.subtract).then_inc(p_lo, 1)
            low(0)
            low(1)
            conv_n = 0
            kept = 0
            for j, (kind, u, which, at, size) in enumerate(OUTPUTS):
                first_of_unit = j == 0 or OUTPUTS[j - 1][1] != u
                if first_of_unit and kind != "gates" and u + 1 < len(UNITS):
                    low(2 * u + 2)
                    low(2 * u + 3)
                bank = psum[:, j % P_BANKS, :]
                if kind == "q" and which == 0 and at == 0:
                    gates_keep_dve(dve)
                if kind == "kv" and at == 0:
                    nc.vector.memset(vext[:, :, :, M_DH:M_DH + 1], 1.0)
                if kind == "gates" and at >= N_LAT:
                    gates_dve(dve)
                elif kind in "kq" and at + size == (N_ALL if kind == "k" else N_LAT):
                    dve.wait_ge(p_read_act, read_before(j, False))
                    if conv_n:
                        dve.wait_ge(conv_kept, conv_n)
                    size = 1284 if kind == "k" else N_LAT
                    col = which + (4 if kind == "k" else 0)
                    w = [more[:, 16 + 8 * i + col:17 + 8 * i + col] for i in range(CONV_W)]
                    step(dve, nc.vector.tensor_scalar(conv_sum[:, 0:size], conv_in[:, 0:size], w[0],
                                                      more[:, 56 + col:57 + col], ALU.mult, ALU.add))
                    for i in range(1, CONV_W):
                        last = nc.vector.scalar_tensor_tensor(conv_sum[:, 0:size], conv_in[:, i:i + size], w[i],
                                                              conv_sum[:, 0:size], op0=ALU.mult, op1=ALU.add)
                        if i < CONV_W - 1:
                            step(dve, last)
                    conv_n += 1
                    last.then_inc(conv_done, 1)
                    if kind == "q":
                        dve.wait_ge(conv_kept, conv_n)
                        nc.vector.tensor_scalar_mul(qT[:, which, :], qT[:, which, :], M_DH ** -0.5).then_inc(q_scaled, 1)
                elif kind in ("kv", "qa"):
                    t = at // P
                    dve.wait_ge(p_ready, j + 1)
                    if kept == 0:
                        dve.wait_ge(rope_in, 16 * TL)
                    if kept >= 2:
                        dve.wait_ge(rope_turned, kept - 1)
                    out = rope_out[:, kept % 2]
                    if kind == "kv" and t >= TL:
                        nc.vector.tensor_copy(out[:, 0:P], bank[:, 0:P]).then_inc(roped, 1)
                    else:
                        n = 1 if kind == "kv" else 2
                        w = 2 * n * A_DH
                        src = bank[:, 0:w].rearrange("p (h s f) -> p h s f", s=2, f=A_DH // 2)
                        ta = rope_ab[:, 0, 0:w].rearrange("p (h s f) -> p h s f", s=2, f=A_DH // 2)
                        tb = rope_ab[:, 1, 0:w].rearrange("p (h s f) -> p h s f", s=2, f=A_DH // 2)
                        cs = [rope_tab[:, t, i].unsqueeze(1).to_broadcast([P, 2 * n, A_DH // 2]) for i in range(2)]
                        for s in range(2):
                            step(dve, nc.vector.tensor_tensor(ta[:, :, s], src[:, :, s], cs[0], ALU.mult))
                            step(dve, nc.vector.tensor_tensor(tb[:, :, 1 - s], src[:, :, s], cs[1], ALU.mult))
                        o = out[:, 0:w].rearrange("p (i g s f) -> p g i s f", g=2, s=2, f=A_DH // 2)
                        a = rope_ab[:, 0, 0:w].rearrange("p (g i s f) -> p g i s f", g=2, s=2, f=A_DH // 2)
                        b = rope_ab[:, 1, 0:w].rearrange("p (g i s f) -> p g i s f", g=2, s=2, f=A_DH // 2)
                        step(dve, nc.vector.tensor_tensor(o[:, :, :, 0], a[:, :, :, 0], b[:, :, :, 0], ALU.subtract))
                        nc.vector.tensor_tensor(o[:, :, :, 1], a[:, :, :, 1], b[:, :, :, 1], ALU.add).then_inc(roped, 1)
                    kept += 1
                    if kind == "kv":
                        nc.vector.tensor_copy(va[:, t, :], bank[:, P:2 * P]).then_inc(p_read_dve, 1)
                    else:
                        dve.wait_ge(roped, kept)
                        nc.vector.tensor_copy(minus_half[:, 1:2], minus_half[:, 0:1]).then_inc(p_read_dve, 1)

        def proj_pe(pe):
            kept = 0

            def turn_roped(i):
                j = ROPED[i]
                kind, u, which, at, size = OUTPUTS[j]
                pe.wait_ge(roped, i + 1)
                if i >= 1:
                    pe.wait_ge(rope_kept, i)
                for n in range(1 if kind == "kv" else 2):
                    last = nc.tensor.transpose(psum[:, 7, n * P:(n + 1) * P], rope_out[:, i % 2, n * P:(n + 1) * P], ident[:])
                last.then_inc(rope_turned, 1)

            for j, (kind, u, which, at, size) in enumerate(OUTPUTS):
                o = psum[:, j % P_BANKS, :]
                if j < P_BANKS:
                    if j == 0:
                        pe.wait_ge(T2.scaled, len(T2.units))
                        pe.wait_ge(F1.y_summed, 2 * TA * PAIRS)
                else:
                    i = j - P_BANKS
                    pe.wait_ge(p_read_dve if by_vector[i] else p_read_act, read_before(i, by_vector[i]))
                if kind == "gates":
                    n = CHUNKS_ALL.index((at, size))
                    if n == 0:
                        pe.wait_ge(gate_low, 4)
                    pe.wait_ge(T2.low, KD * (n + 1))
                    for k in range(KD):
                        high, low = xpart(0, k, at, size), xpart(1, k, at, size)
                        nc.tensor.matmul(o[:, 0:size], gate_wh[:, k, :], high, start=k == 0, stop=False)
                        nc.tensor.matmul(o[:, 0:size], gate_wh[:, k, :], low, start=False, stop=False)
                        last = nc.tensor.matmul(o[:, 0:size], gate_wl[:, k, :], high, start=False, stop=k == KD - 1)
                    last.then_inc(p_ready, 1)
                    continue
                if kind == "q" and which == 0 and at == 0:
                    gates_pe(pe)
                if OUTPUTS[j - 1][1] != u:
                    pe.wait_ge(p_lo, 2 * u + 2)
                if kind in "kq":
                    cols = slice((which % 2) * P, (which % 2 + 1) * P)
                    for k in range(KD):
                        high, low = xpart(0, k, at, size), xpart(1, k, at, size)
                        wh, wl = p_wh[:, u % 2, k, cols], p_wl[:, u % 2, k, cols]
                        nc.tensor.matmul(o[:, 0:size], wh, high, start=k == 0, stop=False)
                        nc.tensor.matmul(o[:, 0:size], wh, low, start=False, stop=False)
                        last = nc.tensor.matmul(o[:, 0:size], wl, high, start=False, stop=k == KD - 1)
                else:
                    for k in range(KD):
                        high, low = xpart(0, k, at, P), xpart(1, k, at, P)
                        wh, wl = p_wh[:, u % 2, k, :], p_wl[:, u % 2, k, :]
                        nc.tensor.matmul(o[:, 0:256], high, wh, start=k == 0, stop=False)
                        nc.tensor.matmul(o[:, 0:256], high, wl, start=False, stop=False)
                        last = nc.tensor.matmul(o[:, 0:256], low, wh, start=False, stop=k == KD - 1)
                last.then_inc(p_ready, 1)
                if j - 2 >= ROPED[0] and kept < len(ROPED):
                    turn_roped(kept)
                    kept += 1
            while kept < len(ROPED):
                turn_roped(kept)
                kept += 1

        STEPS = [(0, TL), (1, TL + 1), (0, TL + 1), (1, TL)]
        for s_ in range(TL):
            STEPS += [(0, s_), (1, TL - 1 - s_)]
        LAT0 = 4
        UPDATES = [n for n in range(len(STEPS)) if n < len(STEPS) - 2]

        def chunk_of(n):
            return n // 2

        def state_before(n):
            return max(i for i in range(n) if STEPS[i][0] == STEPS[n][0]) + 1

        kt_turned = sem("kt_turned")
        kt_kept = sem("kt_kept")
        masks_set = sem("masks_set")
        d_ready = sem("d_ready")
        d_done = sem("d_done")
        p_done = sem("p_done")
        inter_ready = sem("inter_ready")
        inter_read = sem("inter_read")
        intra_ready = sem("intra_ready")
        intra_read = sem("intra_read")
        update_ready = sem("update_ready")
        state_done = sem("state_done")
        wv_done = sem("wv_done")
        h_done = sem("h_done")
        read_measured = sem("read_measured")
        read_inverted = sem("read_inverted")
        read_normed = sem("read_normed")
        read_done = sem("read_done")
        o_loaded = [sem(f"o_loaded{i}") for i in range(2)]
        rows_loaded = sem("rows_loaded")
        cores_step = sem("cores_step")

        flat = psum[:].rearrange("p b c -> p (b c)")
        HEAD_COLS = M_DH + 1
        SCORE_AT = (0, 2 * BANK - P)
        PT_AT = 3 * BANK
        VALUE_AT = 5 * BANK
        DECAY_BANK = 6
        OUT_AT = 7 * BANK - 3 * HEAD_COLS

        TILES_DONE = []
        for n, (d_, t_) in enumerate(STEPS):
            if n >= LAT0 and any(STEPS[i][1] == t_ for i in range(LAT0, n)):
                TILES_DONE.append((n, t_))

        def masks_pool(pool):
            pool.wait_ge(p_ready, len(OUTPUTS))
            for i in range(2):
                pool.wait_ge(o_stored[i], 16 * TL)
            n = [0]

            def mstep(i):
                n[0] += 1
                i.then_inc(masks_set, 1)
                pool.wait_ge(masks_set, n[0])
            mstep(nc.gpsimd.tensor_copy(ident_b[:], ident[:]))
            mstep(nc.gpsimd.memset(scan_mask[:], 0.0))
            mstep(nc.gpsimd.memset(band_mask[:], 0.0))
            mstep(nc.gpsimd.affine_select(out=scan_mask[:, 0], in_=scan_mask[:, 0], compare_op=ALU.is_ge, fill=-1e30,
                                          base=0, pattern=[[0, M_HEADS], [1, P]], channel_multiplier=-1))
            mstep(nc.gpsimd.affine_select(out=scan_mask[:, 1], in_=scan_mask[:, 1], compare_op=ALU.is_ge, fill=-1e30,
                                          base=0, pattern=[[0, M_HEADS], [-1, P]], channel_multiplier=1))
            mstep(nc.gpsimd.affine_select(out=band_mask[:, 0], in_=band_mask[:, 0], compare_op=ALU.is_ge, fill=-1e30,
                                          base=0, pattern=[[1, P]], channel_multiplier=-1))
            mstep(nc.gpsimd.affine_select(out=band_mask[:, 1], in_=band_mask[:, 1], compare_op=ALU.is_ge, fill=-1e30,
                                          base=0, pattern=[[-1, P]], channel_multiplier=1))

        MASKS = 7

        def mlstm_sp(sp):
            sp.wait_ge(p_ready, len(OUTPUTS))
            sp.dma_start(norm_gain[:], mh_norm_g[0:1, :].to_broadcast([P, M_WIDTH])).then_inc(rows_loaded, 16)
            sp.dma_start(sink[:], attn_sink[0:1, :].to_broadcast([P, A_HEADS])).then_inc(rows_loaded, 16)
            for i in range(2):
                sp.wait_ge(o_stored[i], 16 * TL)
            for i, (n, t) in enumerate(TILES_DONE):
                if i >= 2:
                    sp.wait_ge(read_done, 2 * (i - 1))
                sp.dma_start(o_in[:, i % 2], o_dram[t]).then_inc(o_loaded[i % 2], 16)

        def mlstm_pool(pool):
            for n in UPDATES:
                d, t = STEPS[n]
                if n >= 2:
                    pool.wait_ge(update_ready, n - 1)
                w = tok_gate[:, 1, t, 4 * d:4 * d + 4].unsqueeze(2).to_broadcast([P, M_HEADS, M_DH + 1])
                nc.gpsimd.tensor_tensor(w_v[:, d], vext[:, t], w, ALU.mult).then_inc(wv_done, 1)
                readout_pool(pool, n)
            for n in range(len(UPDATES), len(STEPS)):
                readout_pool(pool, n)

        def readout_pool(pool, n):
            for i, (m, t) in enumerate(TILES_DONE):
                if m != n:
                    continue
                pool.wait_ge(read_measured, i + 1)
                s = small[:, 32 + 8 * (i % 2):36 + 8 * (i % 2)]
                nc.gpsimd.tensor_tensor(s, s, minus_half[:, 0:1].to_broadcast([P, M_HEADS]), ALU.pow)\
                    .then_inc(read_inverted, 1)
                if i == 0:
                    pool.wait_ge(rows_loaded, 32)
                pool.wait_ge(read_normed, i + 1)
                rows = y_in[:, t, 0:M_WIDTH]
                nc.gpsimd.tensor_tensor(rows, rows, norm_gain[:], ALU.mult).then_inc(read_done, 1)
                pool.wait_ge(read_done, 2 * i + 1)
                pool.wait_ge(o_loaded[i % 2], 16 * (i // 2 + 1))
                nc.gpsimd.tensor_tensor(rows, rows, o_in[:, i % 2], ALU.mult).then_inc(read_done, 1)

        def mlstm_act(act):
            for n in range(TA + TL):
                act.wait_ge(kt_turned, n + 1)
                to = k_tok[:, n] if n < TA else scores[:, n - TA].rearrange("p h t -> p (h t)")
                nc.scalar.activation(to, psum[:, n % 4, :], ACT.Copy).then_inc(kt_kept, 1)

        def decays_act(act, n):
            d, t = STEPS[n]
            i = n - LAT0
            act.wait_ge(d_ready, i + 1)
            if i >= 2:
                act.wait_ge(p_done, i - 1)
            for h in range(M_HEADS):
                last = nc.scalar.activation(d_exp[:, d, h], psum[:, DECAY_BANK, h * P:(h + 1) * P], ACT.Exp,
                                            bias=tok_gate[:, 0, t, 4 * d + h:4 * d + h + 1])
            last.then_inc(d_done, 1)

        cstep = [0]

        def core_step(dve, instruction):
            cstep[0] += 1
            instruction.then_inc(cores_step, 1)
            dve.wait_ge(cores_step, cstep[0])

        def cores_dve(dve):
            def probabilities(n):
                d, t = STEPS[n]
                i = n - LAT0
                dve.wait_ge(d_done, i + 1)
                if i == 0:
                    dve.wait_ge(kt_kept, TA + TL)
                if i >= 2:
                    dve.wait_ge(intra_ready, i - 1)
                nc.vector.tensor_tensor(p_tok[:, d], scores[:, t], d_exp[:, d], ALU.mult).then_inc(p_done, 1)

            def carry(n):
                d, t = STEPS[n]
                dve.wait_ge(update_ready, n + 1)
                if n >= 2:
                    dve.wait_ge(state_done, n - 1)
                for h in range(M_HEADS):
                    bank = flat[:, OUT_AT + h * HEAD_COLS:OUT_AT + (h + 1) * HEAD_COLS]
                    if n < 2:
                        last = nc.vector.tensor_copy(state[:, d, h], bank)
                    else:
                        c = chunk_of(n)
                        last = nc.vector.scalar_tensor_tensor(state[:, d, h], state[:, d, h],
                                                              decay_all[:, 4 * d + h, c:c + 1], bank,
                                                              op0=ALU.mult, op1=ALU.add)
                last.then_inc(state_done, 1)

            outputs_now = flat[:, OUT_AT:OUT_AT + M_HEADS * HEAD_COLS].rearrange("p (h v) -> p h v", h=M_HEADS)

            def inter_part(n):
                d, t = STEPS[n]
                i = n - LAT0
                inter = tok_gate[:, 2, t, 4 * d:4 * d + 4].unsqueeze(2).to_broadcast([P, M_HEADS, HEAD_COLS])
                dve.wait_ge(inter_ready, i + 1)
                nc.vector.tensor_tensor(num[:, d], outputs_now, inter, ALU.mult).then_inc(inter_read, 1)

            def intra_part(n):
                d, t = STEPS[n]
                i = n - LAT0
                dve.wait_ge(inter_read, i + 1)
                dve.wait_ge(intra_ready, i + 1)
                nc.vector.tensor_tensor(num[:, d], outputs_now, num[:, d], ALU.add).then_inc(intra_read, 1)
                dve.wait_ge(intra_read, i + 1)
                den, low = num[:, d, :, M_DH], small[:, 4 * d:4 * d + 4]
                core_step(dve, nc.vector.scalar_tensor_tensor(low, den, -1.0, den, op0=ALU.mult, op1=ALU.max))
                core_step(dve, nc.vector.tensor_tensor(low, low, tok_gate[:, 3, t, 4 * d:4 * d + 4], ALU.max))
                core_step(dve, nc.vector.reciprocal(low, low))
                wide = low.unsqueeze(2).to_broadcast([P, M_HEADS, M_DH])
                rows = y_in[:, t, 0:M_WIDTH].rearrange("p (h v) -> p h v", h=M_HEADS)
                first = all(STEPS[m][1] != t for m in range(LAT0, n))
                core_step(dve, nc.vector.tensor_tensor(rows if first else h_new[:], num[:, d, :, 0:M_DH], wide, ALU.mult))
                if not first:
                    core_step(dve, nc.vector.tensor_tensor(rows, rows, h_new[:], ALU.add))

            def readout(i):
                t = TILES_DONE[i][1]
                st = small[:, 8:32]
                mv = small[:, 48:56]
                var = small[:, 32 + 8 * (i % 2):36 + 8 * (i % 2)]
                for h in range(M_HEADS):
                    nc.vector.bn_stats(st[:, 6 * h:6 * h + 6], y_in[:, t, h * M_DH:(h + 1) * M_DH])\
                        .then_inc(cores_step, 1)
                    cstep[0] += 1
                dve.wait_ge(cores_step, cstep[0])
                for h in range(M_HEADS):
                    last = nc.vector.bn_aggr(mv[:, 2 * h:2 * h + 2], st[:, 6 * h:6 * h + 6])
                core_step(dve, last)
                nc.vector.tensor_scalar_add(var, mv.rearrange("p (h c) -> p h c", c=2)[:, :, 1], LN_EPS)\
                    .then_inc(read_measured, 1)
                dve.wait_ge(read_inverted, i + 1)
                for h in range(M_HEADS):
                    rows = y_in[:, t, h * M_DH:(h + 1) * M_DH]
                    last = nc.vector.tensor_scalar(rows, rows, mv[:, 2 * h:2 * h + 1], var[:, h:h + 1],
                                                   ALU.subtract, ALU.mult)
                last.then_inc(read_normed, 1)

            for n in range(LAT0):
                carry(n)
            probabilities(LAT0)
            dve.wait_ge(rows_loaded, 32)
            maxima(dve, 0)
            done = 0
            for n in range(LAT0, len(STEPS)):
                pair = 2 * (n - LAT0)
                maxima(dve, pair + 1)
                value_dve(dve, 2 * pair)
                inter_part(n)
                value_dve(dve, 2 * pair + 1)
                if n in UPDATES:
                    carry(n)
                maxima(dve, pair + 2)
                value_dve(dve, 2 * pair + 2)
                intra_part(n)
                value_dve(dve, 2 * pair + 3)
                if done < len(TILES_DONE) and TILES_DONE[done][0] <= n:
                    readout(done)
                    done += 1
                if n + 1 < len(STEPS):
                    probabilities(n + 1)
            nc.vector.memset(small[:, 60:61], 0.0).then_inc(h_done, 1)

        def cores_pe(pe):
            for n in range(TA + TL):
                if n < 4:
                    if n == 0:
                        pe.wait_ge(p_read_act, read_before(len(OUTPUTS) - 1, False))
                        pe.wait_ge(p_read_dve, read_before(len(OUTPUTS) - 1, True))
                        pe.wait_ge(conv_kept, 8)
                        pe.wait_ge(q_scaled, 4)
                else:
                    pe.wait_ge(kt_kept, n - 3)
                for h in range(M_HEADS):
                    o = psum[:, n % 4, h * P:(h + 1) * P]
                    if n < TA:
                        last = nc.tensor.transpose(o, kT[:, h, n * P:(n + 1) * P], ident[:])
                    else:
                        cols = slice((n - TA) * P, (n - TA + 1) * P)
                        last = nc.tensor.matmul(o, kT[:, h, cols], qT[:, h, cols], start=True, stop=True)
                last.then_inc(kt_turned, 1)

            def decays(n):
                d, t = STEPS[n]
                i = n - LAT0
                if i:
                    pe.wait_ge(intra_read, i)
                nc.tensor.matmul(psum[:, DECAY_BANK, :], ident_b[:], scan_mask[:, d].rearrange("p h t -> p (h t)"),
                                 start=True, stop=False)
                for h in range(M_HEADS):
                    last = nc.tensor.matmul(psum[:, DECAY_BANK, h * P:(h + 1) * P],
                                            ident[0:64, 32 * d + h:32 * d + h + 1].to_broadcast([64, P]),
                                            u_row[0:64, t * P:(t + 1) * P], start=False, stop=h == M_HEADS - 1)
                last.then_inc(d_ready, 1)

            def four(first, lhs, rhs):
                for h in range(M_HEADS):
                    o = flat[:, first + h * HEAD_COLS:first + (h + 1) * HEAD_COLS]
                    last = nc.tensor.matmul(o, lhs(h), rhs(h), start=True, stop=True)
                return last

            def update(n):
                d, t = STEPS[n]
                pe.wait_ge(wv_done, n + 1)
                if n == 0:
                    pe.wait_ge(kt_kept, TA)
                else:
                    pe.wait_ge(state_done, n)
                four(OUT_AT, lambda h: k_tok[:, t, h * M_DH:(h + 1) * M_DH], lambda h: w_v[:, d, h])\
                    .then_inc(update_ready, 1)

            pe.wait_ge(kt_kept, TA + TL)
            pe.wait_ge(masks_set, MASKS)
            for n in range(LAT0):
                update(n)
            pe.wait_ge(state_done, LAT0)
            decays(LAT0)
            pe.wait_ge(rope_kept, len(ROPED))
            scores_pe(pe, 0)
            for n in range(LAT0, len(STEPS)):
                d, t = STEPS[n]
                i = n - LAT0

                def inter():
                    pe.wait_ge(state_done, state_before(n))
                    pe.wait_ge(d_done, i + 1)
                    four(OUT_AT, lambda h: qT[:, h, t * P:(t + 1) * P], lambda h: state[:, d, h])\
                        .then_inc(inter_ready, 1)

                def state_update():
                    pe.wait_ge(inter_read, i + 1)
                    if n in UPDATES:
                        update(n)

                def intra():
                    pe.wait_ge(p_done, i + 1)
                    if n in UPDATES:
                        pe.wait_ge(state_done, n + 1)
                    four(OUT_AT, lambda h: p_tok[:, d, h], lambda h: vext[:, t, h]).then_inc(intra_ready, 1)

                def next_decays():
                    if n + 1 < len(STEPS):
                        decays(n + 1)

                attention_pe(pe, 2 * i, inter)
                state_update()
                attention_pe(pe, 2 * i + 1, intra)
                next_decays()

        ATT = [(j, i, g) for j in range(TL) for g in range(A_KV) for i in range(A_HEADS // 2)]

        def key_tiles(j):
            return [TL, TL + 1] + [t for t in (j - 1, j, j + 1) if 0 <= t < TL]

        s_ready = sem("s_ready")
        s_max = sem("s_max")
        s_exp = sem("s_exp")
        pt_turned = sem("pt_turned")
        pt_kept = sem("pt_kept")
        att_ready = sem("att_ready")
        att_read = sem("att_read")

        A_PAIRS = len(ATT) // 2

        def score(pe, n):
            j, i, g = ATT[n]
            tiles = key_tiles(j)
            rows = slice(64 * g, 64 * g + 64)
            at = SCORE_AT[n % 2]
            q = qaT[rows, i, j * P:(j + 1) * P]
            runs = []
            for m, t in enumerate(tiles):
                if runs and t == tiles[m - 1] + 1 and (at + m * P) % BANK and len(runs[-1]) * P < 2 * P:
                    runs[-1].append((m, t))
                else:
                    runs.append([(m, t)])
            for run in runs:
                (m0, t0), w = run[0], P * len(run)
                edges = [(m, t) for m, t in run if m >= 2 and t != j]
                last = nc.tensor.matmul(flat[:, at + m0 * P:at + m0 * P + w], q, kaT[rows, t0 * P:t0 * P + w],
                                        start=True, stop=not edges)
                for m, t in edges:
                    last = nc.tensor.matmul(flat[:, at + m * P:at + (m + 1) * P], ident_b[:], band_mask[:, int(t > j)],
                                            start=False, stop=(m, t) == edges[-1])
            last.then_inc(s_ready, 1)

        def scores_pe(pe, pair):
            if pair == A_PAIRS:
                return
            if pair:
                pe.wait_ge(s_exp, 2 * pair)
            score(pe, 2 * pair)
            score(pe, 2 * pair + 1)

        def turn_probabilities(pe, n):
            pe.wait_ge(s_exp, n + 1)
            if n:
                pe.wait_ge(pt_kept, n)
            for m in range(len(key_tiles(ATT[n][0]))):
                last = nc.tensor.transpose(flat[:, PT_AT + m * P:PT_AT + (m + 1) * P],
                                           att_p[:, n % 2, m * P:(m + 1) * P], ident[:])
            last.then_inc(pt_turned, 1)

        def value_pe(pe, n):
            j, i, g = ATT[n]
            tiles = key_tiles(j)
            pe.wait_ge(pt_kept, n + 1)
            if n:
                pe.wait_ge(att_read, n)
            for m, t in enumerate(tiles):
                last = nc.tensor.matmul(flat[:, VALUE_AT:VALUE_AT + A_DH], att_pT[:, n % 2, m * P:(m + 1) * P],
                                        va[:, t, g * A_DH:(g + 1) * A_DH], start=m == 0, stop=m == len(tiles) - 1)
            last.then_inc(att_ready, 1)

        def attention_pe(pe, pair, between):
            a, b = 2 * pair, 2 * pair + 1
            turn_probabilities(pe, a)
            scores_pe(pe, pair + 1)
            value_pe(pe, a)
            turn_probabilities(pe, b)
            between()
            value_pe(pe, b)

        def s_view(n):
            return flat[:, SCORE_AT[n % 2]:SCORE_AT[n % 2] + P * len(key_tiles(ATT[n][0]))]

        def exps_act(act, pair):
            if pair == A_PAIRS:
                return
            act.wait_ge(s_max, 2 * pair + 2)
            for n in (2 * pair, 2 * pair + 1):
                j, i, g = ATT[n]
                head = i + 4 * g
                s = att_small[:, n % 4]
                if n >= 2:
                    act.wait_ge(pt_turned, n - 1)
                if n >= 4:
                    act.wait_ge(att_read, n - 3)
                nc.scalar.activation(s[:, 1:2], sink[:, head:head + 1], ACT.Exp, bias=s[:, 0:1])
                nc.scalar.activation(att_p[:, n % 2, 0:P * len(key_tiles(j))], s_view(n), ACT.Exp, bias=s[:, 0:1],
                                     accum_out=s[:, 2:3]).then_inc(s_exp, 1)

        def keep_act(act, n):
            w = P * len(key_tiles(ATT[n][0]))
            act.wait_ge(pt_turned, n + 1)
            if n >= 2:
                act.wait_ge(att_ready, n - 1)
            nc.scalar.activation(att_pT[:, n % 2, 0:w], flat[:, PT_AT:PT_AT + w], ACT.Copy).then_inc(pt_kept, 1)

        def cores_act(act):
            mlstm_act(act)
            decays_act(act, LAT0)
            act.wait_ge(rows_loaded, 32)
            exps_act(act, 0)
            for pair in range(A_PAIRS):
                keep_act(act, 2 * pair)
                keep_act(act, 2 * pair + 1)
                exps_act(act, pair + 1)
                if pair % 2 and pair + 1 < A_PAIRS:
                    decays_act(act, LAT0 + (pair + 1) // 2)

        def maxima(dve, pair):
            if pair == A_PAIRS:
                return
            dve.wait_ge(s_ready, 2 * pair + 2)
            for n in (2 * pair, 2 * pair + 1):
                head = ATT[n][1] + 4 * ATT[n][2]
                s = att_small[:, n % 4]
                core_step(dve, nc.vector.reduce_max(s[:, 3:4], s_view(n), AX_X))
                nc.vector.tensor_scalar(s[:, 0:1], s[:, 3:4], sink[:, head:head + 1], -1.0, ALU.max, ALU.mult)\
                    .then_inc(s_max, 1)

        def value_dve(dve, n):
            j, i, g = ATT[n]
            s = att_small[:, n % 4]
            dve.wait_ge(s_exp, n + 1)
            core_step(dve, nc.vector.tensor_tensor(s[:, 3:4], s[:, 1:2], s[:, 2:3], ALU.add))
            core_step(dve, nc.vector.reciprocal(s[:, 3:4], s[:, 3:4]))
            dve.wait_ge(att_ready, n + 1)
            at = M_WIDTH + (i + 4 * g) * A_DH
            nc.vector.tensor_scalar_mul(y_in[:, j, at:at + A_DH], flat[:, VALUE_AT:VALUE_AT + A_DH],
                                        s[:, 3:4]).then_inc(att_read, 1)

        yt_turned = sem("yt_turned")
        yt_high = sem("yt_high")
        yt_low = sem("yt_low")
        wo_in = [sem(f"wo_in{i}") for i in range(2)]
        wo_hi = sem("wo_hi")
        wo_lo = sem("wo_lo")
        mix_ready = sem("mix_ready")
        mix_read = sem("mix_read")
        ln_in = sem("ln_in")
        x2_stored = sem("x2_stored")
        WO_UNITS = D // 256

        def output_sp(sp):
            sp.wait_ge(intra_ready, len(STEPS) - LAT0)
            sp.wait_ge(h_done, 1)
            for q in range(2 * WO_UNITS):
                if q >= 2:
                    sp.wait_ge(wo_lo, q - 1)
                sp.dma_start(wo_raw[:, q % 2], w_out_view[:, :, q * P:(q + 1) * P]).then_inc(wo_in[q % 2], 16)
                if q == 3:
                    sp.wait_ge(yt_turned, 2 * KD)
                    for i, src in enumerate((ln_g, ln_b)):
                        sp.dma_start(ln_rows2[:, i], src[0, 0:1, :].to_broadcast([P, D])).then_inc(ln_in, 16)
                    for t in range(3):
                        sp.dma_start(res_row2[:, t], x1_dram[t]).then_inc(N2.rows_in[t], 16)
            for t in range(3, TL):
                sp.wait_ge(N2.added, t - 2)
                sp.dma_start(res_row2[:, t % 3], x1_dram[t]).then_inc(N2.rows_in[t % 3], 16)
            for t in range(TL):
                sp.wait_ge(N2.done, t + 1)
                sp.dma_start(x2_dram[t], y[:, t, :]).then_inc(x2_stored, 16)

        def residual_pool(pool, N, rows, gain_bias):
            for t in range(TL):
                pool.wait_ge(N.rows_in[t % 3], 16 * (t // 3 + 1))
                nc.gpsimd.tensor_tensor(rows[:, t % 3], rows[:, t % 3], gain_bias[:, 0], ALU.mult).then_inc(N.affined, 1)
                pool.wait_ge(N.affined, 2 * t + 1)
                nc.gpsimd.tensor_tensor(rows[:, t % 3], rows[:, t % 3], gain_bias[:, 1], ALU.add).then_inc(N.affined, 1)
                if t:
                    norm_pool(pool, N, t - 1)
            norm_pool(pool, N, TL - 1)

        def output_pool(pool):
            pool.wait_ge(ln_in, 32)
            residual_pool(pool, N2, res_row2, ln_rows2)

        def output_act(act):
            for u in range(2 * KD):
                act.wait_ge(yt_turned, u + 1)
                n, k = u // KD, u % KD
                nc.scalar.activation(xh_lat[:, k, n * BANK:(n + 1) * BANK], psum[:, u % 4, :], ACT.Copy).then_inc(yt_high, 1)
                if u == 3:
                    wo_high(act, 0)
                    wo_high(act, 1)
            act.wait_ge(N2.gates_summed, 1)
            for half in range(2):
                nc.scalar.activation(gate_row2[:, 0, half * BANK:(half + 1) * BANK], psum[:, half, :], ACT.Copy)\
                    .then_inc(N2.gates_kept, 1)
            for q in range(2, 2 * WO_UNITS):
                wo_high(act, q)
            for t in range(TL):
                norm_act(act, N2, t)
            turn_act(act, T3, (0, 1, 2, 3), turn_buf3, lambda a: None)

        def wo_high(act, q):
            u = q // 2
            act.wait_ge(wo_in[q % 2], 16 * (q // 2 + 1))
            if u >= 2:
                act.wait_ge(mix_ready, TL * (u - 1))
            nc.scalar.activation(wo_h[:, u % 2, :, (q % 2) * P:(q % 2 + 1) * P], wo_raw[:, q % 2], ACT.Copy)\
                .then_inc(wo_hi, 1)

        def output_dve(dve):
            def low(q):
                u = q // 2
                dve.wait_ge(wo_hi, q + 1)
                cols = slice((q % 2) * P, (q % 2 + 1) * P)
                nc.vector.tensor_tensor(wo_l[:, u % 2, :, cols], wo_raw[:, q % 2], wo_h[:, u % 2, :, cols].bitcast(F32),
                                        ALU.subtract).then_inc(wo_lo, 1)
            for u in range(2 * KD):
                n, k = u // KD, u % KD
                dve.wait_ge(yt_high, u + 1)
                nc.vector.tensor_tensor(xl_lat[:, k, n * BANK:(n + 1) * BANK], psum[:, u % 4, :],
                                        xh_lat[:, k, n * BANK:(n + 1) * BANK].bitcast(F32), ALU.subtract)\
                    .then_inc(yt_low, 1)
                if u == 3:
                    low(0)
                    low(1)
            affine_of(dve, 1, 7, 6)
            low(2)
            low(3)
            dve.wait_ge(N2.gates_kept, 2)
            for j in range(TL * WO_UNITS):
                u, t = j // TL, j % TL
                if t == 0 and 2 <= u + 1 < WO_UNITS:
                    low(2 * u + 2)
                    low(2 * u + 3)
                dve.wait_ge(mix_ready, j + 1)
                cols = slice(u * 256, (u + 1) * 256)
                nc.vector.tensor_tensor(y[:, t, cols], psum[:, 4 + j % 4, 0:256], gate_row2[:, 0, cols], ALU.mult)\
                    .then_inc(mix_read, 1)
                if u == WO_UNITS - 1:
                    dve.wait_ge(mix_read, j + 1)
                    dve.wait_ge(N2.affined, 2 * t + 2)
                    nc.vector.scalar_tensor_tensor(y[:, t, :], res_row2[:, t % 3, :], ALPHA, y[:, t, :],
                                                   op0=ALU.mult, op1=ALU.add).then_inc(N2.added, 1)
                    dve.wait_ge(N2.added, t + 1)
                    norm_sums_dve(dve, N2, t, None)
            turn_dve(dve, T3, turn_buf3)
            dve.wait_ge(x2_stored, 16 * TL)

        def output_pe(pe):
            pe.wait_ge(read_done, 2 * TL)
            pe.wait_ge(att_read, len(ATT))
            for u in range(2 * KD):
                n, k = u // KD, u % KD
                if u >= 4:
                    pe.wait_ge(yt_low, u - 3)
                for i in range(4):
                    last = nc.tensor.transpose(psum[:, u % 4, i * P:(i + 1) * P], y_in[:, 4 * n + i, k * P:(k + 1) * P],
                                               ident[:])
                last.then_inc(yt_turned, 1)
            pe.wait_ge(yt_low, 2 * KD)
            gate_rows_pe(pe, N2, 5, 1)
            for j in range(TL * WO_UNITS):
                u, t = j // TL, j % TL
                if t == 0:
                    pe.wait_ge(wo_lo, 2 * u + 2)
                if j >= 4:
                    pe.wait_ge(mix_read, j - 3)
                o = psum[:, 4 + j % 4, 0:256]
                for k in range(KD):
                    high, low = xpart(0, k, t * P, P), xpart(1, k, t * P, P)
                    wh, wl = wo_h[:, u % 2, k, :], wo_l[:, u % 2, k, :]
                    nc.tensor.matmul(o, high, wh, start=k == 0, stop=False)
                    nc.tensor.matmul(o, high, wl, start=False, stop=False)
                    last = nc.tensor.matmul(o, low, wh, start=False, stop=k == KD - 1)
                last.then_inc(mix_ready, 1)

            def normed(pe, n):
                if n == 0:
                    pe.wait_ge(N2.gates_kept, 2)
                pe.wait_ge(N2.done, (4, 8)[n])
            turn_pe(pe, T3, (0, 1, 2, 3), normed)

        out_affined = sem("out_affined")
        ln_in3 = sem("ln_in3")

        def last_sp(sp):
            sp.wait_ge(F2.ab_ready, 2 * F2.n * PAIRS)
            sp.wait_ge(F2.lo, 6 * PAIRS)
            for t in range(TL):
                if t >= 3:
                    sp.wait_ge(N3.added, t - 2)
                sp.dma_start(res_row[:, t % 3], x2_dram[t]).then_inc(N3.rows_in[t % 3], 16)
                if t == 0:
                    for i, src in enumerate((ln_g[0, 1:2, :], ln_b[0, 1:2, :], ln_g[0, 2:3, :], ln_b[0, 2:3, :])):
                        sp.dma_start(ln_rows3[:, i], src.to_broadcast([P, D])).then_inc(ln_in3, 16)
            for t in range(TL):
                sp.wait_ge(out_affined, 2 * t + 2)
                sp.dma_start(out_rows[t], y[:, t, :]).then_inc(out_done, 16)
            sp.wait_ge(out_done, 16 * TL)

        def last_pool(pool):
            pool.wait_ge(ln_in3, 64)
            residual_pool(pool, N3, res_row, ln_rows3)

        def last_act(act):
            act.wait_ge(F2.lo, 6 * PAIRS)
            gate_rows_act(act, N3, 1, HALF)
            for t in range(TL):
                norm_act(act, N3, t)

        def affine_out(dve, t):
            dve.wait_ge(N3.done, t + 1)
            nc.vector.tensor_tensor(y[:, t, :], y[:, t, :], ln_rows3[:, 2], ALU.mult).then_inc(out_affined, 1)
            dve.wait_ge(out_affined, 2 * t + 1)
            nc.vector.tensor_tensor(y[:, t, :], y[:, t, :], ln_rows3[:, 3], ALU.add).then_inc(out_affined, 1)

        def last_tiles_dve(dve, t):
            if t == 0:
                dve.wait_ge(N3.gates_kept, 2)
                dve.wait_ge(ln_in3, 64)
            step(dve, nc.vector.tensor_tensor(y[:, t, :], y[:, t, :], gate_row[:, 0, :], ALU.mult))
            dve.wait_ge(N3.affined, 2 * t + 2)
            nc.vector.scalar_tensor_tensor(y[:, t, :], res_row[:, t % 3, :], ALPHA, y[:, t, :],
                                           op0=ALU.mult, op1=ALU.add).then_inc(N3.added, 1)
            dve.wait_ge(N3.added, t + 1)
            norm_sums_dve(dve, N3, t, None)
            if t:
                affine_out(dve, t - 1)
            if t == TL - 1:
                affine_out(dve, t)

        more_c = more[:, 0:16].rearrange("p (v k) -> p k v", v=2)

        T1 = Turn("t1", CHUNKS_ALL)
        F1 = Ffn("f1", 0, CHUNKS_ALL, True)
        N1 = Norm("n1")
        T2 = Turn("t2", CHUNKS_ALL)
        N2 = Norm("n2")
        T3 = Turn("t3", CHUNKS_LAT)
        F2 = Ffn("f2", 1, CHUNKS_LAT, False)
        N3 = Norm("n3")

        block = keep.enter_context(nc.Block())

        @block.sync
        def _(sp):
            sp.dma_start(rows_a[0:72, :], b_ada.rearrange("l (r p) -> (l r) p", p=P)).then_inc(rows_in, 16)
            sp.dma_start(rows_a[72:96, :], ln_g.rearrange("l s (r p) -> (l s r) p", p=P)).then_inc(rows_in, 16)
            sp.dma_start(rows_a[96:120, :], ln_b.rearrange("l s (r p) -> (l s r) p", p=P)).then_inc(rows_in, 16)
            sp.dma_start(rows_b[0:8, :], c.rearrange("l (r p) -> (l r) p", p=P)).then_inc(rows_in, 16)
            sp.dma_start(rows_b[8:16, :], c_ctx.rearrange("(r p) -> r p", p=P)).then_inc(rows_in, 16)
            sp.dma_start(rows_b[16:56, :], conv_w.rearrange("l j (r p) -> (l j r) p", p=P)).then_inc(rows_in, 16)
            sp.dma_start(rows_b[56:64, :], conv_b.rearrange("l (r p) -> (l r) p", p=P)).then_inc(rows_in, 16)
            for n in range(ADA_EARLY):
                if n >= EARLY:
                    sp.wait_ge(early_used, n - EARLY + 1)
                sp.dma_start(ada_early[:, n % EARLY], ada_view[:, :, n * P:(n + 1) * P]).then_inc(early_in[n % EARLY], 16)
            for t in range(TA):
                sp.dma_start(y[:, t, :], token_rows(t)).then_inc(x_in[t // 4], 16)
            ffn_sp(sp, F1)
            sp.wait_ge(ada_used, PAIRS * ADA_PER_PAIR + 1)
            sp.wait_ge(F1.ab_ready, 2 * F1.n * PAIRS)
            for t in range(TA):
                if t >= 3:
                    sp.wait_ge(N1.added, t - 2)
                sp.dma_start(res_row[:, t % 3, :], token_rows(t)).then_inc(N1.rows_in[t % 3], 16)
            proj_sp(sp)
            mlstm_sp(sp)
            output_sp(sp)
            sp.wait_ge(mix_ready, TL * WO_UNITS)
            sp.wait_ge(T3.low, 1)
            sp.wait_ge(T3.scaled, 2 * KD)
            sp.wait_ge(N2.added, TL)
            ffn_sp(sp, F2)
            last_sp(sp)

        @block.gpsimd
        def _(pool):
            nc.gpsimd.memset(ident[:], 0.0).then_inc(ident_set, 1)
            nc.gpsimd.memset(minus_half[:], -0.5).then_inc(const_set, 1)
            pool.wait_ge(ident_set, 1)
            nc.gpsimd.affine_select(out=ident[:], in_=ident[:], compare_op=ALU.not_equal, fill=1.0, base=0,
                                    pattern=[[-1, P]], channel_multiplier=1).then_inc(ident_set, 1)
            for t in range(TA):
                norm_pool(pool, N1, t)
            masks_pool(pool)
            mlstm_pool(pool)
            output_pool(pool)
            last_pool(pool)

        @block.scalar
        def _(act):
            act.wait_ge(rows_in, 7 * 16)
            nc.scalar.activation(rows_b[0:16, :], rows_b[0:16, :], ACT.Silu).then_inc(c_silu, 1)

            def scale_known(act):
                act.wait_ge(dve_step, 3)
            turn_act(act, T1, (0, 1, 2, 3, 4, 5, 6), turn_buf1, scale_known)
            ffn_act(act, F1)
            act.wait_ge(F1.lo, 6 * PAIRS)
            gate_rows_act(act, N1, 2, HALF)
            T2_BANKS = (0, 1, 2, 3)
            for t in range(TA):
                norm_act(act, N1, t)
            turn_act(act, T2, T2_BANKS, turn_buf2, lambda a: None)
            proj_act(act)
            cores_act(act)
            output_act(act)
            ffn_act(act, F2)
            last_act(act)

        @block.vector
        def _(dve):
            dve.wait_ge(rows_turned, 2)
            nc.vector.tensor_copy(params[:], psum[:, 0, 0:120]).then_inc(rows_kept, 1)
            nc.vector.tensor_copy(more[:], psum[:, 1, 0:64]).then_inc(rows_kept, 1)
            dve.wait_ge(rows_kept, 2)
            dve.wait_ge(early_used, ADA_EARLY)
            nc.vector.tensor_tensor(mod[:, 0:ADA_EARLY, :],
                                    psum[:, 7, 0:2 * ADA_EARLY].rearrange("p (a b) -> p a b", b=2),
                                    params[:, 0:ADA_EARLY].unsqueeze(2).to_broadcast([P, ADA_EARLY, 2]),
                                    ALU.add).then_inc(mod_ready, 1)
            dve.wait_ge(mod_ready, 1)
            for v in range(2):
                step(dve, nc.vector.tensor_scalar_add(in_scale[:, v, :], mod[:, KD:2 * KD, v], 1.0))
            step(dve, nc.vector.tensor_copy(in_shift[:], mod[:, 0:KD, :].rearrange("p k v -> p v k")))
            turn_dve(dve, T1, turn_buf1)

            def before_last_y(dve):
                dve.wait_ge(ada_used, PAIRS * ADA_PER_PAIR + 1)
                nc.vector.tensor_tensor(mod[:, N_MOD * KD - 1, :], psum[:, 7, 10:12],
                                        params[:, N_MOD * KD - 1:N_MOD * KD].to_broadcast([P, 2]),
                                        ALU.add).then_inc(mod_ready, 1)
                dve.wait_ge(mod_ready, PAIRS + 2)
                affine_of(dve, 0, 4, 3)
            ffn_dve(dve, F1, before_last_y, ffn_residual_dve(dve, F1, N1, 2))
            turn_dve(dve, T2, turn_buf2)
            dve.wait_ge(F1.y_ready, 2 * TA * PAIRS)
            nc.vector.memset(gate_bias[:], 0.0).then_inc(gate_clear, 1)
            nc.vector.memset(gate_wh[:].bitcast(F32), 0.0)
            nc.vector.memset(gate_wl[:].bitcast(F32), 0.0).then_inc(gate_clear, 1)
            dve.wait_ge(x1_stored, 16 * TL)
            nc.vector.memset(conv_in[:], 0.0).then_inc(pads_set, 1)
            proj_dve(dve)
            cores_dve(dve)
            output_dve(dve)
            ffn_dve(dve, F2, lambda e: None, last_tiles_dve)

        @block.tensor
        def _(pe):
            pe.wait_ge(ident_set, 2)
            pe.wait_ge(rows_in, 7 * 16)
            nc.tensor.transpose(psum[:, 0, 0:120], rows_a[0:120, :], ident[0:120, 0:120]).then_inc(rows_turned, 1)
            pe.wait_ge(c_silu, 1)
            nc.tensor.transpose(psum[:, 1, 0:64], rows_b[0:64, :], ident[0:64, 0:64]).then_inc(rows_turned, 1)
            pe.wait_ge(rows_kept, 2)
            for n in range(ADA_EARLY):
                pe.wait_ge(early_in[n % EARLY], 16 * (n // EARLY + 1))
                for k in range(KD):
                    last = nc.tensor.matmul(psum[:, 7, 2 * n:2 * n + 2], ada_early[:, n % EARLY, k, :], more_c[:, k, :],
                                            start=k == 0, stop=k == KD - 1)
                last.then_inc(early_used, 1)
            turn_pe(pe, T1, (0, 1, 2, 3, 4, 5, 6),
                    lambda e, n: e.wait_ge(x_in[n], 16 * (4 if n < 2 else 2)))

            def before_last_y(pe):
                pe.wait_ge(mod_ready, PAIRS + 1)
                pe.wait_ge(ada_in, 16 * (PAIRS * ADA_PER_PAIR + 1))
                for k in range(KD):
                    last = nc.tensor.matmul(psum[:, 7, 10:12], ada_raw[:, k, :], more_c[:, k, :],
                                            start=k == 0, stop=k == KD - 1)
                last.then_inc(ada_used, 1)
                pe.wait_ge(F1.glu_ready, 2 * F1.n * PAIRS)
                gate_rows_pe(pe, N1, 2, 2)
            ffn_pe(pe, F1, T1, before_last_y)

            def normed(pe, n):
                if n == 0:
                    pe.wait_ge(N1.gates_kept, 4)
                pe.wait_ge(N1.done, (4, 8, 10)[n])
            turn_pe(pe, T2, (0, 1, 2, 3), normed)
            proj_pe(pe)
            cores_pe(pe)
            output_pe(pe)

            def before_last(pe):
                pe.wait_ge(F2.glu_ready, 2 * F2.n * PAIRS)
                gate_rows_pe(pe, N3, 8, 1)
            ffn_pe(pe, F2, T3, before_last)


_INS = ["x", "c", "ctx", "c_ctx", "w_ada", "b_ada", "ln_g", "ln_b", "ffn_w13", "ffn_w2", "w_in", "b_gates",
        "conv_w", "conv_b", "mh_norm_g", "attn_sink", "w_out"]
GRID_W = 64
ROPE_BASE = 10000.0


def rope_table():
    rows = N_LAT // GRID_W
    row = np.repeat(np.arange(rows, dtype=np.float32), GRID_W)
    col = np.tile(np.arange(GRID_W, dtype=np.float32), rows)
    n_freq = A_DH // 4
    inv = np.float32(ROPE_BASE) ** (-np.arange(n_freq, dtype=np.float32) / np.float32(n_freq))
    angle = np.concatenate([row[:, None] * inv, col[:, None] * inv], -1).astype(np.float32)
    return np.stack([np.cos(angle), np.sin(angle)]).astype(np.float32)


def kernel(**inputs):
    import concourse.bacc as _bacc
    from concourse.bass_utils import run_bass_kernel_spmd as _run

    nc = _bacc.Bacc("TRN2", target_bir_lowering=False, num_devices=1)
    arrays, args = {}, []
    for name in _INS:
        arrays[f"in_{name}"] = np.ascontiguousarray(inputs[name])
    arrays["rope"] = rope_table()
    for name, a in arrays.items():
        args.append(nc.dram_tensor(name, a.shape, mybir.dt.from_np(a.dtype), kind="ExternalInput").ap())
    out = nc.dram_tensor("out", (1, N_LAT, D), F32, kind="ExternalOutput").ap()
    hybrid_block(nc, *args, out)
    r = _run(nc, [arrays], core_ids=[0])
    return r.results[0]["out"]
```

```python
from contextlib import ExitStack

import numpy as np

import concourse.bass as bass
from concourse import mybir

P = 128
F32 = mybir.dt.float32
F32R = mybir.dt.float32r
BF16 = mybir.dt.bfloat16
ALU = mybir.AluOpType
ACT = mybir.ActivationFunctionType
AX_X = mybir.AxisListType.X

D = 1024
KD = D // P
N_LAT, N_CTX = 1024, 256
TL, TC = N_LAT // P, N_CTX // P
TA = TL + TC
N_ALL = N_LAT + N_CTX
D_FF = 2816
FB = D_FF // P
PAIRS = FB // 2
N_MOD = 9
LN_EPS = 1e-5
ALPHA = 2.0 ** 0.25
HALF = 0.5
BANK = 512

M_HEADS, M_DH, M_WIDTH = 4, 128, 512
A_HEADS, A_KV, A_DH = 8, 2, 64
OFF_Q, OFF_K, OFF_V, OFF_O, OFF_G = 0, 512, 1024, 1536, 2048
OFF_QA = OFF_G + 16
OFF_KA = OFF_QA + A_HEADS * A_DH
OFF_VA = OFF_KA + A_KV * A_DH
N_IN = OFF_VA + A_KV * A_DH
CONV_W = 5

ADA_PER_PAIR = 5
ADA_EARLY = N_MOD * KD - ADA_PER_PAIR * PAIRS

CHUNKS_ALL = [(0, 512), (512, 512), (1024, 256)]
CHUNKS_LAT = [(0, 512), (512, 512)]


def hybrid_block(nc, x, c, ctx, c_ctx, w_ada, b_ada, ln_g, ln_b, ffn_w13, ffn_w2, w_in, b_gates,
                 conv_w, conv_b, mh_norm_g, attn_sink, w_out, rope_cs, out):
    with ExitStack() as keep:
        def tensor(stack, name, shape, dt=F32):
            return stack.enter_context(nc.sbuf_tensor(name, shape, dt))

        def sem(name):
            return keep.enter_context(nc.semaphore(name))

        x_rows = x.rearrange("b (t p) d -> (b t) p d", p=P)
        ctx_rows = ctx.rearrange("b (t p) d -> (b t) p d", p=P)
        out_rows = out.rearrange("b (t p) d -> (b t) p d", p=P)
        ada_view = w_ada.rearrange("l (k p) n -> (l p) k n", p=P)
        w13_view = [ffn_w13[0, i].rearrange("(k p) n -> p k n", p=P) for i in range(2)]
        w2_view = [ffn_w2[0, i] for i in range(2)]
        w_in_view = w_in.rearrange("l (k p) n -> (l p) k n", p=P)
        w_out_view = w_out.rearrange("l (k p) n -> (l p) k n", p=P)

        def token_rows(t):
            return x_rows[t] if t < TL else ctx_rows[t - TL]

        psum = keep.enter_context(nc.psum_tensor("psum", [P, 8, BANK], F32))

        ident = tensor(keep, "ident", [P, P])
        params = tensor(keep, "params", [P, 120])
        more = tensor(keep, "more", [P, 64])
        mod = tensor(keep, "mod", [P, N_MOD * KD, 2])
        in_scale = tensor(keep, "in_scale", [P, 2, KD])
        in_shift = tensor(keep, "in_shift", [P, 2, KD])
        ln_stats = tensor(keep, "ln_stats", [P, 2, 24])
        ones = tensor(keep, "ones", [P, 1])
        minus_half = tensor(keep, "minus_half", [P, 8])
        tok_gate = tensor(keep, "tok_gate", [P, 4, TA, 2 * M_HEADS])
        ada_sum = tok_gate[:].rearrange("p a t r -> p (a t r)")[:, 0:2 * P].rearrange("p (v n) -> p v n", v=2)
        decay_all = tensor(keep, "decay_all", [P, 2 * M_HEADS, TA])
        decay = tensor(keep, "decay", [P, 32])

        arena_at = nc.sbuf_base

        def place(name, kib, shape, dt=F32):
            return nc.alloc_sbuf_tensor_at(name, shape, dt, offset=arena_at + int(kib * 1024))

        xh_lat = place("xh_lat", 0, [P, KD, N_LAT], F32R)
        xl_lat = place("xl_lat", 32, [P, KD, N_LAT], F32R)
        xh_ctx = place("xh_ctx", 64, [P, KD, N_CTX], F32R)
        xl_ctx = place("xl_ctx", 72, [P, KD, N_CTX], F32R)
        y = place("y", 80, [P, TA, D])
        raw = place("raw", 120, [P, 2, KD, P])
        ada_raw = place("ada_raw", 128, [P, KD, P])
        w13h = place("w13h", 132, [P, 2, 2, KD, P], F32R)
        w13l = place("w13l", 148, [P, 2, 2, KD, P], F32R)
        w2h = place("w2h", 164, [P, 2, D], F32R)
        w2l = place("w2l", 172, [P, 2, D], F32R)
        gh = place("gh", 180, [P, 2, N_ALL], F32R)
        gl = place("gl", 190, [P, 2, N_ALL], F32R)
        glu_sig = place("glu_sig", 200, [P, BANK])
        glu = place("glu", 202, [P, BANK])
        ada_early = place("ada_early", 0, [P, ADA_EARLY, KD, P])
        early_sum = place("early_sum", 166, [P, ADA_EARLY, 2, P])
        rows_a = place("rows_a", 188, [P, P])
        rows_b = place("rows_b", 188.5, [P, P])
        turn_buf1 = place("turn_buf1", 172, [P, 2, BANK])
        gate_row = place("gate_row", 120, [P, 2, D])
        res_row = place("res_row", 128, [P, 3, D])
        turn_buf2 = place("turn_buf2", 140, [P, 2, BANK])

        qT = place("qT", 80, [P, M_HEADS, N_LAT])
        kT = place("kT", 96, [P, M_HEADS, N_ALL])
        qaT = place("qaT", 64, [P, A_HEADS // 2, N_LAT])
        kaT = place("kaT", 116, [P, N_ALL])
        va = place("va", 121, [P, TA, P])
        vext = place("vext", 126, [P, TA, M_HEADS, M_DH + 1])
        u_row = place("u_row", 146.25, [P, N_ALL])
        conv_in = place("conv_in", 151.5, [P, 1288])
        conv_sum = place("conv_sum", 156.625, [P, 1284])
        p_raw = place("p_raw", 162, [P, 2, KD, P])
        p_wh = place("p_wh", 170, [P, 2, KD, 256], F32R)
        p_wl = place("p_wl", 186, [P, 2, KD, 256], F32R)
        gate_wh = place("gate_wh", 178, [P, KD, P], F32R)
        gate_wl = place("gate_wl", 194, [P, KD, P], F32R)
        gate_raw = place("gate_raw", 182, [P, KD, 16])
        gate_bias = place("gate_bias", 182.5, [P, 1])
        rope_ab = place("rope_ab", 202, [P, 2, 256])
        rope_tab = place("rope_tab", 152, [P, TL, 2, A_DH // 2])
        rope_out = place("rope_out", 154, [P, 2, 256])
        o_sig = place("o_sig", 156, [P, 2, 256])
        gate_all = place("gate_all", 116, [P, N_ALL])
        gate_abs = place("gate_abs", 121, [P, N_ALL])
        li_row = place("li_row", 126, [P, N_ALL])
        lf_row = place("lf_row", 131, [P, N_ALL])
        b_row = place("b_row", 136, [P, N_ALL])
        m_row = place("m_row", 141, [P, N_ALL])
        a_row = place("a_row", 80, [P, N_ALL])
        e_row = place("e_row", 85, [P, N_ALL])
        a_nat = place("a_nat", 90, [P, N_ALL])
        w_nat = place("w_nat", 116, [P, N_ALL])
        inter_nat = place("inter_nat", 121, [P, N_ALL])
        floor_nat = place("floor_nat", 126, [P, N_ALL])

        k_tok = place("k_tok", 0, [P, TA, M_WIDTH])
        scores = place("scores", 20, [P, TL, M_HEADS, P])
        att_p = place("att_p", 36, [P, 2, 640])
        att_pT = place("att_pT", 41, [P, 2, 640])
        norm_gain = place("norm_gain", 47, [P, M_WIDTH])
        o_in = place("o_in", 49, [P, 2, M_WIDTH])
        d_exp = place("d_exp", 54, [P, 2, M_HEADS, P])
        p_tok = place("p_tok", 58, [P, 2, M_HEADS, P])
        state = place("state", 151.5, [P, 2, M_HEADS, M_DH + 1])
        w_v = place("w_v", 155.75, [P, 2, M_HEADS, M_DH + 1])
        num = place("num", 160, [P, 2, M_HEADS, M_DH + 1])
        h_new = place("h_new", 164.25, [P, M_HEADS, M_DH])
        y_in = place("y_in", 168, [P, TL, D])
        scan_mask = place("scan_mask", 200, [P, 2, M_HEADS, P], BF16)
        band_mask = place("band_mask", 202, [P, 2, P], BF16)
        ident_b = place("ident_b", 202.5, [P, P], BF16)
        sink = place("sink", 202.75, [P, A_HEADS])
        small = place("small", 203, [P, 64])
        att_small = place("att_small", 203.25, [P, 4, 4])
        wo_h = place("wo_h", 126, [P, 2, KD, 256], F32R)
        wo_l = place("wo_l", 142, [P, 2, KD, 256], F32R)
        wo_raw = place("wo_raw", 158, [P, 2, KD, P])
        gate_row2 = place("gate_row2", 112, [P, 1, D])
        res_rows2 = [place(f"res_row2_{t}", at, [P, D]) for t, at in enumerate((168, 172, 176, 192, 196, 64, 68, 116))]
        ln_rows_x2 = place("ln_rows_x2", 72, [P, 2, D])
        turn_buf3 = place("turn_buf3", 180, [P, 2, BANK])
        ln_rows2 = place("ln_rows2", 184, [P, 2, D])
        ln_rows3 = place("ln_rows3", 144, [P, 2, D])

        x2_dram = nc.dram_tensor("x2_rows", [TL, P, D], F32, kind="Internal").ap()
        x1_dram = nc.dram_tensor("x1_rows", [TL, P, D], F32, kind="Internal").ap()
        o_dram = nc.dram_tensor("o_rows", [TL, P, M_WIDTH], F32, kind="Internal").ap()

        def xpart(low, k, at, size):
            if at < N_LAT:
                return (xl_lat if low else xh_lat)[:, k, at:at + size]
            return (xl_ctx if low else xh_ctx)[:, k, at - N_LAT:at - N_LAT + size]

        ident_set = sem("ident_set")
        const_set = sem("const_set")
        rows_in = sem("rows_in")
        c_silu = sem("c_silu")
        rows_turned = sem("rows_turned")
        rows_kept = sem("rows_kept")
        early_in = [sem(f"early_in{i}") for i in range(3)]
        early_dve = sem("early_dve")
        early_used = sem("early_used")
        mod_ready = sem("mod_ready")
        dve_step = sem("dve_step")
        x_in = [sem(f"x_in{t}") for t in range(3)]
        ada_in = sem("ada_in")
        ada_read = sem("ada_read")
        ada_used = sem("ada_used")
        out_done = sem("out_done")

        steps = [0]

        def step(dve, instruction):
            steps[0] += 1
            instruction.then_inc(dve_step, 1)
            dve.wait_ge(dve_step, steps[0])

        class Turn:

            def __init__(self, name, chunks):
                self.chunks = chunks
                self.units = [(n, k) for n in range(len(chunks)) for k in range(KD)]
                self.turned = sem(name + "_turned")
                self.scaled = sem(name + "_scaled")
                self.high = sem(name + "_high")
                self.low = sem(name + "_low")

        T1_BANKS = ((4, 5, 6),) * 3
        T2_BANKS = ((0, 1, 2, 3),) * 3
        T3_BANKS = ((2, 3), (4, 5, 6))

        def turn_pe(pe, T, banks, rows_wait, only=None):
            for u, (n, k) in enumerate(T.units):
                if only not in (None, n, (n, k)):
                    continue
                at, size = T.chunks[n]
                if k == 0:
                    rows_wait(pe, n)
                mine = banks[n]
                if k >= len(mine):
                    pe.wait_ge(T.scaled, u - len(mine) + 1)
                elif n:
                    pe.wait_ge(T.scaled, KD * n)
                for i in range(size // P):
                    last = nc.tensor.transpose(psum[:, mine[k % len(mine)], i * P:(i + 1) * P],
                                               y[:, at // P + i, k * P:(k + 1) * P], ident[:])
                last.then_inc(T.turned, 1)

        def turn_act(act, T, banks, buf, before, only=None):
            before(act)
            for u, (n, k) in enumerate(T.units):
                if only not in (None, n):
                    continue
                at, size = T.chunks[n]
                v = int(at >= N_LAT)
                act.wait_ge(T.turned, u + 1)
                if u >= 2:
                    act.wait_ge(T.low, u - 1)
                nc.scalar.activation(buf[:, u % 2, 0:size], psum[:, banks[n][k % len(banks[n])], 0:size], ACT.Identity,
                                     bias=in_shift[:, v, k:k + 1], scale=in_scale[:, v, k:k + 1]).then_inc(T.scaled, 1)

        def turn_dve(dve, T, buf, only=None):
            for u, (n, k) in enumerate(T.units):
                if only not in (None, n):
                    continue
                at, size = T.chunks[n]
                dve.wait_ge(T.scaled, u + 1)
                high = xpart(0, k, at, size)
                nc.vector.tensor_copy(high, buf[:, u % 2, 0:size]).then_inc(T.high, 1)
                dve.wait_ge(T.high, u + 1)
                nc.vector.tensor_tensor(xpart(1, k, at, size), buf[:, u % 2, 0:size], high.bitcast(F32),
                                        ALU.subtract).then_inc(T.low, 1)
                turned = u + 1
            dve.wait_ge(T.low, turned)

        class Ffn:

            def __init__(self, name, which, chunks, ada):
                self.which, self.chunks, self.ada = which, chunks, ada
                self.tiles = sum(size for _, size in chunks) // P
                self.n = len(chunks)
                self.hi = sem(name + "_hi")
                self.lo = sem(name + "_lo")
                self.ab_ready = sem(name + "_ab_ready")
                self.sig_ready = sem(name + "_sig_ready")
                self.glu_ready = sem(name + "_glu_ready")
                self.gh_ready = sem(name + "_gh_ready")
                self.gl_ready = sem(name + "_gl_ready")
                self.y_ready = sem(name + "_y_ready")
                self.y_summed = sem(name + "_y_summed")
                self.raw_in = [sem(f"{name}_raw_in{i}") for i in range(2)]

        def piece_of(pair, i):
            return 2 + 6 * pair + i

        Y_BANKS = (4, 5, 6)

        def ffn_sp(sp, F, beside=lambda stage: None):
            w13, w2 = w13_view[F.which], w2_view[F.which]

            def w13_piece(q, slot, block, part):
                sp.dma_start(raw[:, slot], w13[:, :, bass.ds(part * D_FF + block * P, P)]).then_inc(F.raw_in[slot], 16)

            def w2_piece(slot, block):
                sp.dma_start(raw[:, slot].rearrange("p k n -> p (k n)"), w2[bass.ds(block * P, P), :])\
                    .then_inc(F.raw_in[slot], 16)

            def ada_piece(pair, i, first):
                n = pair * ADA_PER_PAIR + i
                if not F.ada:
                    return
                if i or not first:
                    sp.wait_ge(ada_read, 2 * KD * n)
                sp.dma_start(ada_raw[:], ada_view[:, :, bass.ds((ADA_EARLY + n) * P, P)]).then_inc(ada_in, 16)

            def pair_pieces(pair, first, last):
                q = piece_of(pair, 0)
                for i in range(2):
                    sp.wait_ge(F.lo, q + i - 1)
                    w13_piece(q + i, i, 2 * pair + 1, i)
                if first:
                    beside(0)
                ada_piece(pair, 0, first)
                for i in range(2):
                    sp.wait_ge(F.lo, q + 2 + i - 1)
                    w2_piece(i, 2 * pair + i)
                if first:
                    beside(1)
                ada_piece(pair, 1, first)
                if not last:
                    for i in range(2):
                        sp.wait_ge(F.lo, q + 4 + i - 1)
                        w13_piece(q + 4 + i, i, 2 * pair + 2, i)
                for i in range(2, ADA_PER_PAIR):
                    ada_piece(pair, i, first)

            for i in range(2):
                w13_piece(i, i, 0, i)
            pair_pieces(0, True, False)
            with sp.Fori(1, PAIRS - 1) as pair:
                pair_pieces(pair, False, False)
            pair_pieces(PAIRS - 1, False, True)
        def split_target(q_in_pair):
            if q_in_pair in (0, 1):
                return w13h[:, 1, q_in_pair], w13l[:, 1, q_in_pair]
            if q_in_pair in (2, 3):
                i = q_in_pair - 2
                return (w2h[:, i].rearrange("p (k n) -> p k n", k=KD), w2l[:, i].rearrange("p (k n) -> p k n", k=KD))
            return w13h[:, 0, q_in_pair - 4], w13l[:, 0, q_in_pair - 4]

        EARLY_DVE = [n for n in range(ADA_EARLY) if n % 2]

        def piece_sums(dve, piece, sums, done, count, blocks=range(KD)):
            for k in blocks:
                for v in range(2):
                    factor = more[:, v * KD + k:v * KD + k + 1]
                    if k:
                        dve.wait_ge(done, count + 2 * k + v - 1)
                        nc.vector.scalar_tensor_tensor(sums[:, v], piece[:, k], factor, sums[:, v],
                                                       op0=ALU.mult, op1=ALU.add).then_inc(done, 1)
                    else:
                        nc.vector.tensor_scalar_mul(sums[:, v], piece[:, k], factor).then_inc(done, 1)

        ADA_AFTER = (0, 2, 3)
        ADA_TAKEN = (2, 3, 5)

        def early_pe(pe):
            for n in range(ADA_EARLY):
                if n in EARLY_DVE:
                    continue
                pe.wait_ge(early_in[n % 3], 16 * (n // 3 + 1))
                for k in range(KD):
                    last = nc.tensor.matmul(psum[:, 7, 2 * n:2 * n + 2], ada_early[:, n, k, :], more_c[:, k, :],
                                            start=k == 0, stop=k == KD - 1)
                last.then_inc(early_used, 1)
            for i, n in enumerate(EARLY_DVE):
                pe.wait_ge(early_dve, 2 * KD * (i + 1))
                for v in range(2):
                    last = nc.tensor.matmul(psum[:, 7, 2 * n + v:2 * n + v + 1], early_sum[:, n, v], ones[:],
                                            start=True, stop=True)
                last.then_inc(early_used, 1)

        def ffn_act(act, F, turn_chunk):
            per = 2 * F.n

            def split_high(q, count, to, slot, free_sem=None, free=None):
                act.wait_ge(F.raw_in[slot], count)
                if free_sem is not None:
                    act.wait_ge(free_sem, free)
                nc.scalar.activation(to[0], raw[:, slot], ACT.Copy).then_inc(F.hi, 1)

            def glu_act(pair, first, b, n):
                g = pair * per + b * F.n + n
                at, size = F.chunks[n]
                k = (b * F.n + n) % 2
                act.wait_ge(F.ab_ready, g + 1)
                if not (first and b == 0 and n == 0):
                    act.wait_ge(F.glu_ready, g)
                nc.scalar.activation(glu_sig[:, 0:size], psum[:, 2 * k, 0:size], ACT.Silu).then_inc(F.sig_ready, 1)
                act.wait_ge(F.glu_ready, g + 1)
                if not first:
                    act.wait_ge(F.y_ready, 2 * F.tiles * pair)
                nc.scalar.activation(gh[:, b, at:at + size], glu[:, 0:size], ACT.Copy).then_inc(F.gh_ready, 1)

            def body(pair, first, last):
                def splits(i0, free_sem, free):
                    for i in (i0, i0 + 1):
                        q = piece_of(pair, i)
                        split_high(q, 16 * (3 * pair + 2 + i // 2), split_target(i), i % 2,
                                   free_sem, free)
                splits(0, None if first else F.ab_ready, per * pair)
                glu_act(pair, first, 0, 0)
                if first and F.n > 2:
                    turn_chunk(2)
                splits(2, None if first else F.y_ready, 2 * F.tiles * pair)
                for n in range(1, F.n):
                    glu_act(pair, first, 0, n)
                glu_act(pair, first, 1, 0)
                if not last:
                    splits(4, F.ab_ready, per * pair + F.n)
                for n in range(1, F.n):
                    glu_act(pair, first, 1, n)

            for i in range(2):
                split_high(i, 16, (w13h[:, 0, i], None), i)
            turn_chunk(1)
            body(0, True, False)
            with act.Fori(1, PAIRS - 1) as pair:
                body(pair, False, False)
            body(PAIRS - 1, False, True)

        def ffn_dve(dve, F, before_last_y, tile_summed, turn_chunk, before_first_y=lambda: None):
            per = 2 * F.n

            def split_low(q, to, slot):
                dve.wait_ge(F.hi, q + 1)
                nc.vector.tensor_tensor(to[1], raw[:, slot], to[0].bitcast(F32), ALU.subtract).then_inc(F.lo, 1)

            def glu_dve(pair, first, b, n):
                g = pair * per + b * F.n + n
                at, size = F.chunks[n]
                k = (b * F.n + n) % 2
                dve.wait_ge(F.sig_ready, g + 1)
                if not (first and b == 0 and n == 0):
                    dve.wait_ge(F.gl_ready, g)
                nc.vector.tensor_tensor(glu[:, 0:size], psum[:, 2 * k + 1, 0:size], glu_sig[:, 0:size],
                                        ALU.mult).then_inc(F.glu_ready, 1)
                dve.wait_ge(F.gh_ready, g + 1)
                nc.vector.tensor_tensor(gl[:, b, at:at + size], glu[:, 0:size],
                                        gh[:, b, at:at + size].bitcast(F32), ALU.subtract).then_inc(F.gl_ready, 1)
                if F.ada and b * F.n + n in ADA_AFTER:
                    ada_dve(pair, ADA_AFTER.index(b * F.n + n), first)

            def ada_dve(pair, i, first, blocks=range(KD)):
                piece = pair * ADA_PER_PAIR + i
                if blocks[0] == 0:
                    dve.wait_ge(ada_in, 16 * (piece + 1))
                    if i or not first:
                        dve.wait_ge(ada_used, piece)
                piece_sums(dve, ada_raw, ada_sum, ada_read, 2 * KD * piece, blocks)

            def body(pair, first, last):
                def splits(i0):
                    for i in (i0, i0 + 1):
                        split_low(piece_of(pair, i), split_target(i), i % 2)
                splits(0)
                glu_dve(pair, first, 0, 0)
                if first and F.n > 2:
                    turn_chunk(2)
                splits(2)
                for n in range(1, F.n):
                    glu_dve(pair, first, 0, n)
                glu_dve(pair, first, 1, 0)
                if not last:
                    splits(4)
                for n in range(1, F.n):
                    glu_dve(pair, first, 1, n)
                if last:
                    if F.ada:
                        for i in range(len(ADA_AFTER), ADA_PER_PAIR):
                            ada_dve(pair, i, first)
                        modulation(pair)
                    before_last_y(dve)
                if not first:
                    dve.wait_ge(F.y_summed, 2 * F.tiles * pair)
                if first:
                    before_first_y()
                for u in range(2 * F.tiles):
                    dve.wait_ge(F.y_ready, 2 * F.tiles * pair + u + 1)
                    rows = y[:, u // 2, (u % 2) * BANK:(u % 2 + 1) * BANK]
                    bank = psum[:, Y_BANKS[u % 3], :]
                    if first:
                        nc.vector.tensor_copy(rows, bank).then_inc(F.y_summed, 1)
                    else:
                        nc.vector.tensor_tensor(rows, bank, rows, ALU.add).then_inc(F.y_summed, 1)
                    if last and u % 2 == 1:
                        dve.wait_ge(F.y_summed, 2 * F.tiles * pair + u + 1)
                        tile_summed(dve, u // 2)
                    if F.ada and not last and u < KD * (ADA_PER_PAIR - len(ADA_AFTER)):
                        ada_dve(pair, len(ADA_AFTER) + u // KD, first, [u % KD])
                if F.ada and not last:
                    modulation(pair)

            def modulation(pair):
                if F.ada:
                    dve.wait_ge(ada_used, ADA_PER_PAIR * (pair + 1))
                    at = ADA_EARLY + ADA_PER_PAIR * pair
                    nc.vector.tensor_tensor(
                        mod[:, bass.ds(at, ADA_PER_PAIR), :],
                        psum[:, 7, 0:2 * ADA_PER_PAIR].rearrange("p (a b) -> p a b", b=2),
                        params[:, bass.ds(at, ADA_PER_PAIR)].unsqueeze(2).to_broadcast([P, ADA_PER_PAIR, 2]),
                        ALU.add).then_inc(mod_ready, 1)

            for i in range(2):
                split_low(i, (w13h[:, 0, i], w13l[:, 0, i]), i)
            turn_chunk(1)
            body(0, True, False)
            with dve.Fori(1, PAIRS - 1) as pair:
                body(pair, False, False)
            body(PAIRS - 1, False, True)

        def ffn_pe(pe, F, turn, before_last_y, turn_unit):
            per = 2 * F.n
            units = 2 * F.tiles
            prev_user = {u: (u - 3 if u >= 3 else max(v for v in range(units) if v % 3 == u) - units)
                         for u in range(units)}

            def ada(pair, i):
                if not F.ada:
                    return
                n = pair * ADA_PER_PAIR + i
                if i == 0:
                    pe.wait_ge(mod_ready, pair + 1)
                pe.wait_ge(ada_read, 2 * KD * (n + 1))
                for v in range(2):
                    last = nc.tensor.matmul(psum[:, 7, 2 * i + v:2 * i + v + 1], ada_sum[:, v], ones[:],
                                            start=True, stop=True)
                last.then_inc(ada_used, 1)

            def body(pair, first, last_pair):
                for b in range(2):
                    pe.wait_ge(F.lo, piece_of(pair, 0) + 2 * b)
                    for n, (at, size) in enumerate(F.chunks):
                        g = pair * per + b * F.n + n
                        k2 = (b * F.n + n) % 2
                        if not (first and b * F.n + n < 2):
                            pe.wait_ge(F.glu_ready, g - 1)
                        for part in range(2):
                            o = psum[:, 2 * k2 + part, 0:size]
                            for k in range(KD):
                                if first and b == 0 and part == 0:
                                    pe.wait_ge(turn.low, KD * n + k + 1)
                                wh, wl = w13h[:, b, part, k], w13l[:, b, part, k]
                                high, low = xpart(0, k, at, size), xpart(1, k, at, size)
                                nc.tensor.matmul(o, wh, high, start=k == 0, stop=False)
                                nc.tensor.matmul(o, wh, low, start=False, stop=False)
                                last = nc.tensor.matmul(o, wl, high, start=False, stop=k == KD - 1)
                                if k == KD - 1 and part:
                                    last.then_inc(F.ab_ready, 1)
                                if first and b == 0 and n + 1 < F.n and k % 2:
                                    turn_unit(n + 1, (KD * part + k) // 2)
                        if b * F.n + n in ADA_TAKEN:
                            ada(pair, ADA_TAKEN.index(b * F.n + n))
                if last_pair:
                    for i in range(len(ADA_TAKEN), ADA_PER_PAIR):
                        ada(pair, i)
                    before_last_y(pe)
                pe.wait_ge(F.lo, piece_of(pair, 4))
                for u in range(units):
                    t, half = u // 2, u % 2
                    n = next(i for i, (at, size) in enumerate(F.chunks) if at <= t * P < at + size)
                    if half == 0 and (t * P == F.chunks[n][0]):
                        pe.wait_ge(F.gl_ready, pair * per + F.n + n + 1)
                    if not first or u >= 3:
                        pe.wait_ge(F.y_summed, units * pair + prev_user[u] + 1)
                    o = psum[:, Y_BANKS[u % 3], :]
                    cols = slice(half * BANK, (half + 1) * BANK)
                    for b in range(2):
                        lh, ll = gh[:, b, t * P:(t + 1) * P], gl[:, b, t * P:(t + 1) * P]
                        nc.tensor.matmul(o, lh, w2h[:, b, cols], start=b == 0, stop=False)
                        nc.tensor.matmul(o, lh, w2l[:, b, cols], start=False, stop=False)
                        last = nc.tensor.matmul(o, ll, w2h[:, b, cols], start=False, stop=b == 1)
                    last.then_inc(F.y_ready, 1)
                    if u in (KD + 1, 2 * KD + 1) and not last_pair:
                        ada(pair, len(ADA_TAKEN) + u // KD - 1)

            body(0, True, False)
            with pe.Fori(1, PAIRS - 1) as pair:
                body(pair, False, False)
            body(PAIRS - 1, False, True)

        class Norm:

            def __init__(self, name):
                self.gates_summed = sem(name + "_gates_summed")
                self.gates_kept = sem(name + "_gates_kept")
                self.rows_in = [sem(f"{name}_rows_in{i}") for i in range(3)]
                self.added = sem(name + "_added")
                self.measured = sem(name + "_measured")
                self.inverted = sem(name + "_inverted")
                self.done = sem(name + "_done")
                self.prepared = sem(name + "_prepared")

        def gate_rows_pe(pe, N, which, vectors):
            for v in range(vectors):
                for k in range(KD):
                    column = mod[:, which * KD + k, v:v + 1].to_broadcast([P, P])
                    last = nc.tensor.matmul(psum[:, 2 * v + k // 4, (k % 4) * P:(k % 4 + 1) * P], column, ident[:],
                                            start=True, stop=True)
            last.then_inc(N.gates_summed, 1)

        def gate_rows_act(act, N, vectors, scale):
            act.wait_ge(N.gates_summed, 1)
            for v in range(vectors):
                for half in range(2):
                    nc.scalar.activation(gate_row[:, v, half * BANK:(half + 1) * BANK], psum[:, 2 * v + half, :],
                                         ACT.Copy, scale=scale).then_inc(N.gates_kept, 1)

        def norm_sums_dve(dve, N, t, residual):
            s = ln_stats[:, t % 2]
            if t >= 2:
                dve.wait_ge(N.done, t - 1)
            for half in range(2):
                step(dve, nc.vector.bn_stats(s[:, 6 * half:6 * half + 6], y[:, t, half * BANK:(half + 1) * BANK]))
            step(dve, nc.vector.bn_aggr(s[:, 12:14], s[:, 0:12].rearrange("p (a b) -> p a b", b=6)))
            step(dve, nc.vector.tensor_scalar_add(s[:, 14:15], s[:, 13:14], LN_EPS))
            nc.vector.tensor_scalar_mul(s[:, 15:16], s[:, 12:13], -1.0).then_inc(N.measured, 1)

        def norm_pool(pool, N, t):
            s = ln_stats[:, t % 2]
            pool.wait_ge(N.measured, t + 1)
            nc.gpsimd.tensor_tensor(s[:, 16:17], s[:, 14:15], minus_half[:, 0:1], ALU.pow).then_inc(N.inverted, 1)
            pool.wait_ge(N.inverted, 2 * t + 1)
            nc.gpsimd.tensor_tensor(s[:, 17:18], s[:, 15:16], s[:, 16:17], ALU.mult).then_inc(N.inverted, 1)

        def norm_act(act, N, t):
            s = ln_stats[:, t % 2]
            act.wait_ge(N.inverted, 2 * t + 2)
            nc.scalar.activation(y[:, t, :], y[:, t, :], ACT.Identity, bias=s[:, 17:18], scale=s[:, 16:17])\
                .then_inc(N.done, 1)

        def first_norm_dve(dve, t):
            for t in [t - 1] * (t > 0) + [t] * (t == TA - 1):
                dve.wait_ge(N1.prepared, t + 1)
                dve.wait_ge(N1.rows_in[t % 3], 16 * (t // 3 + 1))
                nc.vector.scalar_tensor_tensor(y[:, t, :], res_row[:, t % 3, :], ALPHA, y[:, t, :],
                                               op0=ALU.mult, op1=ALU.add).then_inc(N1.added, 1)
                dve.wait_ge(N1.added, t + 1)
                norm_sums_dve(dve, N1, t, None)

        def first_norm_pool(pool):
            pool.wait_ge(N1.gates_kept, 4)
            for t in range(TA):
                pool.wait_ge(F1.y_summed, 2 * TA * (PAIRS - 1) + 2 * t + 2)
                nc.gpsimd.tensor_tensor(y[:, t, :], y[:, t, :], gate_row[:, int(t >= TL), :], ALU.mult)\
                    .then_inc(N1.prepared, 1)
                if t:
                    norm_pool(pool, N1, t - 1)
            norm_pool(pool, N1, TA - 1)

        def affine_of(dve, norm, scale_at, shift_at):
            gain = params[:, 72 + norm * KD:72 + (norm + 1) * KD].unsqueeze(1).to_broadcast([P, 2, KD])
            bias = params[:, 96 + norm * KD:96 + (norm + 1) * KD].unsqueeze(1).to_broadcast([P, 2, KD])
            scale = mod[:, scale_at * KD:(scale_at + 1) * KD, :].rearrange("p k v -> p v k")
            shift = mod[:, shift_at * KD:(shift_at + 1) * KD, :].rearrange("p k v -> p v k")
            step(dve, nc.vector.scalar_tensor_tensor(in_scale[:], scale, 1.0, gain, op0=ALU.add, op1=ALU.mult))
            step(dve, nc.vector.scalar_tensor_tensor(in_shift[:], scale, 1.0, bias, op0=ALU.add, op1=ALU.mult))
            step(dve, nc.vector.tensor_tensor(in_shift[:], in_shift[:], shift, ALU.add))

        UNITS = [("k", OFF_K, OFF_K + P, 0), ("k", OFF_K + 2 * P, OFF_K + 3 * P, 1),
                 ("q", OFF_Q, OFF_Q + P, 0), ("q", OFF_Q + 2 * P, OFF_Q + 3 * P, 1),
                 ("v", OFF_V, OFF_V + P, 0), ("v", OFF_V + 2 * P, OFF_V + 3 * P, 1),
                 ("kv", OFF_KA, OFF_VA, 0),
                 ("qa", OFF_QA, OFF_QA + 2 * P, 0), ("qa", OFF_QA + P, OFF_QA + 3 * P, 1),
                 ("o", OFF_O, OFF_O + P, 0), ("o", OFF_O + 2 * P, OFF_O + 3 * P, 1)]

        def outputs():
            out = [("gates", -1, 0, at, size) for at, size in CHUNKS_ALL]
            for u, (kind, _, _, which) in enumerate(UNITS):
                if kind in "kq":
                    for half in range(2):
                        for at, size in (CHUNKS_ALL if kind == "k" else CHUNKS_LAT):
                            out.append((kind, u, 2 * which + half, at, size))
                else:
                    for t in range(TA if kind in ("v", "kv") else TL):
                        out.append((kind, u, which, t * P, P))
            return out

        OUTPUTS = outputs()
        P_BANKS = 7
        by_vector = [kind in ("kv", "qa") for kind, *_ in OUTPUTS]

        def read_before(j, vector):
            return sum(1 for i in range(j + 1) if by_vector[i] == vector)

        p_in = [sem(f"p_in{i}") for i in range(2)]
        gate_in = sem("gate_in")
        gate_clear = sem("gate_clear")
        gate_w = sem("gate_w")
        gate_low = sem("gate_low")
        p_hi = sem("p_hi")
        p_lo = sem("p_lo")
        p_ready = sem("p_ready")
        p_read_act = sem("p_read_act")
        p_read_dve = sem("p_read_dve")
        conv_done = sem("conv_done")
        conv_kept = sem("conv_kept")
        q_scaled = sem("q_scaled")
        x1_stored = sem("x1_stored")
        rope_in = sem("rope_in")
        roped = sem("roped")
        rope_turned = sem("rope_turned")
        rope_kept = sem("rope_kept")
        o_stored = [sem(f"o_stored{i}") for i in range(2)]
        pads_set = sem("pads_set")
        gate_step_act = sem("gate_step_act")
        gate_step_dve = sem("gate_step_dve")
        gate_args = sem("gate_args")
        gate_exps = sem("gate_exps")
        gate_copies = sem("gate_copies")
        gate_turned = sem("gate_turned")
        gate_kept = sem("gate_kept")
        ROPED = [j for j, (kind, u, which, at, size) in enumerate(OUTPUTS)
                 if kind == "qa" or kind == "kv"]

        def unit_last(u):
            return max(j for j, o in enumerate(OUTPUTS) if o[1] == u)

        def proj_sp(sp):
            sp.wait_ge(F1.y_ready, 2 * TA * PAIRS)
            sp.dma_start(gate_raw[:], w_in_view[:, :, OFF_G:OFF_G + 16]).then_inc(gate_in, 16)
            sp.wait_ge(gate_clear, 1)
            for row, at in ((0, 0), (32, 8), (64, 4), (96, 12)):
                sp.dma_start(gate_bias[row:row + 4, :], b_gates[0, at:at + 4].rearrange("(p a) -> p a", a=1))\
                    .then_inc(gate_in, 16)

            def piece(q):
                if q >= 2:
                    sp.wait_ge(p_lo, q - 1)
                at = UNITS[q // 2][1 + q % 2]
                sp.dma_start(p_raw[:, q % 2], w_in_view[:, :, at:at + P]).then_inc(p_in[q % 2], 16)
            piece(0)
            piece(1)
            for t in range(TL):
                sp.wait_ge(N1.done, t + 1)
                sp.dma_start(x1_dram[t], y[:, t, :]).then_inc(x1_stored, 16)
            for q in range(2, 2 * len(UNITS)):
                piece(q)
                if UNITS[q // 2][0] == "kv" and q % 2 == 0:
                    sp.wait_ge(conv_kept, 8)
                    for t in range(TL):
                        sp.dma_start(rope_tab[:, t], rope_cs[:, t * P:(t + 1) * P, :].rearrange("s p f -> p s f"))\
                            .then_inc(rope_in, 16)
            n = 0
            for j, (kind, u, which, at, size) in enumerate(OUTPUTS):
                if kind == "o":
                    sp.wait_ge(p_read_act, read_before(j, False))
                    sp.dma_start(o_dram[at // P, :, which * 256:(which + 1) * 256], o_sig[:, n % 2]).then_inc(o_stored[n % 2], 16)
                    n += 1

        def spans(row):
            def nat(t, at, size):
                part = t[row:row + 32, at:at + size]
                return part if row == 0 else part[:, ::-1]
            return [(slice(0, N_CTX), lambda t: nat(t, N_LAT, N_CTX)),
                    (slice(N_CTX, N_ALL), lambda t: nat(t, 0, N_LAT))]

        def proj_high(act, q):
            u = q // 2
            act.wait_ge(p_in[q % 2], 16 * (q // 2 + 1))
            if u >= 2:
                act.wait_ge(p_ready, unit_last(u - 2) + 1)
            elif u == 1:
                act.wait_ge(p_ready, 3)
            nc.scalar.activation(p_wh[:, u % 2, :, (q % 2) * P:(q % 2 + 1) * P], p_raw[:, q % 2], ACT.Copy)\
                .then_inc(p_hi, 1)

        def first_weights_act(act):
            act.wait_ge(gate_clear, 2)
            act.wait_ge(gate_in, 16 * 5)
            for row, at in ((0, 0), (32, 8), (64, 4), (96, 12)):
                nc.scalar.activation(gate_wh[:, :, row:row + 4], gate_raw[:, :, at:at + 4], ACT.Copy).then_inc(gate_w, 1)
            proj_high(act, 0)
            proj_high(act, 1)

        def proj_act(act):
            conv_n = 0
            o_n = 0
            kept = 0
            for j, (kind, u, which, at, size) in enumerate(OUTPUTS):
                first_of_unit = j == 0 or OUTPUTS[j - 1][1] != u
                if first_of_unit and kind != "gates" and u + 1 < len(UNITS):
                    proj_high(act, 2 * u + 2)
                    proj_high(act, 2 * u + 3)
                bank = psum[:, j % P_BANKS, :]
                if kind == "gates":
                    act.wait_ge(p_ready, j + 1)
                    nc.scalar.activation(gate_all[:, at:at + size], bank[:, 0:size], ACT.Identity, bias=gate_bias[:, 0:1])\
                        .then_inc(p_read_act, 1)
                    if at >= N_LAT:
                        gates_act_logs(act)
                elif kind in "kq":
                    act.wait_ge(p_ready, j + 1)
                    if at == 0 and conv_n:
                        act.wait_ge(conv_done, conv_n)
                    if at == 0 and not conv_n:
                        act.wait_ge(pads_set, 1)
                        act.wait_ge(x1_stored, 16 * TL)
                    to = 2 + at if at < N_LAT else 1030 + at - N_LAT
                    nc.scalar.activation(conv_in[:, to:to + size], bank[:, 0:size], ACT.Copy).then_inc(p_read_act, 1)
                    last = at + size == (N_ALL if kind == "k" else N_LAT)
                    if last:
                        conv_n += 1
                        act.wait_ge(conv_done, conv_n)
                        dst = (kT if kind == "k" else qT)[:, which, :]
                        inst = nc.scalar.activation(dst[:, 0:N_LAT], conv_sum[:, 0:N_LAT], ACT.Silu)
                        if kind == "k":
                            inst = nc.scalar.activation(dst[:, N_LAT:N_ALL], conv_sum[:, 1028:1028 + N_CTX], ACT.Silu)
                        inst.then_inc(conv_kept, 1)
                        if conv_n == 1:
                            gates_act_exps(act)
                elif kind == "v":
                    act.wait_ge(p_ready, j + 1)
                    nc.scalar.activation(vext[:, at // P, 2 * which:2 * which + 2, 0:M_DH],
                                         bank[:, 0:256].rearrange("p (h d) -> p h d", h=2), ACT.Copy).then_inc(p_read_act, 1)
                elif kind == "o":
                    act.wait_ge(p_ready, j + 1)
                    if o_n >= 2:
                        act.wait_ge(o_stored[o_n % 2], 16 * (o_n // 2))
                    nc.scalar.activation(o_sig[:, o_n % 2], bank[:, 0:256], ACT.Sigmoid).then_inc(p_read_act, 1)
                    o_n += 1
                else:
                    act.wait_ge(rope_turned, kept + 1)
                    t = at // P
                    if kind == "kv":
                        nc.scalar.activation(kaT[:, at:at + P], psum[:, 7, 0:P], ACT.Copy).then_inc(rope_kept, 1)
                    else:
                        nc.scalar.activation(qaT[:, 2 * which:2 * which + 2, at:at + P],
                                             psum[:, 7, 0:256].rearrange("p (a b) -> p a b", a=2), ACT.Copy,
                                             scale=A_DH ** -0.5).then_inc(rope_kept, 1)
                    kept += 1

        def gates_act_logs(act):
            act.wait_ge(gate_step_dve, 1)
            nc.scalar.activation(gate_abs[64:P, :], gate_abs[64:P, :], ACT.Exp, scale=-1.0).then_inc(gate_step_act, 1)
            act.wait_ge(gate_step_act, 1)
            nc.scalar.activation(gate_abs[64:P, :], gate_abs[64:P, :], ACT.Ln, bias=1.0).then_inc(gate_step_act, 1)

        def gates_act_exps(act):
            act.wait_ge(gate_args, 1)
            nc.scalar.activation(decay[0:64, 20:30], decay[0:64, 20:30], ACT.Exp)
            for row in (0, 32):
                (c_scan, c_nat), (l_scan, l_nat) = spans(row)
                rows = slice(row, row + 32)
                nc.scalar.activation(c_nat(w_nat), e_row[rows, c_scan], ACT.Exp)
                nc.scalar.activation(l_nat(w_nat), e_row[rows, l_scan], ACT.Exp)
                nc.scalar.activation(l_nat(inter_nat), lf_row[rows, l_scan], ACT.Exp)
                last = nc.scalar.activation(l_nat(floor_nat), m_row[rows, l_scan], ACT.Exp, scale=-1.0)
            last.then_inc(gate_exps, 1)

        def gates_dve(dve):
            n = [0]

            def gstep(i):
                n[0] += 1
                i.then_inc(gate_step_dve, 1)
                dve.wait_ge(gate_step_dve, n[0])
            dve.wait_ge(p_read_act, 3)
            dve.wait_ge(x1_stored, 16 * TL)
            f = gate_all[64:P, :]
            gstep(nc.vector.scalar_tensor_tensor(gate_abs[64:P, :], f, -1.0, f, op0=ALU.mult, op1=ALU.max))
            gstep(nc.vector.tensor_scalar_min(f, f, 0.0))
            dve.wait_ge(gate_step_act, 2)
            gstep(nc.vector.tensor_tensor(f, f, gate_abs[64:P, :], ALU.subtract))
            for row in (0, 32):
                rows = slice(row, row + 32)
                for scan, nat in spans(row):
                    nc.vector.tensor_copy(li_row[rows, scan], nat(gate_all))
            for row in (0, 32):
                rows = slice(row, row + 32)
                for scan, nat in spans(row):
                    src = gate_all[64 + row:96 + row, :]
                    cols = src[:, N_LAT:N_ALL] if scan.start == 0 else src[:, 0:N_LAT]
                    last = nc.vector.tensor_copy(lf_row[rows, scan], cols if row == 0 else cols[:, ::-1])
            gstep(last)
            for t in range(TA):
                cols = slice(t * P, (t + 1) * P)
                nc.vector.tensor_tensor_scan(b_row[0:64, cols], lf_row[0:64, cols], lf_row[0:64, cols], 0.0,
                                             ALU.add, ALU.bypass)
            gstep(nc.vector.tensor_tensor_scan(m_row[0:64, :], lf_row[0:64, :], li_row[0:64, :], 0.0, ALU.add, ALU.max))
            gstep(nc.vector.tensor_tensor(a_row[0:64, :], li_row[0:64, :], b_row[0:64, :], ALU.subtract))
            gstep(nc.vector.tensor_tensor(b_row[0:64, :], b_row[0:64, :], m_row[0:64, :], ALU.subtract))
            ends = slice(P - 1, N_ALL, P)
            nc.vector.tensor_copy(decay[0:64, 0:TA], b_row[0:64, ends])
            nc.vector.memset(decay[0:64, TA:TA + 1], 0.0)
            gstep(nc.vector.tensor_copy(decay[0:64, TA + 1:2 * TA], m_row[0:64, P - 1:N_ALL - P:P]))
            by_chunk = lambda t: t[0:64, :].rearrange("p (c t) -> p c t", t=P)
            wide = lambda at: decay[0:64, at:at + TA].unsqueeze(2).to_broadcast([64, TA, P])
            nc.vector.tensor_tensor(decay[0:64, 20:30], decay[0:64, 0:TA], decay[0:64, TA:2 * TA], ALU.add)
            nc.vector.tensor_tensor(by_chunk(e_row), by_chunk(a_row), wide(0), ALU.add)
            nc.vector.tensor_tensor(by_chunk(lf_row), by_chunk(b_row), wide(TA), ALU.add).then_inc(gate_args, 1)
            for row in (0, 32):
                rows = slice(row, row + 32)
                for scan, nat in spans(row):
                    nc.vector.tensor_copy(nat(a_nat), a_row[rows, scan])
                    last = nc.vector.tensor_copy(nat(u_row), b_row[rows, scan])
            last.then_inc(gate_copies, 1)

        GATE_TURNS = [(i, t) for i in range(4) for t in range(TA if i < 2 else TL)]
        GATE_ROUNDS = [GATE_TURNS[i:i + 8] for i in range(0, len(GATE_TURNS), 8)]

        def gates_pe(pe):
            pe.wait_ge(gate_exps, 1)
            pe.wait_ge(gate_copies, 1)
            for r, turns in enumerate(GATE_ROUNDS):
                if r:
                    pe.wait_ge(gate_kept, r)
                for n, (i, t) in enumerate(turns):
                    src = (a_nat, w_nat, inter_nat, floor_nat)[i][0:64, t * P:(t + 1) * P]
                    last = nc.tensor.transpose(psum[:, 7, 64 * n:64 * (n + 1)], src, ident[0:64, 0:64])
                if r == len(GATE_ROUNDS) - 1:
                    for i in range(2 * M_HEADS):
                        row = 32 * (i // M_HEADS) + i % M_HEADS
                        last = nc.tensor.matmul(psum[:, 7, 256 + 10 * i:266 + 10 * i],
                                                ident[0:64, row:row + 1].to_broadcast([64, P]), decay[0:64, 20:30],
                                                start=True, stop=True)
                last.then_inc(gate_turned, 1)

        def gates_keep_dve(dve):
            for r, turns in enumerate(GATE_ROUNDS):
                dve.wait_ge(gate_turned, r + 1)
                for i in range(4):
                    mine = [(n, t) for n, (q, t) in enumerate(turns) if q == i]
                    if mine:
                        n0, n1 = mine[0][0], mine[-1][0] + 1
                        t0, t1 = mine[0][1], mine[-1][1] + 1
                        last = nc.vector.tensor_copy(
                            tok_gate[:, i, t0:t1].rearrange("p t (d h) -> p t d h", d=2),
                            psum[:, 7, 64 * n0:64 * n1].rearrange("p (t d r) -> p t d r", d=2, r=32)[:, :, :, 0:M_HEADS])
                if r == len(GATE_ROUNDS) - 1:
                    last = nc.vector.tensor_copy(decay_all[:], psum[:, 7, 256:336].rearrange("p (r c) -> p r c", c=TA))
                last.then_inc(gate_kept, 1)

        def proj_low(dve, q):
            u = q // 2
            dve.wait_ge(p_hi, q + 1)
            cols = slice((q % 2) * P, (q % 2 + 1) * P)
            nc.vector.tensor_tensor(p_wl[:, u % 2, :, cols], p_raw[:, q % 2], p_wh[:, u % 2, :, cols].bitcast(F32),
                                    ALU.subtract).then_inc(p_lo, 1)

        def first_weights_dve(dve):
            for i in range(4):
                row, at = ((0, 0), (32, 8), (64, 4), (96, 12))[i]
                dve.wait_ge(gate_w, i + 1)
                nc.vector.tensor_tensor(gate_wl[:, :, row:row + 4], gate_raw[:, :, at:at + 4],
                                        gate_wh[:, :, row:row + 4].bitcast(F32), ALU.subtract).then_inc(gate_low, 1)

            proj_low(dve, 0)
            proj_low(dve, 1)

        def proj_dve(dve):
            conv_n = 0
            kept = 0
            for j, (kind, u, which, at, size) in enumerate(OUTPUTS):
                first_of_unit = j == 0 or OUTPUTS[j - 1][1] != u
                if first_of_unit and kind != "gates" and u + 1 < len(UNITS):
                    proj_low(dve, 2 * u + 2)
                    proj_low(dve, 2 * u + 3)
                bank = psum[:, j % P_BANKS, :]
                if kind == "k" and which == 2 and at == 0:
                    gates_keep_dve(dve)
                if kind == "kv" and at == 0:
                    nc.vector.memset(vext[:, :, :, M_DH:M_DH + 1], 1.0)
                if kind == "gates" and at >= N_LAT:
                    gates_dve(dve)
                elif kind in "kq" and at + size == (N_ALL if kind == "k" else N_LAT):
                    dve.wait_ge(p_read_act, read_before(j, False))
                    if conv_n:
                        dve.wait_ge(conv_kept, conv_n)
                    size = 1284 if kind == "k" else N_LAT
                    col = which + (4 if kind == "k" else 0)
                    w = [more[:, 16 + 8 * i + col:17 + 8 * i + col] for i in range(CONV_W)]
                    step(dve, nc.vector.tensor_scalar(conv_sum[:, 0:size], conv_in[:, 0:size], w[0],
                                                      more[:, 56 + col:57 + col], ALU.mult, ALU.add))
                    for i in range(1, CONV_W):
                        last = nc.vector.scalar_tensor_tensor(conv_sum[:, 0:size], conv_in[:, i:i + size], w[i],
                                                              conv_sum[:, 0:size], op0=ALU.mult, op1=ALU.add)
                        if i < CONV_W - 1:
                            step(dve, last)
                    conv_n += 1
                    last.then_inc(conv_done, 1)
                    if kind == "q":
                        dve.wait_ge(conv_kept, conv_n)
                        nc.vector.tensor_scalar_mul(qT[:, which, :], qT[:, which, :], M_DH ** -0.5).then_inc(q_scaled, 1)
                elif kind in ("kv", "qa"):
                    t = at // P
                    dve.wait_ge(p_ready, j + 1)
                    if kept == 0:
                        dve.wait_ge(rope_in, 16 * TL)
                    if kept >= 2:
                        dve.wait_ge(rope_turned, kept - 1)
                    out = rope_out[:, kept % 2]
                    if kind == "kv" and t >= TL:
                        nc.vector.tensor_copy(out[:, 0:P], bank[:, 0:P]).then_inc(roped, 1)
                    else:
                        n = 1 if kind == "kv" else 2
                        w = 2 * n * A_DH
                        src = bank[:, 0:w].rearrange("p (h s f) -> p h s f", s=2, f=A_DH // 2)
                        ta = rope_ab[:, 0, 0:w].rearrange("p (h s f) -> p h s f", s=2, f=A_DH // 2)
                        tb = rope_ab[:, 1, 0:w].rearrange("p (h s f) -> p h s f", s=2, f=A_DH // 2)
                        cs = [rope_tab[:, t, i].unsqueeze(1).to_broadcast([P, 2 * n, A_DH // 2]) for i in range(2)]
                        for s in range(2):
                            step(dve, nc.vector.tensor_tensor(ta[:, :, s], src[:, :, s], cs[0], ALU.mult))
                            step(dve, nc.vector.tensor_tensor(tb[:, :, 1 - s], src[:, :, s], cs[1], ALU.mult))
                        o = out[:, 0:w].rearrange("p (i g s f) -> p g i s f", g=2, s=2, f=A_DH // 2)
                        a = rope_ab[:, 0, 0:w].rearrange("p (g i s f) -> p g i s f", g=2, s=2, f=A_DH // 2)
                        b = rope_ab[:, 1, 0:w].rearrange("p (g i s f) -> p g i s f", g=2, s=2, f=A_DH // 2)
                        step(dve, nc.vector.tensor_tensor(o[:, :, :, 0], a[:, :, :, 0], b[:, :, :, 0], ALU.subtract))
                        nc.vector.tensor_tensor(o[:, :, :, 1], a[:, :, :, 1], b[:, :, :, 1], ALU.add).then_inc(roped, 1)
                    kept += 1
                    if kind == "kv":
                        nc.vector.tensor_copy(va[:, t, :], bank[:, P:2 * P]).then_inc(p_read_dve, 1)
                    else:
                        dve.wait_ge(roped, kept)
                        nc.vector.tensor_copy(minus_half[:, 1:2], minus_half[:, 0:1]).then_inc(p_read_dve, 1)

        def proj_pe(pe):
            kept = 0

            def turn_roped(i):
                j = ROPED[i]
                kind, u, which, at, size = OUTPUTS[j]
                pe.wait_ge(roped, i + 1)
                if i >= 1:
                    pe.wait_ge(rope_kept, i)
                for n in range(1 if kind == "kv" else 2):
                    last = nc.tensor.transpose(psum[:, 7, n * P:(n + 1) * P], rope_out[:, i % 2, n * P:(n + 1) * P], ident[:])
                last.then_inc(rope_turned, 1)

            for j, (kind, u, which, at, size) in enumerate(OUTPUTS):
                o = psum[:, j % P_BANKS, :]
                if j < P_BANKS:
                    if j == 0:
                        pe.wait_ge(T2.scaled, len(T2.units))
                        pe.wait_ge(F1.y_summed, 2 * TA * PAIRS)
                else:
                    i = j - P_BANKS
                    pe.wait_ge(p_read_dve if by_vector[i] else p_read_act, read_before(i, by_vector[i]))
                if kind == "gates":
                    n = CHUNKS_ALL.index((at, size))
                    if n == 0:
                        pe.wait_ge(gate_low, 4)
                    pe.wait_ge(T2.low, KD * (n + 1))
                    for k in range(KD):
                        high, low = xpart(0, k, at, size), xpart(1, k, at, size)
                        nc.tensor.matmul(o[:, 0:size], gate_wh[:, k, :], high, start=k == 0, stop=False)
                        nc.tensor.matmul(o[:, 0:size], gate_wh[:, k, :], low, start=False, stop=False)
                        last = nc.tensor.matmul(o[:, 0:size], gate_wl[:, k, :], high, start=False, stop=k == KD - 1)
                    last.then_inc(p_ready, 1)
                    continue
                if kind == "k" and which == 3 and at >= N_LAT:
                    gates_pe(pe)
                if OUTPUTS[j - 1][1] != u:
                    pe.wait_ge(p_lo, 2 * u + 2)
                if kind in "kq":
                    cols = slice((which % 2) * P, (which % 2 + 1) * P)
                    for k in range(KD):
                        high, low = xpart(0, k, at, size), xpart(1, k, at, size)
                        wh, wl = p_wh[:, u % 2, k, cols], p_wl[:, u % 2, k, cols]
                        nc.tensor.matmul(o[:, 0:size], wh, high, start=k == 0, stop=False)
                        nc.tensor.matmul(o[:, 0:size], wh, low, start=False, stop=False)
                        last = nc.tensor.matmul(o[:, 0:size], wl, high, start=False, stop=k == KD - 1)
                else:
                    for k in range(KD):
                        high, low = xpart(0, k, at, P), xpart(1, k, at, P)
                        wh, wl = p_wh[:, u % 2, k, :], p_wl[:, u % 2, k, :]
                        nc.tensor.matmul(o[:, 0:256], high, wh, start=k == 0, stop=False)
                        nc.tensor.matmul(o[:, 0:256], high, wl, start=False, stop=False)
                        last = nc.tensor.matmul(o[:, 0:256], low, wh, start=False, stop=k == KD - 1)
                last.then_inc(p_ready, 1)
                if j - 2 >= ROPED[0] and kept < len(ROPED):
                    turn_roped(kept)
                    kept += 1
            while kept < len(ROPED):
                turn_roped(kept)
                kept += 1

        STEPS = [(0, TL), (1, TL + 1), (0, TL + 1), (1, TL)]
        for s_ in range(TL):
            STEPS += [(0, s_), (1, TL - 1 - s_)]
        LAT0 = 4
        UPDATES = [n for n in range(len(STEPS)) if n < len(STEPS) - 2]

        def chunk_of(n):
            return n // 2

        def state_before(n):
            return max(i for i in range(n) if STEPS[i][0] == STEPS[n][0]) + 1

        kt_turned = sem("kt_turned")
        kt_kept = sem("kt_kept")
        masks_set = sem("masks_set")
        d_ready = sem("d_ready")
        d_done = sem("d_done")
        p_done = sem("p_done")
        inter_ready = sem("inter_ready")
        inter_read = sem("inter_read")
        intra_ready = sem("intra_ready")
        intra_read = sem("intra_read")
        update_ready = sem("update_ready")
        state_done = sem("state_done")
        wv_done = sem("wv_done")
        h_done = sem("h_done")
        read_measured = sem("read_measured")
        read_inverted = sem("read_inverted")
        read_normed = sem("read_normed")
        read_done = sem("read_done")
        o_loaded = [sem(f"o_loaded{i}") for i in range(2)]
        rows_loaded = sem("rows_loaded")
        cores_step = sem("cores_step")

        flat = psum[:].rearrange("p b c -> p (b c)")
        HEAD_COLS = M_DH + 1
        SCORE_AT = (0, 2 * BANK - P)
        PT_AT = 3 * BANK
        VALUE_AT = 5 * BANK
        DECAY_BANK = 6
        OUT_AT = 7 * BANK - 3 * HEAD_COLS

        TILES_DONE = []
        for n, (d_, t_) in enumerate(STEPS):
            if n >= LAT0 and any(STEPS[i][1] == t_ for i in range(LAT0, n)):
                TILES_DONE.append((n, t_))

        def masks_pool(pool):
            pool.wait_ge(p_ready, len(OUTPUTS))
            for i in range(2):
                pool.wait_ge(o_stored[i], 16 * TL)
            n = [0]

            def mstep(i):
                n[0] += 1
                i.then_inc(masks_set, 1)
                pool.wait_ge(masks_set, n[0])
            mstep(nc.gpsimd.tensor_copy(ident_b[:], ident[:]))
            mstep(nc.gpsimd.memset(scan_mask[:], 0.0))
            mstep(nc.gpsimd.memset(band_mask[:], 0.0))
            mstep(nc.gpsimd.affine_select(out=scan_mask[:, 0], in_=scan_mask[:, 0], compare_op=ALU.is_ge, fill=-1e30,
                                          base=0, pattern=[[0, M_HEADS], [1, P]], channel_multiplier=-1))
            mstep(nc.gpsimd.affine_select(out=scan_mask[:, 1], in_=scan_mask[:, 1], compare_op=ALU.is_ge, fill=-1e30,
                                          base=0, pattern=[[0, M_HEADS], [-1, P]], channel_multiplier=1))
            mstep(nc.gpsimd.affine_select(out=band_mask[:, 0], in_=band_mask[:, 0], compare_op=ALU.is_ge, fill=-1e30,
                                          base=0, pattern=[[1, P]], channel_multiplier=-1))
            mstep(nc.gpsimd.affine_select(out=band_mask[:, 1], in_=band_mask[:, 1], compare_op=ALU.is_ge, fill=-1e30,
                                          base=0, pattern=[[-1, P]], channel_multiplier=1))

        MASKS = 7

        def mlstm_sp(sp):
            sp.wait_ge(p_ready, len(OUTPUTS))
            sp.dma_start(norm_gain[:], mh_norm_g[0:1, :].to_broadcast([P, M_WIDTH])).then_inc(rows_loaded, 16)
            sp.dma_start(sink[:], attn_sink[0:1, :].to_broadcast([P, A_HEADS])).then_inc(rows_loaded, 16)
            for i in range(2):
                sp.wait_ge(o_stored[i], 16 * TL)
            for i, (n, t) in enumerate(TILES_DONE):
                if i >= 2:
                    sp.wait_ge(read_done, 2 * (i - 1))
                sp.dma_start(o_in[:, i % 2], o_dram[t]).then_inc(o_loaded[i % 2], 16)

        def mlstm_pool(pool):
            for n in UPDATES:
                d, t = STEPS[n]
                if n >= 2:
                    pool.wait_ge(update_ready, n - 1)
                w = tok_gate[:, 1, t, 4 * d:4 * d + 4].unsqueeze(2).to_broadcast([P, M_HEADS, M_DH + 1])
                nc.gpsimd.tensor_tensor(w_v[:, d], vext[:, t], w, ALU.mult).then_inc(wv_done, 1)
                readout_pool(pool, n - 1)
            for n in range(len(UPDATES) - 1, len(STEPS)):
                readout_pool(pool, n)

        def readout_pool(pool, n):
            for i, (m, t) in enumerate(TILES_DONE):
                if m != n:
                    continue
                pool.wait_ge(read_measured, i + 1)
                s = small[:, 32 + 8 * (i % 2):36 + 8 * (i % 2)]
                nc.gpsimd.tensor_tensor(s, s, minus_half[:, 0:1].to_broadcast([P, M_HEADS]), ALU.pow)\
                    .then_inc(read_inverted, 1)
                if i == 0:
                    pool.wait_ge(rows_loaded, 32)
                pool.wait_ge(read_normed, i + 1)
                rows = y_in[:, t, 0:M_WIDTH]
                nc.gpsimd.tensor_tensor(rows, rows, norm_gain[:], ALU.mult).then_inc(read_done, 1)
                pool.wait_ge(read_done, 2 * i + 1)
                pool.wait_ge(o_loaded[i % 2], 16 * (i // 2 + 1))
                nc.gpsimd.tensor_tensor(rows, rows, o_in[:, i % 2], ALU.mult).then_inc(read_done, 1)

        def mlstm_act(act):
            for n in range(TA + TL):
                act.wait_ge(kt_turned, n + 1)
                to = k_tok[:, n] if n < TA else scores[:, n - TA].rearrange("p h t -> p (h t)")
                nc.scalar.activation(to, psum[:, n % 4, :], ACT.Copy).then_inc(kt_kept, 1)

        def decays_act(act, n):
            d, t = STEPS[n]
            i = n - LAT0
            act.wait_ge(d_ready, i + 1)
            if i >= 2:
                act.wait_ge(p_done, i - 1)
            for h in range(M_HEADS):
                last = nc.scalar.activation(d_exp[:, d, h], psum[:, DECAY_BANK, h * P:(h + 1) * P], ACT.Exp,
                                            bias=tok_gate[:, 0, t, 4 * d + h:4 * d + h + 1])
            last.then_inc(d_done, 1)

        cstep = [0]

        def core_step(dve, instruction):
            cstep[0] += 1
            instruction.then_inc(cores_step, 1)
            dve.wait_ge(cores_step, cstep[0])

        def cores_dve(dve):
            def probabilities(n):
                d, t = STEPS[n]
                i = n - LAT0
                dve.wait_ge(d_done, i + 1)
                if i == 0:
                    dve.wait_ge(kt_kept, TA + TL)
                if i >= 2:
                    dve.wait_ge(intra_ready, i - 1)
                nc.vector.tensor_tensor(p_tok[:, d], scores[:, t], d_exp[:, d], ALU.mult).then_inc(p_done, 1)

            def carry(n):
                d, t = STEPS[n]
                dve.wait_ge(update_ready, n + 1)
                if n >= 2:
                    dve.wait_ge(state_done, n - 1)
                for h in range(M_HEADS):
                    bank = flat[:, OUT_AT + h * HEAD_COLS:OUT_AT + (h + 1) * HEAD_COLS]
                    if n < 2:
                        last = nc.vector.tensor_copy(state[:, d, h], bank)
                    else:
                        c = chunk_of(n)
                        last = nc.vector.scalar_tensor_tensor(state[:, d, h], state[:, d, h],
                                                              decay_all[:, 4 * d + h, c:c + 1], bank,
                                                              op0=ALU.mult, op1=ALU.add)
                last.then_inc(state_done, 1)

            outputs_now = flat[:, OUT_AT:OUT_AT + M_HEADS * HEAD_COLS].rearrange("p (h v) -> p h v", h=M_HEADS)

            def inter_part(n):
                d, t = STEPS[n]
                i = n - LAT0
                inter = tok_gate[:, 2, t, 4 * d:4 * d + 4].unsqueeze(2).to_broadcast([P, M_HEADS, HEAD_COLS])
                dve.wait_ge(inter_ready, i + 1)
                nc.vector.tensor_tensor(num[:, d], outputs_now, inter, ALU.mult).then_inc(inter_read, 1)

            def intra_part(n):
                d, t = STEPS[n]
                i = n - LAT0
                dve.wait_ge(inter_read, i + 1)
                dve.wait_ge(intra_ready, i + 1)
                nc.vector.tensor_tensor(num[:, d], outputs_now, num[:, d], ALU.add).then_inc(intra_read, 1)
                dve.wait_ge(intra_read, i + 1)
                den, low = num[:, d, :, M_DH], small[:, 4 * d:4 * d + 4]
                core_step(dve, nc.vector.scalar_tensor_tensor(low, den, -1.0, den, op0=ALU.mult, op1=ALU.max))
                core_step(dve, nc.vector.tensor_tensor(low, low, tok_gate[:, 3, t, 4 * d:4 * d + 4], ALU.max))
                core_step(dve, nc.vector.reciprocal(low, low))
                wide = low.unsqueeze(2).to_broadcast([P, M_HEADS, M_DH])
                rows = y_in[:, t, 0:M_WIDTH].rearrange("p (h v) -> p h v", h=M_HEADS)
                first = all(STEPS[m][1] != t for m in range(LAT0, n))
                core_step(dve, nc.vector.tensor_tensor(rows if first else h_new[:], num[:, d, :, 0:M_DH], wide, ALU.mult))
                if not first:
                    core_step(dve, nc.vector.tensor_tensor(rows, rows, h_new[:], ALU.add))

            def readout_stats(i):
                t = TILES_DONE[i][1]
                st = small[:, 8:32]
                mv = small[:, 48:56]
                var = small[:, 32 + 8 * (i % 2):36 + 8 * (i % 2)]
                for h in range(M_HEADS):
                    nc.vector.bn_stats(st[:, 6 * h:6 * h + 6], y_in[:, t, h * M_DH:(h + 1) * M_DH])\
                        .then_inc(cores_step, 1)
                    cstep[0] += 1
                dve.wait_ge(cores_step, cstep[0])
                for h in range(M_HEADS):
                    last = nc.vector.bn_aggr(mv[:, 2 * h:2 * h + 2], st[:, 6 * h:6 * h + 6])
                core_step(dve, last)
                nc.vector.tensor_scalar_add(var, mv.rearrange("p (h c) -> p h c", c=2)[:, :, 1], LN_EPS)\
                    .then_inc(read_measured, 1)

            def readout_norm(i):
                t = TILES_DONE[i][1]
                mv = small[:, 48:56]
                var = small[:, 32 + 8 * (i % 2):36 + 8 * (i % 2)]
                dve.wait_ge(read_inverted, i + 1)
                for h in range(M_HEADS):
                    rows = y_in[:, t, h * M_DH:(h + 1) * M_DH]
                    last = nc.vector.tensor_scalar(rows, rows, mv[:, 2 * h:2 * h + 1], var[:, h:h + 1],
                                                   ALU.subtract, ALU.mult)
                last.then_inc(read_normed, 1)

            for n in range(LAT0):
                carry(n)
            dve.wait_ge(rows_loaded, 32)
            maxima(dve, 0)
            done = measured = 0
            for n in range(LAT0, len(STEPS)):
                pair = 2 * (n - LAT0)
                maxima(dve, pair + 1)
                value_dve(dve, 2 * pair)
                inter_part(n)
                probabilities(n)
                value_dve(dve, 2 * pair + 1)
                if n in UPDATES:
                    carry(n)
                if measured < len(TILES_DONE) and TILES_DONE[measured][0] < n:
                    readout_stats(measured)
                    measured += 1
                maxima(dve, pair + 2)
                value_dve(dve, 2 * pair + 2)
                intra_part(n)
                value_dve(dve, 2 * pair + 3)
                if done < measured:
                    readout_norm(done)
                    done += 1
            readout_stats(done)
            readout_norm(done)
            nc.vector.memset(small[:, 60:61], 0.0).then_inc(h_done, 1)

        def cores_pe(pe):
            for n in range(TA + TL):
                if n < 4:
                    if n == 0:
                        pe.wait_ge(p_read_act, read_before(len(OUTPUTS) - 1, False))
                        pe.wait_ge(p_read_dve, read_before(len(OUTPUTS) - 1, True))
                        pe.wait_ge(conv_kept, 8)
                        pe.wait_ge(q_scaled, 4)
                else:
                    pe.wait_ge(kt_kept, n - 3)
                for h in range(M_HEADS):
                    o = psum[:, n % 4, h * P:(h + 1) * P]
                    if n < TA:
                        last = nc.tensor.transpose(o, kT[:, h, n * P:(n + 1) * P], ident[:])
                    else:
                        cols = slice((n - TA) * P, (n - TA + 1) * P)
                        last = nc.tensor.matmul(o, kT[:, h, cols], qT[:, h, cols], start=True, stop=True)
                last.then_inc(kt_turned, 1)

            def decays(n):
                d, t = STEPS[n]
                i = n - LAT0
                if i:
                    pe.wait_ge(intra_read, i)
                nc.tensor.matmul(psum[:, DECAY_BANK, :], ident_b[:], scan_mask[:, d].rearrange("p h t -> p (h t)"),
                                 start=True, stop=False)
                for h in range(M_HEADS):
                    last = nc.tensor.matmul(psum[:, DECAY_BANK, h * P:(h + 1) * P],
                                            ident[0:64, 32 * d + h:32 * d + h + 1].to_broadcast([64, P]),
                                            u_row[0:64, t * P:(t + 1) * P], start=False, stop=h == M_HEADS - 1)
                last.then_inc(d_ready, 1)

            def four(first, lhs, rhs):
                for h in range(M_HEADS):
                    o = flat[:, first + h * HEAD_COLS:first + (h + 1) * HEAD_COLS]
                    last = nc.tensor.matmul(o, lhs(h), rhs(h), start=True, stop=True)
                return last

            def update(n):
                d, t = STEPS[n]
                pe.wait_ge(wv_done, n + 1)
                if n == 0:
                    pe.wait_ge(kt_kept, TA)
                else:
                    pe.wait_ge(state_done, n)
                four(OUT_AT, lambda h: k_tok[:, t, h * M_DH:(h + 1) * M_DH], lambda h: w_v[:, d, h])\
                    .then_inc(update_ready, 1)

            pe.wait_ge(kt_kept, TA + TL)
            pe.wait_ge(masks_set, MASKS)
            for n in range(LAT0):
                update(n)
            pe.wait_ge(state_done, LAT0)
            decays(LAT0)
            pe.wait_ge(rope_kept, len(ROPED))
            scores_pe(pe, 0)
            for n in range(LAT0, len(STEPS)):
                d, t = STEPS[n]
                i = n - LAT0

                def inter():
                    pe.wait_ge(state_done, state_before(n))
                    pe.wait_ge(d_done, i + 1)
                    four(OUT_AT, lambda h: qT[:, h, t * P:(t + 1) * P], lambda h: state[:, d, h])\
                        .then_inc(inter_ready, 1)

                def state_update():
                    pe.wait_ge(inter_read, i + 1)
                    if n in UPDATES:
                        update(n)

                def intra():
                    pe.wait_ge(p_done, i + 1)
                    if n in UPDATES:
                        pe.wait_ge(state_done, n + 1)
                    four(OUT_AT, lambda h: p_tok[:, d, h], lambda h: vext[:, t, h]).then_inc(intra_ready, 1)

                def next_decays():
                    if n + 1 < len(STEPS):
                        decays(n + 1)

                attention_pe(pe, 2 * i, inter)
                state_update()
                attention_pe(pe, 2 * i + 1, intra)
                next_decays()

        ATT = [(j, i, g) for j in range(TL) for g in range(A_KV) for i in range(A_HEADS // 2)]

        def key_tiles(j):
            return [TL, TL + 1] + [t for t in (j - 1, j, j + 1) if 0 <= t < TL]

        s_ready = sem("s_ready")
        s_max = sem("s_max")
        s_exp = sem("s_exp")
        pt_turned = sem("pt_turned")
        pt_kept = sem("pt_kept")
        att_ready = sem("att_ready")
        att_read = sem("att_read")

        A_PAIRS = len(ATT) // 2

        def score(pe, n):
            j, i, g = ATT[n]
            tiles = key_tiles(j)
            rows = slice(64 * g, 64 * g + 64)
            at = SCORE_AT[n % 2]
            q = qaT[rows, i, j * P:(j + 1) * P]
            runs = []
            for m, t in enumerate(tiles):
                if runs and t == tiles[m - 1] + 1 and (at + m * P) % BANK and len(runs[-1]) * P < 2 * P:
                    runs[-1].append((m, t))
                else:
                    runs.append([(m, t)])
            for run in runs:
                (m0, t0), w = run[0], P * len(run)
                edges = [(m, t) for m, t in run if m >= 2 and t != j]
                last = nc.tensor.matmul(flat[:, at + m0 * P:at + m0 * P + w], q, kaT[rows, t0 * P:t0 * P + w],
                                        start=True, stop=not edges)
                for m, t in edges:
                    last = nc.tensor.matmul(flat[:, at + m * P:at + (m + 1) * P], ident_b[:], band_mask[:, int(t > j)],
                                            start=False, stop=(m, t) == edges[-1])
            last.then_inc(s_ready, 1)

        def scores_pe(pe, pair):
            if pair == A_PAIRS:
                return
            if pair:
                pe.wait_ge(s_exp, 2 * pair)
            score(pe, 2 * pair)
            score(pe, 2 * pair + 1)

        def turn_probabilities(pe, n):
            pe.wait_ge(s_exp, n + 1)
            if n:
                pe.wait_ge(pt_kept, n)
            for m in range(len(key_tiles(ATT[n][0]))):
                last = nc.tensor.transpose(flat[:, PT_AT + m * P:PT_AT + (m + 1) * P],
                                           att_p[:, n % 2, m * P:(m + 1) * P], ident[:])
            last.then_inc(pt_turned, 1)

        def value_pe(pe, n):
            j, i, g = ATT[n]
            tiles = key_tiles(j)
            pe.wait_ge(pt_kept, n + 1)
            if n:
                pe.wait_ge(att_read, n)
            for m, t in enumerate(tiles):
                last = nc.tensor.matmul(flat[:, VALUE_AT:VALUE_AT + A_DH], att_pT[:, n % 2, m * P:(m + 1) * P],
                                        va[:, t, g * A_DH:(g + 1) * A_DH], start=m == 0, stop=m == len(tiles) - 1)
            last.then_inc(att_ready, 1)

        def attention_pe(pe, pair, between):
            a, b = 2 * pair, 2 * pair + 1
            turn_probabilities(pe, a)
            scores_pe(pe, pair + 1)
            value_pe(pe, a)
            turn_probabilities(pe, b)
            between()
            value_pe(pe, b)

        def s_view(n):
            return flat[:, SCORE_AT[n % 2]:SCORE_AT[n % 2] + P * len(key_tiles(ATT[n][0]))]

        def exps_act(act, pair):
            if pair == A_PAIRS:
                return
            act.wait_ge(s_max, 2 * pair + 2)
            for n in (2 * pair, 2 * pair + 1):
                j, i, g = ATT[n]
                head = i + 4 * g
                s = att_small[:, n % 4]
                if n >= 2:
                    act.wait_ge(pt_turned, n - 1)
                if n >= 4:
                    act.wait_ge(att_read, n - 3)
                nc.scalar.activation(s[:, 1:2], sink[:, head:head + 1], ACT.Exp, bias=s[:, 0:1])
                nc.scalar.activation(att_p[:, n % 2, 0:P * len(key_tiles(j))], s_view(n), ACT.Exp, bias=s[:, 0:1],
                                     accum_out=s[:, 2:3]).then_inc(s_exp, 1)

        def keep_act(act, n):
            w = P * len(key_tiles(ATT[n][0]))
            act.wait_ge(pt_turned, n + 1)
            if n >= 2:
                act.wait_ge(att_ready, n - 1)
            nc.scalar.activation(att_pT[:, n % 2, 0:w], flat[:, PT_AT:PT_AT + w], ACT.Copy).then_inc(pt_kept, 1)

        def cores_act(act):
            mlstm_act(act)
            decays_act(act, LAT0)
            act.wait_ge(rows_loaded, 32)
            exps_act(act, 0)
            for pair in range(A_PAIRS):
                keep_act(act, 2 * pair)
                keep_act(act, 2 * pair + 1)
                exps_act(act, pair + 1)
                if pair % 2 and pair + 1 < A_PAIRS:
                    decays_act(act, LAT0 + (pair + 1) // 2)

        def maxima(dve, pair):
            if pair == A_PAIRS:
                return
            dve.wait_ge(s_ready, 2 * pair + 2)
            for n in (2 * pair, 2 * pair + 1):
                head = ATT[n][1] + 4 * ATT[n][2]
                s = att_small[:, n % 4]
                core_step(dve, nc.vector.reduce_max(s[:, 3:4], s_view(n), AX_X))
                nc.vector.tensor_scalar(s[:, 0:1], s[:, 3:4], sink[:, head:head + 1], -1.0, ALU.max, ALU.mult)\
                    .then_inc(s_max, 1)

        def value_dve(dve, n):
            j, i, g = ATT[n]
            s = att_small[:, n % 4]
            dve.wait_ge(s_exp, n + 1)
            core_step(dve, nc.vector.tensor_tensor(s[:, 3:4], s[:, 1:2], s[:, 2:3], ALU.add))
            core_step(dve, nc.vector.reciprocal(s[:, 3:4], s[:, 3:4]))
            dve.wait_ge(att_ready, n + 1)
            at = M_WIDTH + (i + 4 * g) * A_DH
            nc.vector.tensor_scalar_mul(y_in[:, j, at:at + A_DH], flat[:, VALUE_AT:VALUE_AT + A_DH],
                                        s[:, 3:4]).then_inc(att_read, 1)

        yt_turned = sem("yt_turned")
        yt_high = sem("yt_high")
        yt_low = sem("yt_low")
        wo_in = [sem(f"wo_in{i}") for i in range(2)]
        wo_hi = sem("wo_hi")
        wo_lo = sem("wo_lo")
        mix_ready = sem("mix_ready")
        mix_read = sem("mix_read")
        ln_in = sem("ln_in")
        x2_stored = sem("x2_stored")
        x2_affined = sem("x2_affined")
        x2_gains_in = sem("x2_gains_in")
        WO_UNITS = D // 256

        def output_sp(sp):
            sp.wait_ge(intra_ready, len(STEPS) - LAT0)
            sp.wait_ge(h_done, 1)
            for q in range(2 * WO_UNITS):
                if q >= 2:
                    sp.wait_ge(wo_lo, q - 1)
                sp.dma_start(wo_raw[:, q % 2], w_out_view[:, :, q * P:(q + 1) * P]).then_inc(wo_in[q % 2], 16)
                if q == 3:
                    sp.wait_ge(yt_turned, 2 * KD)
                    for i, src in enumerate((ln_g, ln_b)):
                        sp.dma_start(ln_rows2[:, i], src[0, 0:1, :].to_broadcast([P, D])).then_inc(ln_in, 16)
                    for t in range(TL):
                        if t >= 3:
                            sp.wait_ge(N2.rows_in[t % 3], 16 * (t // 3))
                        sp.dma_start(res_rows2[t][:], x1_dram[t]).then_inc(N2.rows_in[t % 3], 16)
                    for i, src in enumerate((ln_g, ln_b)):
                        sp.dma_start(ln_rows_x2[:, i], src[0, 1:2, :].to_broadcast([P, D])).then_inc(x2_gains_in, 16)

        def x2_store(sp, tiles):
            for t in tiles:
                sp.wait_ge(x2_affined, 2 * t + 2)
                sp.dma_start(x2_dram[t], y[:, t, :]).then_inc(x2_stored, 16)

        def x2_pool(pool):
            pool.wait_ge(x2_gains_in, 32)
            for t in range(TL):
                pool.wait_ge(T3.turned, KD * (t // 4 + 1))
                nc.gpsimd.tensor_tensor(y[:, t, :], y[:, t, :], ln_rows_x2[:, 0], ALU.mult).then_inc(x2_affined, 1)
                pool.wait_ge(x2_affined, 2 * t + 1)
                nc.gpsimd.tensor_tensor(y[:, t, :], y[:, t, :], ln_rows_x2[:, 1], ALU.add).then_inc(x2_affined, 1)

        def output_pool(pool):
            pool.wait_ge(ln_in, 32)
            for t in range(TL):
                pool.wait_ge(N2.rows_in[t % 3], 16 * (t // 3 + 1))
                rows = res_rows2[t][:]
                nc.gpsimd.tensor_tensor(rows, rows, ln_rows2[:, 0], ALU.mult).then_inc(N2.prepared, 1)
                pool.wait_ge(N2.prepared, 2 * t + 1)
                nc.gpsimd.tensor_tensor(rows, rows, ln_rows2[:, 1], ALU.add).then_inc(N2.prepared, 1)
            for t in range(TL):
                norm_pool(pool, N2, t)
            x2_pool(pool)

        def output_act(act):
            for u in range(2 * KD):
                act.wait_ge(yt_turned, u + 1)
                n, k = u // KD, u % KD
                nc.scalar.activation(xh_lat[:, k, n * BANK:(n + 1) * BANK], psum[:, u % 4, :], ACT.Copy).then_inc(yt_high, 1)
                if u == 3:
                    wo_high(act, 0)
                    wo_high(act, 1)
            act.wait_ge(N2.gates_summed, 1)
            for half in range(2):
                nc.scalar.activation(gate_row2[:, 0, half * BANK:(half + 1) * BANK], psum[:, half, :], ACT.Copy)\
                    .then_inc(N2.gates_kept, 1)
            for q in range(2, 2 * WO_UNITS):
                wo_high(act, q)
            for t in range(TL):
                norm_act(act, N2, t)
            turn_act(act, T3, T3_BANKS, turn_buf3, lambda a: None, 0)

        def wo_high(act, q):
            u = q // 2
            act.wait_ge(wo_in[q % 2], 16 * (q // 2 + 1))
            if u >= 2:
                act.wait_ge(mix_ready, TL * (u - 1))
            nc.scalar.activation(wo_h[:, u % 2, :, (q % 2) * P:(q % 2 + 1) * P], wo_raw[:, q % 2], ACT.Copy)\
                .then_inc(wo_hi, 1)

        def output_dve(dve):
            def low(q):
                u = q // 2
                dve.wait_ge(wo_hi, q + 1)
                cols = slice((q % 2) * P, (q % 2 + 1) * P)
                nc.vector.tensor_tensor(wo_l[:, u % 2, :, cols], wo_raw[:, q % 2], wo_h[:, u % 2, :, cols].bitcast(F32),
                                        ALU.subtract).then_inc(wo_lo, 1)
            for u in range(2 * KD):
                n, k = u // KD, u % KD
                dve.wait_ge(yt_high, u + 1)
                nc.vector.tensor_tensor(xl_lat[:, k, n * BANK:(n + 1) * BANK], psum[:, u % 4, :],
                                        xh_lat[:, k, n * BANK:(n + 1) * BANK].bitcast(F32), ALU.subtract)\
                    .then_inc(yt_low, 1)
                if u == 3:
                    low(0)
                    low(1)
            affine_of(dve, 1, 7, 6)
            low(2)
            low(3)
            dve.wait_ge(N2.gates_kept, 2)
            for j in range(TL * WO_UNITS):
                u, t = j // TL, j % TL
                if t == 0 and 2 <= u + 1 < WO_UNITS:
                    low(2 * u + 2)
                    low(2 * u + 3)
                dve.wait_ge(mix_ready, j + 1)
                cols = slice(u * 256, (u + 1) * 256)
                nc.vector.tensor_tensor(y[:, t, cols], psum[:, 4 + j % 4, 0:256], gate_row2[:, 0, cols], ALU.mult)\
                    .then_inc(mix_read, 1)
                if u == WO_UNITS - 1:
                    dve.wait_ge(mix_read, j + 1)
                    dve.wait_ge(N2.prepared, 2 * t + 2)
                    nc.vector.scalar_tensor_tensor(y[:, t, :], res_rows2[t][:], ALPHA, y[:, t, :],
                                                   op0=ALU.mult, op1=ALU.add).then_inc(N2.added, 1)
                    dve.wait_ge(N2.added, t + 1)
                    norm_sums_dve(dve, N2, t, None)
            turn_dve(dve, T3, turn_buf3, 0)

        def norm2_done(pe, n):
            if n == 0:
                pe.wait_ge(N2.gates_kept, 2)
            else:
                pe.wait_ge(mix_read, TL * WO_UNITS)
            pe.wait_ge(N2.done, (4, 8)[n])

        def output_pe(pe):
            pe.wait_ge(read_done, 2 * TL)
            pe.wait_ge(att_read, len(ATT))
            for u in range(2 * KD):
                n, k = u // KD, u % KD
                if u >= 4:
                    pe.wait_ge(yt_low, u - 3)
                for i in range(4):
                    last = nc.tensor.transpose(psum[:, u % 4, i * P:(i + 1) * P], y_in[:, 4 * n + i, k * P:(k + 1) * P],
                                               ident[:])
                last.then_inc(yt_turned, 1)
            pe.wait_ge(yt_low, 2 * KD)
            gate_rows_pe(pe, N2, 5, 1)
            for j in range(TL * WO_UNITS):
                u, t = j // TL, j % TL
                if t == 0:
                    pe.wait_ge(wo_lo, 2 * u + 2)
                if j >= 4:
                    pe.wait_ge(mix_read, j - 3)
                o = psum[:, 4 + j % 4, 0:256]
                for k in range(KD):
                    high, low = xpart(0, k, t * P, P), xpart(1, k, t * P, P)
                    wh, wl = wo_h[:, u % 2, k, :], wo_l[:, u % 2, k, :]
                    nc.tensor.matmul(o, high, wh, start=k == 0, stop=False)
                    nc.tensor.matmul(o, high, wl, start=False, stop=False)
                    last = nc.tensor.matmul(o, low, wh, start=False, stop=k == KD - 1)
                last.then_inc(mix_ready, 1)

            turn_pe(pe, T3, T3_BANKS, norm2_done, 0)

        out_last = sem("out_last")
        ln_in3 = sem("ln_in3")

        def last_sp(sp):
            sp.wait_ge(F2.ab_ready, 2 * F2.n * PAIRS)
            sp.wait_ge(F2.lo, 6 * PAIRS)
            for t in range(TL):
                if t >= 3:
                    sp.wait_ge(N3.added, t - 2)
                sp.dma_start(res_row[:, t % 3], x2_dram[t]).then_inc(N3.rows_in[t % 3], 16)
                if t == 2:
                    for i, src in enumerate((ln_g[0, 2:3, :], ln_b[0, 2:3, :])):
                        sp.dma_start(ln_rows3[:, i], src.to_broadcast([P, D])).then_inc(ln_in3, 16)
            for t in range(TL):
                if t < TL - 1:
                    sp.wait_ge(N3.prepared, 2 * t + 2)
                else:
                    sp.wait_ge(out_last, 2)
                sp.dma_start(out_rows[t], y[:, t, :]).then_inc(out_done, 16)
            sp.wait_ge(out_done, 16 * TL)

        def last_pool(pool):
            pool.wait_ge(ln_in3, 32)
            for t in range(TL):
                norm_pool(pool, N3, t)
                if t:
                    affine_out(pool, nc.gpsimd, t - 1, N3.prepared, t - 1)

        def last_act(act):
            act.wait_ge(F2.lo, 6 * PAIRS)
            gate_rows_act(act, N3, 1, HALF)
            for t in range(TL):
                norm_act(act, N3, t)

        def affine_out(engine, ops, t, done, before):
            engine.wait_ge(N3.done, t + 1)
            ops.tensor_tensor(y[:, t, :], y[:, t, :], ln_rows3[:, 0], ALU.mult).then_inc(done, 1)
            engine.wait_ge(done, 2 * before + 1)
            ops.tensor_tensor(y[:, t, :], y[:, t, :], ln_rows3[:, 1], ALU.add).then_inc(done, 1)

        def last_tiles_dve(dve, t):
            if t == 0:
                dve.wait_ge(N3.gates_kept, 2)
            step(dve, nc.vector.tensor_tensor(y[:, t, :], y[:, t, :], gate_row[:, 0, :], ALU.mult))
            dve.wait_ge(N3.rows_in[t % 3], 16 * (t // 3 + 1))
            nc.vector.scalar_tensor_tensor(y[:, t, :], res_row[:, t % 3, :], ALPHA, y[:, t, :],
                                           op0=ALU.mult, op1=ALU.add).then_inc(N3.added, 1)
            dve.wait_ge(N3.added, t + 1)
            norm_sums_dve(dve, N3, t, None)
            if t == TL - 1:
                dve.wait_ge(ln_in3, 32)
                affine_out(dve, nc.vector, t, out_last, 0)

        more_c = more[:, 0:16].rearrange("p (v k) -> p k v", v=2)

        T1 = Turn("t1", CHUNKS_ALL)
        F1 = Ffn("f1", 0, CHUNKS_ALL, True)
        N1 = Norm("n1")
        T2 = Turn("t2", CHUNKS_ALL)
        N2 = Norm("n2")
        T3 = Turn("t3", CHUNKS_LAT)
        F2 = Ffn("f2", 1, CHUNKS_LAT, False)
        N3 = Norm("n3")

        block = keep.enter_context(nc.Block())

        @block.sync
        def _(sp):
            sp.dma_start(rows_a[0:72, :], b_ada.rearrange("l (r p) -> (l r) p", p=P)).then_inc(rows_in, 16)
            sp.dma_start(rows_a[72:96, :], ln_g.rearrange("l s (r p) -> (l s r) p", p=P)).then_inc(rows_in, 16)
            sp.dma_start(rows_a[96:120, :], ln_b.rearrange("l s (r p) -> (l s r) p", p=P)).then_inc(rows_in, 16)
            sp.dma_start(rows_b[0:8, :], c.rearrange("l (r p) -> (l r) p", p=P)).then_inc(rows_in, 16)
            sp.dma_start(rows_b[8:16, :], c_ctx.rearrange("(r p) -> r p", p=P)).then_inc(rows_in, 16)
            sp.dma_start(rows_b[16:56, :], conv_w.rearrange("l j (r p) -> (l j r) p", p=P)).then_inc(rows_in, 16)
            sp.dma_start(rows_b[56:64, :], conv_b.rearrange("l (r p) -> (l r) p", p=P)).then_inc(rows_in, 16)
            for n in range(ADA_EARLY):
                if n >= 3:
                    sp.wait_ge(early_in[n % 3], 16 * (n // 3))
                sp.dma_start(ada_early[:, n], ada_view[:, :, n * P:(n + 1) * P]).then_inc(early_in[n % 3], 16)
            for t in range(TA):
                sp.dma_start(y[:, t, :], token_rows(t)).then_inc(x_in[t // 4], 16)
            ffn_sp(sp, F1)
            sp.wait_ge(ada_used, PAIRS * ADA_PER_PAIR)
            sp.wait_ge(F1.ab_ready, 2 * F1.n * PAIRS)
            for t in range(TA):
                if t >= 3:
                    sp.wait_ge(N1.added, t - 2)
                sp.dma_start(res_row[:, t % 3, :], token_rows(t)).then_inc(N1.rows_in[t % 3], 16)
            proj_sp(sp)
            mlstm_sp(sp)
            output_sp(sp)
            sp.wait_ge(mix_ready, TL * WO_UNITS)
            ffn_sp(sp, F2, lambda stage: x2_store(sp, range(4 * stage, 4 * stage + 4)))
            last_sp(sp)

        @block.gpsimd
        def _(pool):
            nc.gpsimd.memset(ident[:], 0.0).then_inc(ident_set, 1)
            nc.gpsimd.memset(minus_half[:], -0.5).then_inc(const_set, 1)
            nc.gpsimd.memset(ones[:], 1.0).then_inc(const_set, 1)
            pool.wait_ge(ident_set, 1)
            nc.gpsimd.affine_select(out=ident[:], in_=ident[:], compare_op=ALU.not_equal, fill=1.0, base=0,
                                    pattern=[[-1, P]], channel_multiplier=1).then_inc(ident_set, 1)
            first_norm_pool(pool)
            masks_pool(pool)
            mlstm_pool(pool)
            output_pool(pool)
            last_pool(pool)

        @block.scalar
        def _(act):
            act.wait_ge(rows_in, 7 * 16)
            nc.scalar.activation(rows_b[0:16, :], rows_b[0:16, :], ACT.Silu).then_inc(c_silu, 1)

            def scale_known(act):
                act.wait_ge(dve_step, 3)
            turn_act(act, T1, T1_BANKS, turn_buf1, scale_known, 0)
            ffn_act(act, F1, lambda n: turn_act(act, T1, T1_BANKS, turn_buf1, lambda a: None, n))
            act.wait_ge(F1.lo, 6 * PAIRS)
            gate_rows_act(act, N1, 2, HALF)
            for t in range(TA):
                norm_act(act, N1, t)
                if t == TA - 2:
                    first_weights_act(act)
            turn_act(act, T2, T2_BANKS, turn_buf2, lambda a: None)
            proj_act(act)
            cores_act(act)
            output_act(act)
            ffn_act(act, F2, lambda n: turn_act(act, T3, T3_BANKS, turn_buf3, lambda a: None, n))
            last_act(act)

        @block.vector
        def _(dve):
            dve.wait_ge(rows_turned, 2)
            nc.vector.tensor_copy(params[:], psum[:, 0, 0:120]).then_inc(rows_kept, 1)
            nc.vector.tensor_copy(more[:], psum[:, 1, 0:64]).then_inc(rows_kept, 1)
            dve.wait_ge(rows_kept, 2)
            for i, n in enumerate(EARLY_DVE):
                dve.wait_ge(early_in[n % 3], 16 * (n // 3 + 1))
                piece_sums(dve, ada_early[:, n], early_sum[:, n], early_dve, 2 * KD * i)
            dve.wait_ge(early_used, ADA_EARLY)
            nc.vector.tensor_tensor(mod[:, 0:ADA_EARLY, :],
                                    psum[:, 7, 0:2 * ADA_EARLY].rearrange("p (a b) -> p a b", b=2),
                                    params[:, 0:ADA_EARLY].unsqueeze(2).to_broadcast([P, ADA_EARLY, 2]),
                                    ALU.add).then_inc(mod_ready, 1)
            dve.wait_ge(mod_ready, 1)
            for v in range(2):
                step(dve, nc.vector.tensor_scalar_add(in_scale[:, v, :], mod[:, KD:2 * KD, v], 1.0))
            step(dve, nc.vector.tensor_copy(in_shift[:], mod[:, 0:KD, :].rearrange("p k v -> p v k")))
            turn_dve(dve, T1, turn_buf1, 0)

            def before_last_y(dve):
                affine_of(dve, 0, 4, 3)
            ffn_dve(dve, F1, before_last_y, first_norm_dve, lambda n: turn_dve(dve, T1, turn_buf1, n))
            dve.wait_ge(F1.y_ready, 2 * TA * PAIRS)
            nc.vector.memset(gate_bias[:], 0.0).then_inc(gate_clear, 1)
            nc.vector.memset(gate_wh[:].bitcast(F32), 0.0)
            nc.vector.memset(gate_wl[:].bitcast(F32), 0.0).then_inc(gate_clear, 1)
            nc.vector.memset(conv_in[:], 0.0).then_inc(pads_set, 1)
            first_weights_dve(dve)
            turn_dve(dve, T2, turn_buf2)
            proj_dve(dve)
            cores_dve(dve)
            output_dve(dve)
            ffn_dve(dve, F2, lambda e: None, last_tiles_dve, lambda n: turn_dve(dve, T3, turn_buf3, n),
                    lambda: dve.wait_ge(x2_stored, 16 * TL))

        @block.tensor
        def _(pe):
            pe.wait_ge(ident_set, 2)
            pe.wait_ge(rows_in, 7 * 16)
            nc.tensor.transpose(psum[:, 0, 0:120], rows_a[0:120, :], ident[0:120, 0:120]).then_inc(rows_turned, 1)
            pe.wait_ge(c_silu, 1)
            nc.tensor.transpose(psum[:, 1, 0:64], rows_b[0:64, :], ident[0:64, 0:64]).then_inc(rows_turned, 1)
            pe.wait_ge(rows_kept, 2)
            early_pe(pe)
            def x_rows_in(e, n):
                e.wait_ge(x_in[n], 16 * (4 if n < 2 else 2))
            pe.wait_ge(rows_kept, 2)
            turn_pe(pe, T1, T1_BANKS, x_rows_in, 0)

            def before_last_y(pe):
                pe.wait_ge(F1.glu_ready, 2 * F1.n * PAIRS)
                gate_rows_pe(pe, N1, 2, 2)
            ffn_pe(pe, F1, T1, before_last_y, lambda n, k: turn_pe(pe, T1, T1_BANKS, x_rows_in, (n, k)))

            def normed(pe, n):
                if n == 0:
                    pe.wait_ge(N1.gates_kept, 4)
                pe.wait_ge(N1.done, (4, 8, 10)[n])
            turn_pe(pe, T2, T2_BANKS, normed)
            proj_pe(pe)
            cores_pe(pe)
            output_pe(pe)

            def before_last(pe):
                pe.wait_ge(F2.glu_ready, 2 * F2.n * PAIRS)
                gate_rows_pe(pe, N3, 8, 1)
            ffn_pe(pe, F2, T3, before_last, lambda n, k: turn_pe(pe, T3, T3_BANKS, norm2_done, (n, k)))


_INS = ["x", "c", "ctx", "c_ctx", "w_ada", "b_ada", "ln_g", "ln_b", "ffn_w13", "ffn_w2", "w_in", "b_gates",
        "conv_w", "conv_b", "mh_norm_g", "attn_sink", "w_out"]
GRID_W = 64
ROPE_BASE = 10000.0


def rope_table():
    rows = N_LAT // GRID_W
    row = np.repeat(np.arange(rows, dtype=np.float32), GRID_W)
    col = np.tile(np.arange(GRID_W, dtype=np.float32), rows)
    n_freq = A_DH // 4
    inv = np.float32(ROPE_BASE) ** (-np.arange(n_freq, dtype=np.float32) / np.float32(n_freq))
    angle = np.concatenate([row[:, None] * inv, col[:, None] * inv], -1).astype(np.float32)
    return np.stack([np.cos(angle), np.sin(angle)]).astype(np.float32)


def kernel(**inputs):
    import concourse.bacc as _bacc
    from concourse.bass_utils import run_bass_kernel_spmd as _run

    nc = _bacc.Bacc("TRN2", target_bir_lowering=False, num_devices=1)
    arrays, args = {}, []
    for name in _INS:
        arrays[f"in_{name}"] = np.ascontiguousarray(inputs[name])
    arrays["rope"] = rope_table()
    for name, a in arrays.items():
        args.append(nc.dram_tensor(name, a.shape, mybir.dt.from_np(a.dtype), kind="ExternalInput").ap())
    out = nc.dram_tensor("out", (1, N_LAT, D), F32, kind="ExternalOutput").ap()
    hybrid_block(nc, *args, out)
    r = _run(nc, [arrays], core_ids=[0])
    return r.results[0]["out"]
```
